# Optimizing a Trainium2 kernel written in Bass

```python
import math
import jax, jax.numpy as jnp
from jax import lax
import numpy as np

D_MODEL = 1024
BATCH = 1
SEQ = 512
DEPTH = 2

GRID_W = 64
CTX_LEN = 256
HEAD_DIM = 64
N_HEADS_A = 8
N_KV_A = 2
N_HEADS_B = 8
N_HEADS_C = 8
N_KV_C = 2
MIX_WIDTH = HEAD_DIM * (N_HEADS_A + N_HEADS_B + N_HEADS_C)
Q_BLOCK = 128
NB_ROWS = 8
NB_COLS = 16
WINDOW = 128
ROPE_THETA = 10000.0
EPS = 1e-6
IN_SIZES = (
    N_HEADS_A * HEAD_DIM, N_KV_A * HEAD_DIM, N_KV_A * HEAD_DIM,
    N_HEADS_B * HEAD_DIM, N_HEADS_B * HEAD_DIM, N_HEADS_B * HEAD_DIM,
    N_HEADS_C * HEAD_DIM, N_KV_C * HEAD_DIM, N_KV_C * HEAD_DIM,
    MIX_WIDTH,
)
IN_WIDTH = sum(IN_SIZES)


def rmsnorm(x, w):
    xf = x.astype(jnp.float32)
    y = xf * lax.rsqrt(jnp.mean(xf * xf, axis=-1, keepdims=True) + EPS)
    return y.astype(x.dtype) * w

def softmax_f32(s, dtype):
    return jax.nn.softmax(s.astype(jnp.float32), axis=-1).astype(dtype)

def heads(z, h):
    return z.reshape(z.shape[:-1] + (h, HEAD_DIM))

def split_cols(z):
    outs, off = [], 0
    for sz in IN_SIZES:
        outs.append(z[..., off:off + sz])
        off += sz
    return outs

def axial_rope(n, dtype):
    t = jnp.arange(n, dtype=jnp.int32)
    rows = (t // GRID_W).astype(jnp.float32)
    cols = (t % GRID_W).astype(jnp.float32)
    n_freq = HEAD_DIM // 4
    freq = ROPE_THETA ** (-jnp.arange(n_freq, dtype=jnp.float32) / n_freq)
    ang = jnp.concatenate([rows[:, None] * freq, cols[:, None] * freq], axis=-1)
    return jnp.cos(ang).astype(dtype), jnp.sin(ang).astype(dtype)

def apply_rope(x, cos, sin):
    x1, x2 = jnp.split(x, 2, axis=-1)
    c = cos[None, :, None, :]
    s = sin[None, :, None, :]
    return jnp.concatenate([x1 * c - x2 * s, x1 * s + x2 * c], axis=-1)

def global_gqa(q, k, v, qc, kc, vc, cos, sin, qn, kn, need_ctx):
    B, N = q.shape[0], q.shape[1]
    C = qc.shape[1]
    G = N_HEADS_A // N_KV_A
    scale = HEAD_DIM ** -0.5
    q = apply_rope(rmsnorm(heads(q, N_HEADS_A), qn), cos, sin) * scale
    k = apply_rope(rmsnorm(heads(k, N_KV_A), kn), cos, sin)
    v = heads(v, N_KV_A)
    qc = rmsnorm(heads(qc, N_HEADS_A), qn) * scale
    kc = rmsnorm(heads(kc, N_KV_A), kn)
    vc = heads(vc, N_KV_A)
    k_all = jnp.concatenate([k, kc], axis=1)
    v_all = jnp.concatenate([v, vc], axis=1)
    nblk = N // Q_BLOCK
    qb = q.reshape(B, nblk, Q_BLOCK, N_KV_A, G, HEAD_DIM).transpose(1, 0, 2, 3, 4, 5)

    def block(qi):
        s = jnp.einsum('bqhgd,bkhd->bhgqk', qi, k_all)
        p = softmax_f32(s, v_all.dtype)
        return jnp.einsum('bhgqk,bkhd->bqhgd', p, v_all)

    y = lax.map(block, qb).transpose(1, 0, 2, 3, 4, 5).reshape(B, N, N_HEADS_A * HEAD_DIM)
    yc = None
    if need_ctx:
        qcg = qc.reshape(B, C, N_KV_A, G, HEAD_DIM)
        p = softmax_f32(jnp.einsum('bqhgd,bkhd->bhgqk', qcg, kc), vc.dtype)
        yc = jnp.einsum('bhgqk,bkhd->bqhgd', p, vc).reshape(B, C, N_HEADS_A * HEAD_DIM)
    return y, yc

def neighbourhood_attn(q, k, v, qc, kc, vc, rpb, need_ctx):
    B, N = q.shape[0], q.shape[1]
    C = qc.shape[1]
    H = N_HEADS_B
    scale = HEAD_DIM ** -0.5
    rows = N // GRID_W
    kh = min(NB_ROWS, rows)
    kw = NB_COLS
    t = jnp.arange(N, dtype=jnp.int32)
    r = t // GRID_W
    col = t % GRID_W
    rs = jnp.clip(r - kh // 2, 0, rows - kh)
    cs = jnp.clip(col - kw // 2, 0, GRID_W - kw)
    key_r = rs[:, None, None] + jnp.arange(kh, dtype=jnp.int32)[None, :, None]
    key_c = cs[:, None, None] + jnp.arange(kw, dtype=jnp.int32)[None, None, :]
    idx = (key_r * GRID_W + key_c).reshape(N, kh * kw)
    rel = ((key_r - r[:, None, None] + NB_ROWS - 1) * (2 * NB_COLS - 1)
           + (key_c - col[:, None, None] + NB_COLS - 1)).reshape(N, kh * kw)
    rpb_flat = rpb.reshape(H, -1)
    q = heads(q, H) * scale
    k = heads(k, H)
    v = heads(v, H)
    qc = heads(qc, H) * scale
    kc = heads(kc, H)
    vc = heads(vc, H)
    nblk = N // Q_BLOCK
    kn = kh * kw
    xs = (q.reshape(B, nblk, Q_BLOCK, H, HEAD_DIM).transpose(1, 0, 2, 3, 4),
          idx.reshape(nblk, Q_BLOCK, kn), rel.reshape(nblk, Q_BLOCK, kn))

    def block(args):
        qi, ii, ri = args
        kg = jnp.take(k, ii, axis=1)
        vg = jnp.take(v, ii, axis=1)
        s_nb = jnp.einsum('bqhd,bqkhd->bhqk', qi, kg) + jnp.take(rpb_flat, ri, axis=1)[None]
        s_ctx = jnp.einsum('bqhd,bchd->bhqc', qi, kc)
        p = softmax_f32(jnp.concatenate([s_nb, s_ctx], axis=-1), v.dtype)
        return (jnp.einsum('bhqk,bqkhd->bqhd', p[..., :kn], vg)
                + jnp.einsum('bhqc,bchd->bqhd', p[..., kn:], vc))

    y = lax.map(block, xs).transpose(1, 0, 2, 3, 4).reshape(B, N, H * HEAD_DIM)
    yc = None
    if need_ctx:
        p = softmax_f32(jnp.einsum('bqhd,bchd->bhqc', qc, kc), vc.dtype)
        yc = jnp.einsum('bhqc,bchd->bqhd', p, vc).reshape(B, C, H * HEAD_DIM)
    return y, yc

def window_gqa(q, k, v, qc, kc, vc, cos, sin, sink, need_ctx):
    B, N = q.shape[0], q.shape[1]
    C = qc.shape[1]
    G = N_HEADS_C // N_KV_C
    scale = HEAD_DIM ** -0.5
    q = (apply_rope(heads(q, N_HEADS_C), cos, sin) * scale).reshape(B, N, N_KV_C, G, HEAD_DIM)
    k = apply_rope(heads(k, N_KV_C), cos, sin)
    v = heads(v, N_KV_C)
    qc = (heads(qc, N_HEADS_C) * scale).reshape(B, C, N_KV_C, G, HEAD_DIM)
    kc = heads(kc, N_KV_C)
    vc = heads(vc, N_KV_C)
    pad = ((0, 0), (WINDOW, WINDOW), (0, 0), (0, 0))
    kp = jnp.pad(k, pad)
    vp = jnp.pad(v, pad)
    span = Q_BLOCK + 2 * WINDOW
    sink_l = sink.astype(jnp.float32).reshape(N_KV_C, G)
    neg = jnp.finfo(jnp.float32).min
    nblk = N // Q_BLOCK
    qs = q.reshape(B, nblk, Q_BLOCK, N_KV_C, G, HEAD_DIM).transpose(1, 0, 2, 3, 4, 5)

    def block(args):
        i, qi = args
        start = i * Q_BLOCK
        kb = lax.dynamic_slice_in_dim(kp, start, span, axis=1)
        vb = lax.dynamic_slice_in_dim(vp, start, span, axis=1)
        qpos = start + jnp.arange(Q_BLOCK, dtype=jnp.int32)
        kpos = start - WINDOW + jnp.arange(span, dtype=jnp.int32)
        valid = (jnp.abs(qpos[:, None] - kpos[None, :]) <= WINDOW) & (kpos >= 0)[None, :] & (kpos < N)[None, :]
        s = jnp.where(valid, jnp.einsum('bqhgd,bkhd->bhgqk', qi, kb).astype(jnp.float32), neg)
        s_ctx = jnp.einsum('bqhgd,bkhd->bhgqk', qi, kc).astype(jnp.float32)
        s_sink = jnp.broadcast_to(sink_l[None, :, :, None, None], s.shape[:-1] + (1,))
        p = softmax_f32(jnp.concatenate([s, s_ctx, s_sink], axis=-1), v.dtype)
        return (jnp.einsum('bhgqk,bkhd->bqhgd', p[..., :span], vb)
                + jnp.einsum('bhgqk,bkhd->bqhgd', p[..., span:span + C], vc))

    y = lax.map(block, (jnp.arange(nblk, dtype=jnp.int32), qs))
    y = y.transpose(1, 0, 2, 3, 4, 5).reshape(B, N, N_HEADS_C * HEAD_DIM)
    yc = None
    if need_ctx:
        s = jnp.einsum('bqhgd,bkhd->bhgqk', qc, kc).astype(jnp.float32)
        s_sink = jnp.broadcast_to(sink_l[None, :, :, None, None], s.shape[:-1] + (1,))
        p = softmax_f32(jnp.concatenate([s, s_sink], axis=-1), vc.dtype)
        yc = jnp.einsum('bhgqk,bkhd->bqhgd', p[..., :C], vc).reshape(B, C, N_HEADS_C * HEAD_DIM)
    return y, yc

def layer(x, cx, c_silu, cctx_silu, norm_w, ada_w, ada_b, w_in, w_out, qn, kn, rpb, sink, cos, sin, need_ctx):
    mod = c_silu @ ada_w + ada_b
    mod_c = cctx_silu @ ada_w + ada_b
    shift, scale, gate = jnp.split(mod, 3, axis=-1)
    shift_c, scale_c, gate_c = jnp.split(mod_c, 3, axis=-1)
    hx = rmsnorm(x, norm_w) * (1 + scale[:, None, :]) + shift[:, None, :]
    hc = rmsnorm(cx, norm_w) * (1 + scale_c) + shift_c
    px = split_cols(hx @ w_in)
    pc = split_cols(hc @ w_in)
    ya, yca = global_gqa(px[0], px[1], px[2], pc[0], pc[1], pc[2], cos, sin, qn, kn, need_ctx)
    yb, ycb = neighbourhood_attn(px[3], px[4], px[5], pc[3], pc[4], pc[5], rpb, need_ctx)
    yc_, ycc = window_gqa(px[6], px[7], px[8], pc[6], pc[7], pc[8], cos, sin, sink, need_ctx)
    ux = jnp.concatenate([ya, yb, yc_], axis=-1) * jax.nn.silu(px[9])
    x = x + gate[:, None, :] * (ux @ w_out)
    if need_ctx:
        uc = jnp.concatenate([yca, ycb, ycc], axis=-1) * jax.nn.silu(pc[9])
        cx = cx + gate_c * (uc @ w_out)
    return x, cx

def first_inputs(seed: int = 0) -> dict:
    key = jax.random.key(seed)
    ks = jax.random.split(key, 14)
    f32 = jnp.float32
    n_rel = (2 * NB_ROWS - 1, 2 * NB_COLS - 1)
    return {
        "x": jax.random.normal(ks[0], (BATCH, SEQ, D_MODEL), f32),
        "c": jax.random.normal(ks[1], (BATCH, D_MODEL), f32),
        "ctx": jax.random.normal(ks[2], (BATCH, CTX_LEN, D_MODEL), f32),
        "c_ctx": jax.random.normal(ks[3], (D_MODEL,), f32),
        "norm_w": 1.0 + 0.05 * jax.random.normal(ks[4], (DEPTH, D_MODEL), f32),
        "ada_w": jax.random.normal(ks[5], (DEPTH, D_MODEL, 3 * D_MODEL), f32) * D_MODEL ** -0.5,
        "ada_b": 0.02 * jax.random.normal(ks[6], (DEPTH, 3 * D_MODEL), f32),
        "w_in": jax.random.normal(ks[7], (DEPTH, D_MODEL, IN_WIDTH), f32) * D_MODEL ** -0.5,
        "w_out": jax.random.normal(ks[8], (DEPTH, MIX_WIDTH, D_MODEL), f32) * MIX_WIDTH ** -0.5,
        "q_norm_a": 1.0 + 0.05 * jax.random.normal(ks[9], (DEPTH, HEAD_DIM), f32),
        "k_norm_a": 1.0 + 0.05 * jax.random.normal(ks[10], (DEPTH, HEAD_DIM), f32),
        "rpb_b": 0.1 * jax.random.normal(ks[11], (DEPTH, N_HEADS_B) + n_rel, f32),
        "sink_c": 0.5 * jax.random.normal(ks[12], (DEPTH, N_HEADS_C), f32),
        "final_norm_w": 1.0 + 0.05 * jax.random.normal(ks[13], (D_MODEL,), f32),
    }

def first_block(x, c, ctx, c_ctx, norm_w, ada_w, ada_b, w_in, w_out, q_norm_a, k_norm_a, rpb_b, sink_c, final_norm_w):
    n_tok = x.shape[1]
    cos, sin = axial_rope(n_tok, x.dtype)
    c_silu = jax.nn.silu(c)
    cctx_silu = jax.nn.silu(c_ctx)
    cx = ctx
    for l in range(DEPTH):
        x, cx = layer(x, cx, c_silu, cctx_silu, norm_w[l], ada_w[l], ada_b[l], w_in[l], w_out[l],
                      q_norm_a[l], k_norm_a[l], rpb_b[l], sink_c[l], cos, sin, l < DEPTH - 1)
    return rmsnorm(x, final_norm_w)


N_EVEN = (DEPTH + 1) // 2
N_ODD = DEPTH // 2
RNN_WIDTH = D_MODEL // 2
LRU_HEADS = 8
LRU_HEAD_DIM = RNN_WIDTH // LRU_HEADS
LRU_CONV = 4
LRU_C = 8.0
LRU_A_MIN = 0.9
LRU_A_MAX = 0.999
HYENA_WIDTH = D_MODEL // 2
HYENA_ORDER = 2
HYENA_SHORT_CONV = 3
FILTER_EMB = 33
FILTER_HIDDEN = 64
HYENA_DECAY_TARGET = 1e-2
HYENA_FAST_PCT = 0.3
HYENA_SLOW_PCT = 1.5
HYENA_SHIFT = 0.05
IN_WIDTH_2 = 2 * RNN_WIDTH + (HYENA_ORDER + 1) * HYENA_WIDTH
CONF_KERNEL = 31
N_EXPERTS = 16
EC_CAPACITY = 2
EXPERT_FF = 1024
N_MOD = 6


def _rmsnorm(x, g):
    xf = x.astype(jnp.float32)
    y = xf * lax.rsqrt(jnp.mean(xf * xf, axis=-1, keepdims=True) + EPS)
    return (y * g.astype(jnp.float32)).astype(x.dtype)

def _layernorm(x, g, b):
    xf = x.astype(jnp.float32)
    mu = jnp.mean(xf, axis=-1, keepdims=True)
    var = jnp.mean(jnp.square(xf - mu), axis=-1, keepdims=True)
    y = (xf - mu) * lax.rsqrt(var + EPS) * g.astype(jnp.float32) + b.astype(jnp.float32)
    return y.astype(x.dtype)

def _adaln(cvec, w_mod, b_mod, n_chunks):
    m = jax.nn.silu(cvec) @ w_mod[:, :n_chunks * D_MODEL] + b_mod[:n_chunks * D_MODEL]
    return [m[:, None, j * D_MODEL:(j + 1) * D_MODEL] for j in range(n_chunks)]

def _modulate(h, shift, scale):
    return h * (1 + scale) + shift

def _dwconv1d(x, w, b):
    k = w.shape[0]
    y = lax.conv_general_dilated(x, w[:, None, :], window_strides=(1,),
                                 padding=[((k - 1) // 2, k // 2)],
                                 dimension_numbers=('NWC', 'WIO', 'NWC'),
                                 feature_group_count=x.shape[-1])
    return y + b

def _dwconv_vertical(x, w, b, rows):
    bsz, n, ch = x.shape
    k = w.shape[0]
    grid = x.reshape(bsz, rows, GRID_W, ch)
    y = lax.conv_general_dilated(grid, w[:, None, None, :], window_strides=(1, 1),
                                 padding=[((k - 1) // 2, k // 2), (0, 0)],
                                 dimension_numbers=('NHWC', 'HWIO', 'NHWC'),
                                 feature_group_count=ch)
    return y.reshape(bsz, n, ch) + b

def _lin_combine(left, right):
    a_l, b_l = left
    a_r, b_r = right
    return a_l * a_r, a_r * b_l + b_r

def _rglru(xa_raw, p, h0):
    f32 = jnp.float32
    xa = _dwconv1d(xa_raw, p['conv_a_w'], p['conv_a_b'])
    bsz, n, _ = xa.shape
    xh = xa.reshape(bsz, n, LRU_HEADS, LRU_HEAD_DIM)

    def gate(w, b):
        z = jnp.einsum('bnhi,khij->kbnhj', xh, w).reshape(2, bsz, n, RNN_WIDTH)
        return jax.nn.sigmoid((z + b[:, None, None, :]).astype(f32))

    r = gate(p['lru_wr'], p['lru_br'])
    i = gate(p['lru_wi'], p['lru_bi'])
    log_a = -LRU_C * r * jax.nn.softplus(-p['lru_lam'].astype(f32))[:, None, None, :]
    a = jnp.exp(log_a)
    u = jnp.sqrt(-jnp.expm1(2.0 * log_a)) * i * xa.astype(f32)[None]
    a = jnp.stack([a[0], jnp.flip(a[1], axis=1)])
    u = jnp.stack([u[0], jnp.flip(u[1], axis=1)])
    a_cum, h = lax.associative_scan(_lin_combine, (a, u), axis=2)
    h = h + a_cum * h0[:, :, None, :]
    return h, h[:, :, -1]

def _hyena_filters_fft(n, p):
    f32 = jnp.float32
    t = jnp.linspace(0.0, 1.0, n, dtype=f32)[:, None]
    bands = (FILTER_EMB - 1) // 2
    w = (2.0 * math.pi / n) * jnp.arange(n, dtype=f32)[:, None]
    f = jnp.linspace(1e-4, bands - 1, bands, dtype=f32)[None, :]
    z = jnp.concatenate([t, jnp.cos(f * w), -jnp.sin(f * w)], axis=-1)
    freq = p['filt_freq'].astype(f32)
    hid = jnp.sin(freq[0] * (z @ p['filt_w1'].astype(f32) + p['filt_b1'].astype(f32)))
    hid = jnp.sin(freq[1] * (hid @ p['filt_w2'].astype(f32) + p['filt_b2'].astype(f32)))
    filt = (hid @ p['filt_w3'].astype(f32) + p['filt_b3'].astype(f32))
    filt = filt.reshape(n, HYENA_ORDER, 2, HYENA_WIDTH)
    deltas = jnp.abs(jnp.linspace(math.log(HYENA_DECAY_TARGET) / HYENA_SLOW_PCT,
                                  math.log(HYENA_DECAY_TARGET) / HYENA_FAST_PCT,
                                  HYENA_WIDTH, dtype=f32))
    window = jnp.exp(-t * deltas[None, :]) + HYENA_SHIFT
    filt = filt * window[:, None, None, :]
    fwd, bwd = filt[:, :, 0], filt[:, :, 1]
    kern = jnp.concatenate([fwd, jnp.zeros((1, HYENA_ORDER, HYENA_WIDTH), f32), bwd[:0:-1]], axis=0)
    return jnp.fft.rfft(kern, axis=0)

def _fftconv(u, kf, bias):
    n = u.shape[1]
    uf = u.astype(jnp.float32)
    y = jnp.fft.irfft(jnp.fft.rfft(uf, n=2 * n, axis=1) * kf[None], n=2 * n, axis=1)[:, :n]
    return (y + uf * bias.astype(jnp.float32)).astype(u.dtype)

def _even_mixer(h, p, h0):
    proj = h @ p['w_in']
    gate = proj[..., :RNN_WIDTH]
    xa_raw = proj[..., RNN_WIDTH:2 * RNN_WIDTH]
    hy = proj[..., 2 * RNN_WIDTH:]
    hs, h_last = _rglru(xa_raw, p, h0)
    y_a = jax.nn.gelu(gate) * (hs[0] + jnp.flip(hs[1], axis=1)).astype(h.dtype)
    u = _dwconv1d(hy, p['conv_b_w'], p['conv_b_b'])
    v, *gates = jnp.split(u, HYENA_ORDER + 1, axis=-1)
    kf = _hyena_filters_fft(h.shape[1], p)
    z = v
    for o in range(HYENA_ORDER):
        z = gates[o] * _fftconv(z, kf[:, o], p['filt_bias'][o])
    return jnp.concatenate([y_a, z], axis=-1) @ p['w_out'], h_last

def _conformer_conv(h, p, rows):
    u = h @ p['cf_w1'] + p['cf_b1']
    u = u[..., :D_MODEL] * jax.nn.sigmoid(u[..., D_MODEL:])
    if rows is None:
        u = _dwconv1d(u, p['cf_dw_w'], p['cf_dw_b'])
    else:
        u = _dwconv_vertical(u, p['cf_dw_w'], p['cf_dw_b'], rows)
    u = jax.nn.silu(_layernorm(u, p['cf_ln_g'], p['cf_ln_b']))
    return u @ p['cf_w2'] + p['cf_b2']

def _ec_moe(h, router, w1, w3, w2):
    bsz, n, _ = h.shape
    cap = EC_CAPACITY * n // N_EXPERTS
    probs = jax.nn.softmax(jnp.einsum('bnd,de->ben', h, router).astype(jnp.float32), axis=1)
    gates, idx = lax.top_k(probs, cap)
    bidx = jnp.arange(bsz)[:, None, None]
    xs = h[bidx, idx]
    a = jnp.einsum('becd,edf->becf', xs, w1)
    g = jnp.einsum('becd,edf->becf', xs, w3)
    y = jnp.einsum('becf,efd->becd', jax.nn.silu(a) * g, w2) * gates[..., None].astype(h.dtype)
    return jnp.zeros_like(h).at[bidx, idx].add(y)

def second_inputs(seed: int = 0) -> dict:
    key = jax.random.key(seed)
    ks = iter(jax.random.split(key, 48))
    f32 = jnp.float32
    D = D_MODEL

    def nrm(shape, scale):
        return jax.random.normal(next(ks), shape, f32) * scale

    x = nrm((BATCH, SEQ, D), 1.0)
    c = nrm((BATCH, D), 1.0)
    ctx = nrm((BATCH, CTX_LEN, D), 1.0)
    c_ctx = nrm((D,), 1.0)
    norm1_g = 1.0 + nrm((DEPTH, D), 0.1)
    norm2_g = 1.0 + nrm((DEPTH, D), 0.1)
    w_mod = nrm((DEPTH, D, N_MOD * D), 0.5 * D ** -0.5)
    b_mod = nrm((DEPTH, N_MOD * D), 0.01)
    w_in = nrm((N_EVEN, D, IN_WIDTH_2), D ** -0.5)
    conv_a_w = nrm((N_EVEN, LRU_CONV, RNN_WIDTH), LRU_CONV ** -0.5)
    conv_a_b = nrm((N_EVEN, RNN_WIDTH), 0.01)
    lru_wr = nrm((N_EVEN, 2, LRU_HEADS, LRU_HEAD_DIM, LRU_HEAD_DIM), LRU_HEAD_DIM ** -0.5)
    lru_br = nrm((N_EVEN, 2, RNN_WIDTH), 0.01)
    lru_wi = nrm((N_EVEN, 2, LRU_HEADS, LRU_HEAD_DIM, LRU_HEAD_DIM), LRU_HEAD_DIM ** -0.5)
    lru_bi = nrm((N_EVEN, 2, RNN_WIDTH), 0.01)
    lo, hi = LRU_A_MIN ** (1.0 / LRU_C), LRU_A_MAX ** (1.0 / LRU_C)
    ua = jax.random.uniform(next(ks), (N_EVEN, 2, RNN_WIDTH), f32, lo, hi)
    lru_lam = jnp.log(ua) - jnp.log1p(-ua)
    conv_b_w = nrm((N_EVEN, HYENA_SHORT_CONV, (HYENA_ORDER + 1) * HYENA_WIDTH), HYENA_SHORT_CONV ** -0.5)
    conv_b_b = nrm((N_EVEN, (HYENA_ORDER + 1) * HYENA_WIDTH), 0.01)
    filt_w1 = nrm((N_EVEN, FILTER_EMB, FILTER_HIDDEN), FILTER_EMB ** -0.5)
    filt_b1 = nrm((N_EVEN, FILTER_HIDDEN), 0.1)
    filt_w2 = nrm((N_EVEN, FILTER_HIDDEN, FILTER_HIDDEN), FILTER_HIDDEN ** -0.5)
    filt_b2 = nrm((N_EVEN, FILTER_HIDDEN), 0.1)
    filt_w3 = nrm((N_EVEN, FILTER_HIDDEN, HYENA_ORDER * 2 * HYENA_WIDTH), 0.1 * FILTER_HIDDEN ** -0.5)
    filt_b3 = nrm((N_EVEN, HYENA_ORDER * 2 * HYENA_WIDTH), 0.01)
    filt_freq = 1.0 + nrm((N_EVEN, 2, FILTER_HIDDEN), 0.1)
    filt_bias = nrm((N_EVEN, HYENA_ORDER, HYENA_WIDTH), 0.5)
    w_out = nrm((N_EVEN, RNN_WIDTH + HYENA_WIDTH, D), (RNN_WIDTH + HYENA_WIDTH) ** -0.5)
    cf_w1 = nrm((N_ODD, D, 2 * D), D ** -0.5)
    cf_b1 = nrm((N_ODD, 2 * D), 0.01)
    cf_dw_w = nrm((N_ODD, CONF_KERNEL, D), CONF_KERNEL ** -0.5)
    cf_dw_b = nrm((N_ODD, D), 0.01)
    cf_ln_g = 1.0 + nrm((N_ODD, D), 0.1)
    cf_ln_b = nrm((N_ODD, D), 0.01)
    cf_w2 = nrm((N_ODD, D, D), D ** -0.5)
    cf_b2 = nrm((N_ODD, D), 0.01)
    router = nrm((DEPTH, D, N_EXPERTS), D ** -0.5)
    exp_w1 = nrm((DEPTH, N_EXPERTS, D, EXPERT_FF), D ** -0.5)
    exp_w3 = nrm((DEPTH, N_EXPERTS, D, EXPERT_FF), D ** -0.5)
    exp_w2 = nrm((DEPTH, N_EXPERTS, EXPERT_FF, D), EXPERT_FF ** -0.5)
    final_g = 1.0 + nrm((D,), 0.1)
    return {"x": x, "c": c, "ctx": ctx, "c_ctx": c_ctx,
            "norm1_g": norm1_g, "norm2_g": norm2_g, "w_mod": w_mod, "b_mod": b_mod,
            "w_in": w_in, "conv_a_w": conv_a_w, "conv_a_b": conv_a_b,
            "lru_wr": lru_wr, "lru_br": lru_br, "lru_wi": lru_wi, "lru_bi": lru_bi, "lru_lam": lru_lam,
            "conv_b_w": conv_b_w, "conv_b_b": conv_b_b,
            "filt_w1": filt_w1, "filt_b1": filt_b1, "filt_w2": filt_w2, "filt_b2": filt_b2,
            "filt_w3": filt_w3, "filt_b3": filt_b3, "filt_freq": filt_freq, "filt_bias": filt_bias,
            "w_out": w_out,
            "cf_w1": cf_w1, "cf_b1": cf_b1, "cf_dw_w": cf_dw_w, "cf_dw_b": cf_dw_b,
            "cf_ln_g": cf_ln_g, "cf_ln_b": cf_ln_b, "cf_w2": cf_w2, "cf_b2": cf_b2,
            "router": router, "exp_w1": exp_w1, "exp_w3": exp_w3, "exp_w2": exp_w2,
            "final_g": final_g}

def second_block(x, c, ctx, c_ctx, norm1_g, norm2_g, w_mod, b_mod,
              w_in, conv_a_w, conv_a_b, lru_wr, lru_br, lru_wi, lru_bi, lru_lam,
              conv_b_w, conv_b_b, filt_w1, filt_b1, filt_w2, filt_b2, filt_w3, filt_b3,
              filt_freq, filt_bias, w_out,
              cf_w1, cf_b1, cf_dw_w, cf_dw_b, cf_ln_g, cf_ln_b, cf_w2, cf_b2,
              router, exp_w1, exp_w3, exp_w2, final_g):
    n_lat = x.shape[1]
    rows = n_lat // GRID_W
    last_ctx_layer = ((DEPTH - 1) // 2) * 2
    xl, xc = x, ctx
    for l in range(DEPTH):
        carry_ctx = l < last_ctx_layer
        sh1, sc1, g1, sh2, sc2, g2 = _adaln(c, w_mod[l], b_mod[l], N_MOD)
        hl = _modulate(_rmsnorm(xl, norm1_g[l]), sh1, sc1)
        if l % 2 == 0 or carry_ctx:
            cm = _adaln(c_ctx[None], w_mod[l], b_mod[l], N_MOD if carry_ctx else 2)
            hc = _modulate(_rmsnorm(xc, norm1_g[l]), cm[0], cm[1])
        if l % 2 == 0:
            e = l // 2
            pe = {'w_in': w_in[e], 'conv_a_w': conv_a_w[e], 'conv_a_b': conv_a_b[e],
                  'lru_wr': lru_wr[e], 'lru_br': lru_br[e], 'lru_wi': lru_wi[e], 'lru_bi': lru_bi[e],
                  'lru_lam': lru_lam[e], 'conv_b_w': conv_b_w[e], 'conv_b_b': conv_b_b[e],
                  'filt_w1': filt_w1[e], 'filt_b1': filt_b1[e], 'filt_w2': filt_w2[e],
                  'filt_b2': filt_b2[e], 'filt_w3': filt_w3[e], 'filt_b3': filt_b3[e],
                  'filt_freq': filt_freq[e], 'filt_bias': filt_bias[e], 'w_out': w_out[e]}
            h0_ctx = jnp.zeros((2, xc.shape[0], RNN_WIDTH), jnp.float32)
            if carry_ctx:
                yc, ctx_state = _even_mixer(hc, pe, h0_ctx)
            else:
                _, ctx_state = _rglru(hc @ pe['w_in'][:, RNN_WIDTH:2 * RNN_WIDTH], pe, h0_ctx)
            yl, _ = _even_mixer(hl, pe, ctx_state)
        else:
            o = l // 2
            po = {'cf_w1': cf_w1[o], 'cf_b1': cf_b1[o], 'cf_dw_w': cf_dw_w[o], 'cf_dw_b': cf_dw_b[o],
                  'cf_ln_g': cf_ln_g[o], 'cf_ln_b': cf_ln_b[o], 'cf_w2': cf_w2[o], 'cf_b2': cf_b2[o]}
            yl = _conformer_conv(hl, po, rows)
            if carry_ctx:
                yc = _conformer_conv(hc, po, None)
        xl = xl + g1 * yl
        xl = xl + g2 * _ec_moe(_modulate(_rmsnorm(xl, norm2_g[l]), sh2, sc2),
                               router[l], exp_w1[l], exp_w3[l], exp_w2[l])
        if carry_ctx:
            xc = xc + cm[2] * yc
            xc = xc + cm[5] * _ec_moe(_modulate(_rmsnorm(xc, norm2_g[l]), cm[3], cm[4]),
                                      router[l], exp_w1[l], exp_w3[l], exp_w2[l])
    return _rmsnorm(xl, final_g)


def setup_inputs(seed=0):
    out = dict(first_inputs(seed))
    for name, value in second_inputs(seed + 1).items():
        if name != "x":
            out[name + "_2"] = value
    return out


def reference(
    x, c, ctx, c_ctx, norm_w, ada_w, ada_b, w_in, w_out, q_norm_a, k_norm_a, rpb_b, sink_c,
    final_norm_w, c_2, ctx_2, c_ctx_2, norm1_g_2, norm2_g_2, w_mod_2, b_mod_2, w_in_2,
    conv_a_w_2, conv_a_b_2, lru_wr_2, lru_br_2, lru_wi_2, lru_bi_2, lru_lam_2, conv_b_w_2,
    conv_b_b_2, filt_w1_2, filt_b1_2, filt_w2_2, filt_b2_2, filt_w3_2, filt_b3_2, filt_freq_2,
    filt_bias_2, w_out_2, cf_w1_2, cf_b1_2, cf_dw_w_2, cf_dw_b_2, cf_ln_g_2, cf_ln_b_2, cf_w2_2,
    cf_b2_2, router_2, exp_w1_2, exp_w3_2, exp_w2_2, final_g_2,
):
    x = first_block(
        x, c, ctx, c_ctx, norm_w, ada_w, ada_b, w_in, w_out, q_norm_a, k_norm_a, rpb_b, sink_c,
        final_norm_w,
    )
    return second_block(
        x, c_2, ctx_2, c_ctx_2, norm1_g_2, norm2_g_2, w_mod_2, b_mod_2, w_in_2, conv_a_w_2,
        conv_a_b_2, lru_wr_2, lru_br_2, lru_wi_2, lru_bi_2, lru_lam_2, conv_b_w_2, conv_b_b_2,
        filt_w1_2, filt_b1_2, filt_w2_2, filt_b2_2, filt_w3_2, filt_b3_2, filt_freq_2,
        filt_bias_2, w_out_2, cf_w1_2, cf_b1_2, cf_dw_w_2, cf_dw_b_2, cf_ln_g_2, cf_ln_b_2,
        cf_w2_2, cf_b2_2, router_2, exp_w1_2, exp_w3_2, exp_w2_2, final_g_2,
    )


_drawn_inputs = setup_inputs


def setup_inputs(seed=0):
    import zlib

    import numpy as np

    out = dict(_drawn_inputs(seed))
    spreads = {}
    factors = {'q_norm_a': 8.0,
     'k_norm_a': 8.0,
     'rpb_b': 8.0,
     'sink_c': 8.0,
     'conv_a_b_2': 3.457,
     'lru_br_2': 64.0,
     'lru_bi_2': 38.52,
     'conv_b_b_2': 7.634,
     'cf_b1_2': 8.0,
     'cf_dw_b_2': 8.0,
     'cf_ln_g_2': 2.8,
     'cf_ln_b_2': 33.04,
     'cf_b2_2': 24.26,
     'norm2_g_2': 2.72}
    for name, (base, spread) in spreads.items():
        noise = np.random.default_rng([zlib.crc32(name.encode()), seed]).standard_normal(out[name].shape)
        drawn = base * np.exp(spread * noise) if base else spread * noise
        out[name] = __import__('jax').numpy.asarray(drawn.astype(out[name].dtype))
    for name, factor in factors.items():
        out[name] = (out[name] * factor).astype(out[name].dtype)
    return out
```

```python
import numpy as np
import concourse.bass as bass
from concourse import mybir
from contextlib import ExitStack

P = 128
D = 1024
KT = D // P
N = 512
NC = 256
NA = N + NC
TT = N // P
DEPTH = 2
HD = 64
GRID_W = 64
ROWS = N // GRID_W
N_EXPERTS = 16
CAP = 2 * N // N_EXPERTS
EPS = 1e-6
RING = 6
UNIT = 2048
MASKED = -1e30
PAIRS = [("B", j) for j in range(4)] + [("A", j) for j in range(4)] + [("C", j) for j in range(4)]
TAPS = ROWS - 1
NF = N

VECTORS = [("norm_w", 16), ("final_norm_w", 8), ("norm1_g", 16), ("norm2_g", 16), ("final_g", 8),
           ("qn", 2), ("kn", 2), ("sink", 16), ("mod_b", 288), ("cvec", 32), ("conv_a_w", 16),
           ("conv_a_b", 4), ("lru_br", 8), ("lru_bi", 8), ("lru_lam", 8), ("conv_b_w", 36),
           ("conv_b_b", 12), ("filt_b1", 1), ("filt_b2", 1), ("filt_f0", 1), ("filt_f1", 1),
           ("filt_bias", 8), ("cf_b1", 16), ("cf_dw_w", (2 * TAPS + 1) * 8), ("cf_dw_b", 8),
           ("cf_ln_g", 8), ("cf_ln_b", 8), ("cf_b2", 8), ("iota", CAP), ("kscale", 4)]
NV = sum(n for _, n in VECTORS)
VOFF = {}
_at = 0
for _name, _n in VECTORS:
    VOFF[_name] = _at
    _at += _n
CONSTS = [("ident", P), ("blk", P), ("ones", P), ("rot", P), ("cos", N), ("sin", N),
          ("mprev", P), ("mnext", P), ("sel", 2)]
NK = sum(n for _, n in CONSTS)
COFF = {}
_at = 0
for _name, _n in CONSTS:
    COFF[_name] = _at
    _at += _n
MOD_AT = [0, 48, 96, 192]
MOD_TILES = [24, 24, 48, 48]
BIAS_SLOTS = 3
MOD_UNITS = 3
MOD_STEPS = [n // (2 * MOD_UNITS) for n in MOD_TILES]


def insertions(layer):
    mods = [1] * 4 + [2] * 6 if layer == 0 else [2] * 2 + [3] * 8
    out = []
    for i, (kind, j) in enumerate(PAIRS):
        own = []
        if kind == "B" or j == 0:
            own += [("k", i), ("v", i)]
        own += [("q", i), ("g", i)]
        if kind != "B":
            for what in (("k", "q") if j == 0 else ("q",)):
                if kind == "A":
                    own.append(("norm_" + what, i))
                own.append(("rope_" + what, i))
        if 0 < i <= 10:
            own = [("mod_rows", mods[i - 1])] + own + [("mod_cols", mods[i - 1])]
        out.append(own)
    return out


def schedule(layer):
    tiles = 6 if layer == 0 else 4
    steps = [(i, h, t) for i in range(len(PAIRS)) for t in range(tiles) for h in range(2)]
    per = 2 * tiles
    inserted = insertions(layer)
    order = list(inserted[0])
    last = len(steps) - 1
    for n in range(-1, last + 2):
        if n + 1 <= last:
            order.append(("S", n + 1))
        if 0 <= n - 1 and n % 2 == 0:
            order.append(("O", n - 1))
        if 0 <= n <= last:
            order.append(("T", n))
        if n + 1 <= last:
            order.append(("E", n + 1))
        if 0 <= n <= last:
            i, at = divmod(n, per)
            if i + 1 < len(PAIRS):
                todo = inserted[i + 1]
                room = per - 2
                for x, item in enumerate(todo):
                    if x * room // len(todo) == at:
                        order.append(item)
    return steps, order


def unit_order():
    first = [("ada", 0, u) for u in range(12)]
    mods = {1: [("ada", 1, u) for u in range(12)], 2: [("w_mod", 0, u) for u in range(24)],
            3: [("w_mod", 1, u) for u in range(24)]}
    for layer in range(DEPTH):
        u = 0
        for item in schedule(layer)[1]:
            if item[0] in ("k", "q"):
                first.append(("w_in", layer, u))
                u += 1
            elif item[0] == "mod_rows":
                first += [mods[item[1]].pop(0) for _ in range(MOD_UNITS)]
        first += [("w_out", layer, m) for m in range(KT)]
    first += [("w_in_2", 0, u) for u in range(10)] + [("lru", 0, 0), ("filt_w3", 0, 0)]
    first += [("w_out_2", 0, u) for u in range(4)]
    second = [("cf_w1", 0, u) for u in range(8)] + [("cf_w2", 0, u) for u in range(4)]
    return first, second


class Count:

    def __init__(self):
        self.big = self.pt = 0
        self.seen = {}
        self.i, self.per, self.at_start = None, {}, {}

    def value(self, value, per=0):
        return value if self.i is None else self.i * per + value

    def next(self, name, k=1):
        self.seen[name] = self.seen.get(name, 0) + k
        return self.value(self.seen[name], self.per.get(name, 0))

    def next_big(self):
        self.big += 1
        return self.big - 1

    def next_pt(self):
        self.pt += 1
        return self.pt - 1

    def fills(self, k):
        return self.value(k + 1, self.per.get("big", 0))

    def over(self, k):
        return self.value(k // 2 + 1, self.per.get("big", 0) // 2)

    def pt_fills(self, m):
        return self.value(m + 1, self.per.get("pt", 0))

    def pt_over(self, m):
        return self.value(m + 1, self.per.get("pt", 0))

    def enter(self, i, per):
        self.i, self.per = i, per
        self.at_start = dict(self.seen, big=self.big, pt=self.pt)

    def leave(self, iterations):
        now = dict(self.seen, big=self.big, pt=self.pt)
        for name, value in now.items():
            grown = value - self.at_start.get(name, 0)
            assert grown == self.per.get(name, 0), (name, grown, self.per)
        for name, per in self.per.items():
            if name not in ("big", "pt") and name in self.seen:
                self.seen[name] += per * (iterations - 1)
        self.big += self.per["big"] * (iterations - 1)
        self.pt += self.per["pt"] * (iterations - 1)
        self.i, self.per = None, {}


def build(nc, A):
    F = mybir.dt.float32
    ALU = mybir.AluOpType
    ACT = mybir.ActivationFunctionType
    AX = mybir.AxisListType
    first_units, second_units = unit_order()
    MOE_UNITS = 24
    MOE_PAIRS = N_EXPERTS // 2
    moe_base = [len(first_units), len(first_units) + MOE_UNITS * MOE_PAIRS + len(second_units)]

    with ExitStack() as ctx:
        def sb(name, shape):
            return ctx.enter_context(nc.sbuf_tensor(name, shape, F))

        def pb(name, shape):
            return ctx.enter_context(nc.psum_tensor(name, shape, F))

        W = sb("W", [P, RING, UNIT])
        XC = sb("XC", [P, KT, NA])
        HT = sb("HT", [P, KT, NA])
        CONST = sb("CONST", [P, NK])
        VEC = sb("VEC", [P, NV])
        MOD = sb("MOD", [P, 288])
        CCS = sb("CCS", [P, 64])
        COEF = sb("COEF", [P, 16])
        EPSC = sb("EPSC", [P, 2])
        RS = sb("RS", [P, NA])
        STAT = sb("STAT", [P, 12])
        ARENA_N = 24200
        ARENA = sb("ARENA", [P, ARENA_N])

        BIG = [pb(f"BIG{s}", [P, 1024]) for s in range(2)]
        PT = pb("PT", [P, 1024])
        OP = pb("OP", [P, 512])
        MODP = pb("MODP", [P, 512])

        def const(name, a=0, n=None):
            n = n if n is not None else dict(CONSTS)[name]
            return CONST[:, COFF[name] + a:COFF[name] + a + n]

        def vec(name, a, n=1):
            return VEC[:, VOFF[name] + a:VOFF[name] + a + n]

        def mod(group, chunk, tile, which):
            c = MOD_AT[group] + 2 * (chunk * KT + tile) + which
            return MOD[:, c:c + 1]

        def mod_row(group, chunk, which):
            c = MOD_AT[group] + 2 * chunk * KT + which
            return MOD[:, c:c + 2 * KT - 1:2]

        class Arena:
            def __init__(self):
                self.at = 0

            def __call__(self, *shape):
                n = int(np.prod(shape))
                view = ARENA[:, self.at:self.at + n]
                self.at += n
                assert self.at <= ARENA_N, self.at
                if len(shape) == 2:
                    return view.rearrange("p (a b) -> p a b", b=shape[1])
                if len(shape) == 3:
                    return view.rearrange("p (a b c) -> p a b c", b=shape[1], c=shape[2])
                return view

        at = Arena()
        U = at(12, NA)
        Q = at(2, NA)
        K = at(2, NA)
        V = at(2, 6, P)
        SQT = at(NA)
        GATE_T = at(NA)
        SG = at(2, NA)
        PROB = at(2, NA + 1)
        PTS = at(2, NA)
        RB = at(2, HD)
        BIAS = at(BIAS_SLOTS, 16 * HD)
        ROPE_T = at(N)
        at = Arena()
        HY = at(12, N)
        YA = at(4, N)
        lru_start = at.at
        GATE = at(4, N)
        XAC = at(4, N)
        CXC = at(4, NC)
        IX = at(8, NA)
        raw_start = at.at
        XAR = at(4, N + 4)
        CXR = at(4, NC + 4)
        HYR = at(2, N + 4)
        at.at = raw_start
        LA = at(2, NA)
        LT = at(NA)
        LH = at(2, NA)
        SPT = at(8, 8)
        LR = HT[:, :, :]
        at.at = lru_start
        COS_T = at(4, NF)
        SIN_T = at(4, NF)
        NYQ_T = at(4, P)
        ALT_T = at(N)
        WIN = at(4, N)
        KF = at(8, N)
        ZF = at(8, N)
        FSMALL = ZF[:, 0:2, :].rearrange("p a b -> p (a b)")
        HID1, HARG, HRND = (ZF[:, 2 + x, :] for x in range(3))
        HID2 = at(N)
        HTF = HT[:, :, :].rearrange("p a b -> p (a b)")
        FS, FD, UT = (HTF[:, x * 2048:(x + 1) * 2048].rearrange("p (a b) -> p a b", b=N) for x in range(3))
        at = Arena()
        CU = at(KT, N)
        CY = at(KT, N)
        CSIG = at(2, N)
        CFT = at(2, N)
        at = Arena()
        HTOK = at(TT, D)
        XS = at(KT, P)
        HX = at(D)
        HXT = at(KT, P)
        SIL = at(D)
        YK = at(D)
        ONEH = at(TT, 2, CAP)
        GONEH = at(TT, 2, CAP)
        GSCAT = at(N)
        ROUTER = at(KT, N_EXPERTS)
        PROBS = at(TT, N_EXPERTS)
        SLOT = at(TT, N_EXPERTS + 2)
        ROW0, ROW1, ROW2, ROW3 = at(N), at(N), at(N), at(N)
        MAX8 = at(8)
        SMALL = at(16)

        def sem(name):
            return ctx.enter_context(nc.semaphore(name))

        consts_loaded = sem("consts_loaded")
        x_loaded = sem("x_loaded")
        ctx2_loaded = sem("ctx2_loaded")
        unit_loaded = [sem(f"unit_loaded{s}") for s in range(RING)]
        unit_used = sem("unit_used")
        big_filled = sem("big_filled")
        big_free = [sem("big_free0"), sem("big_free1")]
        pt_filled = sem("pt_filled")
        pt_free = sem("pt_free")
        cvec_ready = sem("cvec_ready")
        mods_filled = sem("mods_filled")
        eps_ready = sem("eps_ready")
        squares = sem("squares")
        rs_ready = sem("rs_ready")
        h_scaled = sem("h_scaled")
        h_ready = sem("h_ready")
        qk_squared = sem("qk_squared")
        qk_rs = sem("qk_rs")
        qk_normed = sem("qk_normed")
        qk_roped = sem("qk_roped")
        gate_tanh = sem("gate_tanh")
        max_ready = sem("max_ready")
        sums_inverted = sem("sums_inverted")
        o_filled = sem("o_filled")
        y_ready = sem("y_ready")
        bias_loaded = [sem(f"bias_loaded{s}") for s in range(BIAS_SLOTS)]
        bias_used = sem("bias_used")
        act_chain = sem("act_chain")
        dve_chain = sem("dve_chain")
        pads_ready = sem("pads_ready")
        xa_ready = sem("xa_ready")
        hy_ready = sem("hy_ready")
        lam_exp = sem("lam_exp")
        decay_ready = sem("decay_ready")
        lru_gates = sem("lru_gates")
        lru_a = sem("lru_a")
        lru_v = sem("lru_v")
        lru_sqrt = sem("lru_sqrt")
        lru_scanned = sem("lru_scanned")
        lru_done = sem("lru_done")
        hyena_loaded = sem("hyena_loaded")
        sin_arg = sem("sin_arg")
        sin_ready = sem("sin_ready")
        filt_ready = sem("filt_ready")
        spec_ready = sem("spec_ready")
        glu_sig = sem("glu_sig")
        dw_base = sem("dw_base")
        dw_ready = sem("dw_ready")
        centred = sem("centred")
        ln_scaled = sem("ln_scaled")
        cf_add = sem("cf_add")
        router_loaded = sem("router_loaded")
        block_done = sem("block_done")
        probs_ready = sem("probs_ready")
        slots_ready = sem("slots_ready")
        logits_exp = sem("logits_exp")
        onehot_ready = sem("onehot_ready")
        gates_ready = sem("gates_ready")
        out_ready = sem("out_ready")
        out_stored = sem("out_stored")

        def key_tiles(kind, t):
            if t >= TT:
                return [4, 5]
            if kind == "C":
                return list(range(max(t - 1, 0), min(t + 1, TT - 1) + 1)) + [4, 5]
            return list(range(6))

        def score_span(kind, t):
            b = NA + (kind == "C")
            if t >= TT:
                return N, b
            if kind == "C":
                return N - (min(t + 1, TT - 1) + 1 - max(t - 1, 0)) * P, b
            return 0, b

        block = ctx.enter_context(nc.Block())
        PER_PAIR = {"big": 8, "pt": 2}

        @block.sync
        def _(sp):
            sp.dma_start(CONST[:, :], A["consts"]).then_inc(consts_loaded, 16)
            sp.dma_start(VEC[:, :], A["vecs"]).then_inc(consts_loaded, 16)

            def load(n, src):
                if n >= RING:
                    sp.wait_ge(unit_used, n - RING + 1)
                sp.dma_start(W[:, n % RING, :], src).then_inc(unit_loaded[n % RING], 16)

            def stream(base, source, count, start):
                done = start
                rounds = (count - done) // RING
                with sp.Fori(0, rounds) as i:
                    for s in range(RING):
                        n = base + done + s
                        sp.wait_ge(unit_used, i * RING + (n - RING + 1))
                        sp.dma_start(W[:, n % RING, :],
                                     source[bass.ds(i * RING + done + s, 1)].rearrange("a p n -> p (a n)"))\
                          .then_inc(unit_loaded[n % RING], 16)
                for u in range(done + rounds * RING, count):
                    load(base + u, source[u])

            def experts(layer, base):
                srcs = [A[w][layer].rearrange("e (q k p) n -> (e q) p k n", k=2, p=P)
                        for w in ("exp_w1", "exp_w3", "exp_w2")]
                with sp.Fori(0, MOE_PAIRS) as i:
                    for s in range(MOE_UNITS):
                        which, q, expert = s // 8, s % 8 // 2, s % 2
                        n = base + s
                        sp.wait_ge(unit_used, i * MOE_UNITS + (n - RING + 1))
                        sp.dma_start(W[:, n % RING, :].rearrange("p (k n) -> p k n", k=2),
                                     srcs[which][bass.ds(i * 8 + (4 * expert + q), 1)]
                                     .rearrange("a p k n -> p (a k) n"))\
                          .then_inc(unit_loaded[n % RING], 16)

            for n in range(RING):
                load(n, A["units1"][n])
                if n == 2:
                    sp.dma_start(XC[:, :, :], A["x0"]).then_inc(x_loaded, 16)
            stream(0, A["units1"], len(first_units), RING)
            experts(0, moe_base[0])
            stream(moe_base[0] + MOE_UNITS * MOE_PAIRS, A["units2"], len(second_units), 0)
            experts(1, moe_base[1])
            for k in range(KT):
                sp.wait_ge(out_ready, k + 1)
                sp.dma_start(A["out"][:, k, :], HT[:, k, 0:N]).then_inc(out_stored, 16)
            sp.wait_ge(out_stored, 16 * KT)

        @block.gpsimd
        def _(pool):
            for layer in range(DEPTH):
                for h in range(8):
                    n = 8 * layer + h
                    if n >= BIAS_SLOTS:
                        pool.wait_ge(bias_used, n - BIAS_SLOTS + 1)
                    pool.dma_start(BIAS[:, n % BIAS_SLOTS, :], A["bias_b"][layer, h])\
                        .then_inc(bias_loaded[n % BIAS_SLOTS], 16)
            pool.wait_ge(h_scaled, 2 * KT)
            pool.dma_start(XC[:, :, N:NA], A["ctx2"]).then_inc(ctx2_loaded, 16)
            pool.wait_ge(lru_done, 4)
            for dst, name in ((COS_T, "dft_cos"), (SIN_T, "dft_sin"), (NYQ_T, "dft_nyq"), (WIN, "window")):
                pool.dma_start(dst, A[name]).then_inc(hyena_loaded, 16)
            pool.dma_start(ALT_T[0:1, :], A["dft_alt"]).then_inc(hyena_loaded, 16)
            pool.dma_start(FSMALL[:, 0:640], A["filt_small"]).then_inc(hyena_loaded, 16)
            for layer in range(DEPTH):
                pool.wait_ge(h_ready, KT * (4 + 3 * layer))
                pool.dma_start(ROUTER, A["router"][layer]).then_inc(router_loaded, 16)

        @block.tensor
        def _(pe):
            me = Count()
            unit = {"n": 0, "open": 0}

            def mm(out, lhsT, rhs, start, stop):
                ins = pe.matmul(out, lhsT, rhs, start=start, stop=stop)
                if unit["open"]:
                    assert not (start and stop)
                    ins.then_inc(unit_used, unit["open"])
                    unit["open"] = 0
                return ins

            def next_unit():
                n = unit["n"]
                unit["n"] += 1
                per = 16 * MOE_UNITS // RING
                pe.wait_ge(unit_loaded[n % RING], me.value(16 * (n // RING + 1), per))
                return W[:, n % RING, :]

            def unit_done():
                unit["open"] += 1

            def mod_rows(group):
                k_use = me.next_big()
                if k_use >= 2:
                    pe.wait_ge(big_free[k_use % 2], me.over(k_use - 2))
                v = 0 if group < 2 else 2
                for x in range(MOD_UNITS):
                    w = next_unit().rearrange("p (k n) -> p k n", k=KT)
                    for half in range(2):
                        for j in range(4):
                            c = 4 * (4 * half + j) + v
                            last = mm(BIG[k_use % 2][32 * j:32 * j + 32, x * 256:x * 256 + 256],
                                      CCS[:, c:c + 32], w[:, 4 * half + j, :], half == 0, half == 1)
                    unit_done()
                last.then_inc(big_filled, 1)
                mod_use[0] = k_use

            def mod_cols(group):
                pe.wait_ge(big_free[mod_use[0] % 2], me.over(mod_use[0]))
                at = MOD_AT[group] + 2 * 2 * MOD_UNITS * mods_done[group]
                for x in range(2 * MOD_UNITS):
                    last = pe.matmul(MODP[:, at + 2 * x:at + 2 * x + 2], RS[:, x * P:x * P + P], const("sel"),
                                     start=True, stop=True)
                last.then_inc(mods_filled, 1)
                mods_done[group] += 1

            mods_done = [0, 0, 0, 0]
            mod_use = [0]

            def project(w, cols, src, n, K_TILES=KT):
                k_use = me.next_big()
                if k_use >= 2:
                    pe.wait_ge(big_free[k_use % 2], me.over(k_use - 2))
                out = BIG[k_use % 2]
                for k in range(K_TILES):
                    lhsT = w[:, k, cols]
                    last = mm(out[:, 0:N], lhsT, src[:, k, 0:N], k == 0, k == K_TILES - 1)
                if n > N:
                    for k in range(K_TILES):
                        last = mm(out[:, N:n], w[:, k, cols], src[:, k, N:n], k == 0, k == K_TILES - 1)
                last.then_inc(big_filled, 1)
                return k_use

            def norm_sums(n):
                k_use = me.next_big()
                if k_use >= 2:
                    pe.wait_ge(big_free[k_use % 2], me.over(k_use - 2))
                out = BIG[k_use % 2]
                for k in range(KT):
                    pe.wait_ge(squares, me.next("squares"))
                    last = mm(out[:, 0:N], const("ones"), HT[:, k, 0:N], k == 0, k == KT - 1)
                if n > N:
                    for k in range(KT):
                        last = mm(out[:, N:n], const("ones"), HT[:, k, N:n], k == 0, k == KT - 1)
                last.then_inc(big_filled, 1)

            def attention(layer):
                steps, order = schedule(layer)
                nq = NA if layer == 0 else N
                pe.wait_ge(h_ready, me.next("h_ready", KT))
                score_use, probs_at, k_ready, q_ready = {}, {}, {}, {}
                raw_use = {}
                kv = {"n": -1}
                buf_of = {}
                w = None
                for what, x in order:
                    if what == "mod_rows":
                        mod_rows(x)
                    elif what == "mod_cols":
                        mod_cols(x)
                    elif what == "k":
                        w = next_unit().rearrange("p (k n) -> p k n", k=KT)
                        raw_use["k", x] = project(w, slice(0, P), HT, NA)
                        kv["n"] += 1
                        if PAIRS[x][0] == "B":
                            k_ready[x] = ("use", raw_use["k", x])
                    elif what == "v":
                        k_use = me.next_big()
                        if k_use >= 2:
                            pe.wait_ge(big_free[k_use % 2], me.over(k_use - 2))
                        for t in range(6):
                            for k in range(KT):
                                last = mm(BIG[k_use % 2][:, t * P:t * P + P], HT[:, k, t * P:t * P + P],
                                          w[:, k, P:2 * P], k == 0, k == KT - 1)
                        last.then_inc(big_filled, 1)
                        unit_done()
                        k_ready["v", x] = k_use
                    elif what == "q":
                        w = next_unit().rearrange("p (k n) -> p k n", k=KT)
                        raw_use["q", x] = project(w, slice(0, P), HT, nq)
                        buf_of[x] = kv["n"] % 2
                        if PAIRS[x][0] == "B":
                            q_ready[x] = ("use", raw_use["q", x])
                    elif what == "g":
                        project(w, slice(P, 2 * P), HT, nq)
                        unit_done()
                    elif what.startswith("norm_"):
                        pe.wait_ge(qk_squared, me.next("qk_squared"))
                        n = NA if what == "norm_k" else nq
                        k_use = me.next_big()
                        if k_use >= 2:
                            pe.wait_ge(big_free[k_use % 2], me.over(k_use - 2))
                        last = pe.matmul(BIG[k_use % 2][:, 0:N], const("blk"), SQT[:, 0:N],
                                         start=True, stop=True)
                        if n > N:
                            last = pe.matmul(BIG[k_use % 2][:, N:n], const("blk"), SQT[:, N:n],
                                             start=True, stop=True)
                        last.then_inc(big_filled, 1)
                    elif what.startswith("rope_"):
                        if PAIRS[x][0] == "A":
                            pe.wait_ge(qk_normed, me.next("qk_normed"))
                        else:
                            pe.wait_ge(big_free[(raw_use[what[5:], x]) % 2], me.over(raw_use[what[5:], x]))
                        src = K[:, kv["n"] % 2, 0:N] if what == "rope_k" else Q[:, x % 2, 0:N]
                        k_use = me.next_big()
                        if k_use >= 2:
                            pe.wait_ge(big_free[k_use % 2], me.over(k_use - 2))
                        pe.matmul(BIG[k_use % 2][:, 0:N], const("rot"), src, start=True, stop=True)\
                            .then_inc(big_filled, 1)
                        (k_ready if what == "rope_k" else q_ready)[x] = ("roped", None)
                    elif what == "S":
                        i, h, t = steps[x]
                        kind, j = PAIRS[i]
                        if h == 0 and t == 0:
                            for ready in (k_ready, q_ready):
                                if i in ready:
                                    how, use = ready[i]
                                    if how == "use":
                                        pe.wait_ge(big_free[use % 2], me.over(use))
                                    else:
                                        pe.wait_ge(qk_roped, me.next("qk_roped"))
                        k_use = score_use[x] = me.next_big()
                        if k_use >= 2:
                            pe.wait_ge(big_free[k_use % 2], me.over(k_use - 2))
                        out = BIG[k_use % 2]
                        rows = slice(HD * h, HD * h + HD)
                        lhsT = Q[rows, i % 2, t * P:t * P + P]
                        keys = K[:, buf_of[i], :]
                        if t < TT:
                            if kind == "C":
                                a, b = max(t - 1, 0), min(t + 1, TT - 1) + 1
                                pe.matmul(out[:, N - (b - a) * P:N], lhsT, keys[rows, a * P:b * P],
                                          start=True, stop=True)
                            else:
                                pe.matmul(out[:, 0:N], lhsT, keys[rows, 0:N], start=True, stop=True)
                        pe.matmul(out[:, N:NA], lhsT, keys[rows, N:NA], start=True, stop=True)\
                            .then_inc(big_filled, 1)
                    elif what == "T":
                        i, h, t = steps[x]
                        pe.wait_ge(big_free[score_use[x] % 2], me.over(score_use[x]))
                        m = probs_at[x] = me.next_pt()
                        if m >= 1:
                            pe.wait_ge(pt_free, me.pt_over(m - 1))
                        tiles = key_tiles(PAIRS[i][0], t)
                        for y in range(len(tiles)):
                            last = pe.transpose(PT[:, y * P:y * P + P], PROB[:, x % 2, y * P:y * P + P],
                                                const("ident"))
                        last.then_inc(pt_filled, 1)
                    elif what == "O":
                        i, h, t = steps[x]
                        kind = PAIRS[i][0]
                        pe.wait_ge(pt_free, me.pt_over(probs_at[x]))
                        if ("v", i) in k_ready and t == 0:
                            pe.wait_ge(big_free[k_ready["v", i] % 2], me.over(k_ready["v", i]))
                        if y_before[layer] + x // 2:
                            pe.wait_ge(y_ready, y_before[layer] + x // 2)
                        tiles = key_tiles(kind, t)
                        for y, tile in enumerate(tiles):
                            for head in range(2):
                                pe.matmul(OP[head * HD:head * HD + HD, 0:P],
                                          V[:, buf_of[i], tile, head * HD:head * HD + HD],
                                          PTS[:, head, y * P:y * P + P], start=y == 0, stop=y == len(tiles) - 1)
                        pe.wait_ge(sums_inverted, me.next("sums_inverted"))
                        pe.matmul(OP[:, P:2 * P], RB.rearrange("p h d -> p (h d)"), const("ident"),
                                  start=True, stop=True).then_inc(o_filled, 1)
                pe.wait_ge(y_ready, y_before[layer] + len(steps) // 2)
                for m in range(KT):
                    w = next_unit()[:, 0:12 * P].rearrange("p (k n) -> p k n", k=12)
                    project(w, slice(0, P), U, nq, 12)
                    unit_done()

            def even_layer():
                pe.wait_ge(h_ready, me.next("h_ready", KT))
                for u in range(10):
                    w = next_unit().rearrange("p (k n) -> p k n", k=KT)
                    for half in range(2):
                        project(w, slice(half * P, half * P + P), HT, NA if u < 2 else N)
                    unit_done()
                w = next_unit().rearrange("p (g n) -> p g n", n=P)
                pe.wait_ge(xa_ready, me.next("xa_ready", 4))
                for t in range(4):
                    for d in range(2):
                        for g in range(2):
                            k_use = me.next_big()
                            if k_use >= 2:
                                pe.wait_ge(big_free[k_use % 2], me.over(k_use - 2))
                            lhsT = w[:, (g * 2 + d) * 4 + t, :]
                            out = BIG[k_use % 2]
                            ins = pe.matmul(out[:, 0:N], lhsT, XAC[:, t, :], start=True, stop=True)
                            if unit["open"]:
                                ins.then_inc(unit_used, unit["open"])
                                unit["open"] = 0
                            pe.matmul(out[:, N:NA], lhsT, CXC[:, t, :], start=True, stop=True)\
                                .then_inc(big_filled, 1)
                unit_done()
                pe.wait_ge(hyena_loaded, me.next("hyena_loaded", 96))
                k_use = me.next_big()
                if k_use >= 2:
                    pe.wait_ge(big_free[k_use % 2], me.over(k_use - 2))
                pe.matmul(BIG[k_use % 2][0:64, 0:N], FSMALL[0:33, 0:64], FSMALL[0:33, 128:640],
                          start=True, stop=True).then_inc(big_filled, 1)
                pe.wait_ge(sin_ready, me.next("sin_ready"))
                k_use = me.next_big()
                if k_use >= 2:
                    pe.wait_ge(big_free[k_use % 2], me.over(k_use - 2))
                pe.matmul(BIG[k_use % 2][0:64, 0:N], FSMALL[0:64, 64:128], HID1[0:64, :],
                          start=True, stop=True).then_inc(big_filled, 1)
                pe.wait_ge(sin_ready, me.next("sin_ready"))
                w = next_unit()
                for o in range(2):
                    for t in range(TT):
                        k_use = me.next_big()
                        if k_use >= 2:
                            pe.wait_ge(big_free[k_use % 2], me.over(k_use - 2))
                        for way in range(2):
                            c = (o * 2 + way) * 512
                            ins = pe.matmul(BIG[k_use % 2][:, way * N:way * N + N], HID2[0:65, t * P:t * P + P],
                                            w[0:65, c:c + 512], start=True, stop=True)
                            if way == 0 and unit["open"]:
                                ins.then_inc(unit_used, unit["open"])
                                unit["open"] = 0
                        ins.then_inc(big_filled, 1)
                    if o == 1:
                        unit_done()
                    pe.wait_ge(filt_ready, me.next("filt_ready", TT))
                    for f in range(4):
                        k_use = me.next_big()
                        if k_use >= 2:
                            pe.wait_ge(big_free[k_use % 2], me.over(k_use - 2))
                        out = BIG[k_use % 2]
                        fs = slice(f * P, f * P + P)
                        for t in range(TT):
                            mm(out[:, 0:N], COS_T[:, t, fs], FS[:, t, :], t == 0, t == TT - 1)
                        for t in range(TT):
                            last = mm(out[:, N:1024], SIN_T[:, t, fs], FD[:, t, :], t == 0, t == TT - 1 and f > 0)
                        if f == 0:
                            for t in range(TT):
                                last = mm(out[:, N:1024], NYQ_T[:, t, :], FS[:, t, :], False, t == TT - 1)
                        last.then_inc(big_filled, 1)
                        spec_use = k_use
                    if o == 0:
                        pe.wait_ge(hy_ready, 12)
                    else:
                        pe.wait_ge(big_free[conv_use % 2], me.over(conv_use))
                    for half in range(2):
                        k_use = me.next_big()
                        if k_use >= 2:
                            pe.wait_ge(big_free[k_use % 2], me.over(k_use - 2))
                        for t in range(2):
                            for c in range(4):
                                tok = (2 * half + t) * P
                                last = pe.transpose(BIG[k_use % 2][:, t * N + c * P:t * N + c * P + P],
                                                    HY[:, c, tok:tok + P], const("ident"))
                        last.then_inc(big_filled, 1)
                    pe.wait_ge(big_free[k_use % 2], me.over(k_use))
                    pe.wait_ge(big_free[(k_use - 1) % 2], me.over(k_use - 1))
                    for f in range(4):
                        k_use = me.next_big()
                        if k_use >= 2:
                            pe.wait_ge(big_free[k_use % 2], me.over(k_use - 2))
                        out = BIG[k_use % 2]
                        fs = slice(f * P, f * P + P)
                        for t in range(TT):
                            mm(out[:, 0:N], COS_T[:, t, fs], UT[:, t, :], t == 0, t == TT - 1)
                        for t in range(TT):
                            last = mm(out[:, N:1024], SIN_T[:, t, fs], UT[:, t, :], t == 0, t == TT - 1 and f > 0)
                        if f == 0:
                            for t in range(TT):
                                last = mm(out[:, N:1024], NYQ_T[:, t, :], UT[:, t, :], False, t == TT - 1)
                        last.then_inc(big_filled, 1)
                    pe.wait_ge(spec_ready, me.next("spec_ready", 4))
                    for c in range(4):
                        k_use = me.next_big()
                        if k_use >= 2:
                            pe.wait_ge(big_free[k_use % 2], me.over(k_use - 2))
                        out = BIG[k_use % 2][:, 0:N]
                        cs = slice(c * P, c * P + P)
                        for f in range(4):
                            mm(out, ZF[:, f, cs], COS_T[:, f, :], f == 0, False)
                        for f in range(4):
                            mm(out, ZF[:, 4 + f, cs], SIN_T[:, f, :], False, False)
                        mm(out, ZF[0:1, 4, cs], ALT_T[0:1, :], False, True).then_inc(big_filled, 1)
                        conv_use = k_use
                pe.wait_ge(big_free[conv_use % 2], me.over(conv_use))
                pe.wait_ge(big_free[(conv_use - 1) % 2], me.over(conv_use - 1))
                for u in range(4):
                    w = next_unit().rearrange("p (k n) -> p k n", k=KT)
                    for half in range(2):
                        k_use = me.next_big()
                        if k_use >= 2:
                            pe.wait_ge(big_free[k_use % 2], me.over(k_use - 2))
                        for k in range(KT):
                            src = YA[:, k, :] if k < 4 else HY[:, k - 4, :]
                            last = mm(BIG[k_use % 2][:, 0:N], w[:, k, half * P:half * P + P], src,
                                      k == 0, k == KT - 1)
                        last.then_inc(big_filled, 1)
                    unit_done()

            def conformer():
                pe.wait_ge(h_ready, me.next("h_ready", KT))
                for j in range(KT):
                    w = next_unit().rearrange("p (k n) -> p k n", k=KT)
                    k_use = me.next_big()
                    if k_use >= 2:
                        pe.wait_ge(big_free[k_use % 2], me.over(k_use - 2))
                    for half in range(2):
                        for k in range(KT):
                            last = mm(BIG[k_use % 2][:, half * N:half * N + N], w[:, k, half * P:half * P + P],
                                      HT[:, k, 0:N], k == 0, k == KT - 1)
                    last.then_inc(big_filled, 1)
                    unit_done()
                for what, ready, src in (("dw_ready", dw_ready, CY), ("squares", squares, HT)):
                    k_use = me.next_big()
                    if k_use >= 2:
                        pe.wait_ge(big_free[k_use % 2], me.over(k_use - 2))
                    for k in range(KT):
                        pe.wait_ge(ready, me.next(what))
                        last = mm(BIG[k_use % 2][:, 0:N], const("ones"), src[:, k, 0:N], k == 0, k == KT - 1)
                    last.then_inc(big_filled, 1)
                pe.wait_ge(h_ready, me.next("h_ready", KT))
                for u in range(4):
                    w = next_unit().rearrange("p (k n) -> p k n", k=KT)
                    for half in range(2):
                        project(w, slice(half * P, half * P + P), CU, N)
                    unit_done()

            def experts(layer):
                pe.wait_ge(h_ready, me.next("h_ready", KT))
                for t in range(TT):
                    k_use = me.next_big()
                    if k_use >= 2:
                        pe.wait_ge(big_free[k_use % 2], me.over(k_use - 2))
                    for k in range(KT):
                        last = pe.transpose(BIG[k_use % 2][:, k * P:k * P + P], HT[:, k, t * P:t * P + P],
                                            const("ident"))
                    last.then_inc(big_filled, 1)
                tok_use = k_use
                pe.wait_ge(router_loaded, me.next("router_loaded", 16))
                m_pt = me.next_pt()
                if m_pt >= 1:
                    pe.wait_ge(pt_free, me.pt_over(m_pt - 1))
                for t in range(TT):
                    for k in range(KT):
                        last = mm(PT[:, t * 16:t * 16 + 16], HT[:, k, t * P:t * P + P], ROUTER[:, k, :],
                                  k == 0, k == KT - 1)
                last.then_inc(pt_filled, 1)
                pe.wait_ge(probs_ready, me.next("probs_ready"))
                m_pt = me.next_pt()
                if m_pt >= 1:
                    pe.wait_ge(pt_free, me.pt_over(m_pt - 1))
                for t in range(TT):
                    last = pe.transpose(PT[0:16, t * P:t * P + P], PROBS[:, t, :], const("ident"))
                last.then_inc(pt_filled, 1)
                pe.wait_ge(slots_ready, me.next("slots_ready"))
                m_pt = me.next_pt()
                if m_pt >= 1:
                    pe.wait_ge(pt_free, me.pt_over(m_pt - 1))
                for t in range(TT):
                    last = pe.transpose(PT[:, t * 16:t * 16 + 16], ROW1[0:16, t * P:t * P + P],
                                        const("ident")[0:16, 0:16])
                last.then_inc(pt_filled, 1)
                pe.wait_ge(big_free[tok_use % 2], me.over(tok_use))
                pe.wait_ge(big_free[(tok_use - 1) % 2], me.over(tok_use - 1))
                assert not unit["open"] and unit["n"] == moe_base[layer]

                def gather():
                    pe.wait_ge(onehot_ready, me.next("onehot_ready"))
                    k_use = me.next_big()
                    pe.wait_ge(big_free[k_use % 2], me.over(k_use - 2))
                    for k in range(KT):
                        for t in range(TT):
                            last = mm(BIG[k_use % 2][:, k * P:k * P + P], HTOK[:, t, k * P:k * P + P],
                                      ONEH[:, t, :, :].rearrange("p a b -> p (a b)"), t == 0, t == TT - 1)
                    last.then_inc(big_filled, 1)
                    return k_use

                k_use = gather()
                pe.wait_ge(big_free[k_use % 2], me.over(k_use))
                with pe.Fori(0, MOE_PAIRS) as i:
                    me.enter(i, dict(PER_PAIR, onehot_ready=1, gates_ready=1))

                    def both_experts(out, rows):
                        for q in range(4):
                            w = [next_unit().rearrange("p (k n) -> p k n", k=2) for _ in range(2)]
                            for k in range(2):
                                for half in range(2):
                                    for e in range(2):
                                        last = mm(out[e * CAP:e * CAP + CAP, half * 512:half * 512 + 512],
                                                  rows[:, 2 * q + k, e * CAP:e * CAP + CAP],
                                                  w[e][:, k, half * 512:half * 512 + 512],
                                                  q == 0 and k == 0, q == 3 and k == 1)
                            unit_done()
                            unit_done()
                        last.then_inc(big_filled, 1)

                    k_use = me.next_big()
                    pe.wait_ge(big_free[k_use % 2], me.over(k_use - 2))
                    both_experts(BIG[k_use % 2], XS)
                    pe.wait_ge(gates_ready, me.next("gates_ready"))
                    m_gate = me.next_pt()
                    pe.wait_ge(pt_free, me.pt_over(m_gate - 1))
                    for t in range(TT):
                        ins = pe.transpose(PT[:, t * P:t * P + P],
                                           GONEH[:, t, :, :].rearrange("p a b -> p (a b)"), const("ident"))
                        if t == 0:
                            ins.then_inc(unit_used, unit["open"])
                            unit["open"] = 0
                    ins.then_inc(pt_filled, 1)
                    k_hidden = me.next_big()
                    pe.wait_ge(big_free[k_hidden % 2], me.over(k_hidden - 2))
                    both_experts(BIG[k_hidden % 2], XS)
                    k_next = gather()
                    pe.wait_ge(big_free[k_hidden % 2], me.over(k_hidden))
                    m_hid = me.next_pt()
                    pe.wait_ge(pt_free, me.pt_over(m_hid - 1))
                    for f in range(KT):
                        ins = pe.transpose(PT[:, f * P:f * P + P], HX[:, f * P:f * P + P], const("ident"))
                    ins.then_inc(pt_filled, 1)
                    pe.wait_ge(big_free[k_next % 2], me.over(k_next))
                    pe.wait_ge(pt_free, me.pt_over(m_hid))
                    k_use = me.next_big()
                    pe.wait_ge(big_free[k_use % 2], me.over(k_use - 2))
                    both_experts(BIG[k_use % 2], HXT)
                    pe.wait_ge(big_free[k_use % 2], me.over(k_use))
                    for m2 in range(4):
                        k_use = me.next_big()
                        if k_use >= 2:
                            pe.wait_ge(big_free[k_use % 2], me.over(k_use - 2))
                        for half in range(2):
                            m = 2 * m2 + half
                            last = pe.matmul(BIG[k_use % 2][:, half * N:half * N + N], YK[:, m * P:m * P + P],
                                             GSCAT[:, :], start=True, stop=True)
                            if m == 0:
                                last.then_inc(unit_used, unit["open"])
                                unit["open"] = 0
                        last.then_inc(big_filled, 1)
                    me.leave(MOE_PAIRS)
                unit["n"] += MOE_UNITS * (MOE_PAIRS - 1)

            y_before = [0, len(PAIRS) * NA // P]
            pe.wait_ge(consts_loaded, 32)
            pe.wait_ge(cvec_ready, me.next("cvec_ready", 2))
            for _ in range(MOD_STEPS[0]):
                mod_rows(0)
                mod_cols(0)
            for layer in range(DEPTH):
                norm_sums(NA)
                attention(layer)
            norm_sums(N)
            norm_sums(NA)
            even_layer()
            norm_sums(N)
            experts(0)
            norm_sums(N)
            conformer()
            norm_sums(N)
            experts(1)
            norm_sums(N)

        @block.scalar
        def _(act):
            me = Count()

            def norm(n, updates, shift):
                for k in range(KT):
                    if updates:
                        act.wait_ge(big_free[updates[k] % 2], me.over(updates[k]))
                    act.activation(HT[:, k, 0:n], XC[:, k, 0:n], ACT.Square).then_inc(squares, 1)
                k_use = me.next_big()
                act.wait_ge(big_filled, me.fills(k_use))
                act.activation(RS[:, 0:n], BIG[k_use % 2][:, 0:n], ACT.Ln, bias=EPSC[:, 0:1], scale=1.0 / D)\
                    .then_inc(big_free[k_use % 2], 1)
                act.wait_ge(big_free[k_use % 2], me.over(k_use))
                act.activation(RS[:, 0:n], RS[:, 0:n], ACT.Exp, scale=-0.5).then_inc(rs_ready, 1)
                if shift is None:
                    return
                for k in range(KT):
                    act.wait_ge(h_scaled, me.next("h_scaled"))
                    ins = act.activation(HT[:, k, 0:N], HT[:, k, 0:N], ACT.Identity, bias=shift(k, 0))
                    if n > N:
                        ins = act.activation(HT[:, k, N:n], HT[:, k, N:n], ACT.Identity, bias=shift(k, 1))
                    ins.then_inc(h_ready, 1)

            def attention(layer):
                steps, order = schedule(layer)
                nq = NA if layer == 0 else N
                kv = -1
                score_use = {}
                for what, x in order:
                    if what == "mod_rows":
                        mod_rows()
                    elif what in ("k", "q"):
                        if what == "k":
                            kv += 1
                        kind = PAIRS[x][0]
                        n = NA if what == "k" else nq
                        k_use = me.next_big()
                        act.wait_ge(big_filled, me.fills(k_use))
                        dst = K[:, kv % 2, 0:n] if what == "k" else Q[:, x % 2, 0:n]
                        scale = HD ** -0.5 if what == "q" and kind != "A" else 1.0
                        act.activation(dst, BIG[k_use % 2][:, 0:n], ACT.Copy, scale=scale)\
                            .then_inc(big_free[k_use % 2], 1)
                        raw = (k_use, dst, n)
                        raws[what, x] = raw
                        if kind == "A" and (what == "q" and PAIRS[x][1] or what == "k"):
                            square(raw)
                    elif what == "v":
                        me.big += 1
                    elif what == "g":
                        k_use = me.next_big()
                        act.wait_ge(big_filled, me.fills(k_use))
                        act.activation(GATE_T[:, 0:nq], BIG[k_use % 2][:, 0:nq], ACT.Tanh, scale=0.5)\
                            .then_inc(gate_tanh, 1)
                    elif what.startswith("norm_"):
                        n = NA if what == "norm_k" else nq
                        k_use = me.next_big()
                        act.wait_ge(big_filled, me.fills(k_use))
                        scale, bias = (1.0 / HD, 0) if what == "norm_k" else (1.0, 1)
                        act.activation(SQT[:, 0:n], BIG[k_use % 2][:, 0:n], ACT.Ln, bias=EPSC[:, bias:bias + 1],
                                       scale=scale).then_inc(big_free[k_use % 2], 1)
                        act.wait_ge(big_free[k_use % 2], me.over(k_use))
                        act.activation(SQT[:, 0:n], SQT[:, 0:n], ACT.Exp, scale=-0.5).then_inc(qk_rs, 1)
                        if what == "norm_k":
                            act.wait_ge(qk_normed, me.next("qk_normed"))
                            square(raws["q", x])
                        else:
                            me.seen["qk_normed"] = me.seen.get("qk_normed", 0) + 1
                    elif what.startswith("rope_"):
                        me.big += 1
                    elif what == "S":
                        k_use = me.big
                        me.big += 1
                        score_use[x] = k_use
                    elif what == "E":
                        i, h, t = steps[x]
                        a, b = score_span(PAIRS[i][0], t)
                        k_use = score_use[x]
                        act.wait_ge(max_ready, me.next("max_ready"))
                        act.activation(PROB[:, x % 2, 0:b - a], BIG[k_use % 2][:, a:b], ACT.Exp,
                                       bias=STAT[:, x % 4:x % 4 + 1],
                                       accum_out=STAT[:, 4 + x % 4:5 + x % 4]).then_inc(big_free[k_use % 2], 1)
                    elif what == "T":
                        i, h, t = steps[x]
                        w = len(key_tiles(PAIRS[i][0], t)) * P
                        m_pt = me.next_pt()
                        act.wait_ge(pt_filled, me.pt_fills(m_pt))
                        act.activation(PTS[:, x % 2, 0:w], PT[:, 0:w], ACT.Copy).then_inc(pt_free, 1)
                uses = list(range(me.big, me.big + KT))
                me.big += KT
                act.wait_ge(mods_filled, me.next("mods_filled"))
                return uses

            raws = {}

            def mod_rows():
                k_use = me.next_big()
                act.wait_ge(big_filled, me.fills(k_use))
                if mod_waits[0]:
                    act.wait_ge(mods_filled, me.next("mods_filled"))
                mod_waits[0] = True
                act.activation(RS[:, :], BIG[k_use % 2][:, 0:NA], ACT.Copy).then_inc(big_free[k_use % 2], 1)

            mod_waits = [False]

            def square(raw):
                k_use, dst, n = raw
                act.wait_ge(big_free[k_use % 2], me.over(k_use))
                act.activation(SQT[:, 0:n], dst, ACT.Square).then_inc(qk_squared, 1)

            def even_layer():
                act.wait_ge(pads_ready, me.next("pads_ready"))
                for t in range(4):
                    k_use = me.next_big()
                    act.wait_ge(big_filled, me.fills(k_use))
                    act.activation(XAR[:, t, 1:1 + N], BIG[k_use % 2][:, 0:N], ACT.Copy)
                    act.activation(CXR[:, t, 1:1 + NC], BIG[k_use % 2][:, N:NA], ACT.Copy)\
                        .then_inc(big_free[k_use % 2], 1)
                for t in range(4):
                    k_use = me.next_big()
                    act.wait_ge(big_filled, me.fills(k_use))
                    act.activation(GATE[:, t, :], BIG[k_use % 2][:, 0:N], ACT.Gelu_apprx_tanh)\
                        .then_inc(big_free[k_use % 2], 1)
                for t in range(12):
                    if t >= 2:
                        act.wait_ge(hy_ready, t - 1)
                    k_use = me.next_big()
                    act.wait_ge(big_filled, me.fills(k_use))
                    act.activation(HYR[:, t % 2, 1:1 + N], BIG[k_use % 2][:, 0:N], ACT.Copy)\
                        .then_inc(big_free[k_use % 2], 1)
                act.wait_ge(hy_ready, 12)
                act.activation(SPT[:, 0, :], vec("lru_lam", 0, 8), ACT.Abs).then_inc(act_chain, 1)
                act.wait_ge(act_chain, me.next("act_chain"))
                act.activation(SPT[:, 1, :], SPT[:, 0, :], ACT.Exp, scale=-1.0).then_inc(lam_exp, 1)
                first = me.big
                for t in range(4):
                    for d in range(2):
                        for g, (dst, name) in enumerate(((LR, "lru_br"), (IX, "lru_bi"))):
                            k_use = me.next_big()
                            act.wait_ge(big_filled, me.fills(k_use))
                            act.activation(dst[:, d * 4 + t, :], BIG[k_use % 2][:, 0:NA], ACT.Sigmoid,
                                           bias=vec(name, d * 4 + t)).then_inc(big_free[k_use % 2], 1)
                act.wait_ge(decay_ready, me.next("decay_ready"))
                act.wait_ge(big_free[(me.big - 2) % 2], me.over(me.big - 2))
                for t in range(4):
                    for d in range(2):
                        n = 2 * t + d
                        s = d * 4 + t
                        if n >= 2:
                            act.wait_ge(lru_scanned, n - 1)
                        act.activation(LA[:, n % 2, :], LR[:, s, :], ACT.Exp, scale=SPT[:, 7, s:s + 1])
                        act.activation(LR[:, s, :], LR[:, s, :], ACT.Tanh, scale=SPT[:, 6, s:s + 1])\
                            .then_inc(lru_a, 1)
                        act.wait_ge(lru_v, me.next("lru_v"))
                        act.activation(LR[:, s, :], LR[:, s, :], ACT.Sqrt).then_inc(lru_sqrt, 1)
                for layer_hidden, (dst) in enumerate((HID1, HID2)):
                    me.big += 1
                    act.wait_ge(sin_arg, me.next("sin_arg"))
                    act.activation(dst[0:64, :], HARG[0:64, :], ACT.Sin).then_inc(sin_ready, 1)
                for o in range(2):
                    me.big += TT
                    for f in range(4):
                        k_use = me.next_big()
                        act.wait_ge(big_filled, me.fills(k_use))
                        for part in range(2):
                            ins = act.activation(KF[:, part * 4 + f, :], BIG[k_use % 2][:, part * N:part * N + N],
                                                 ACT.Copy, scale=vec("kscale", f))
                        ins.then_inc(big_free[k_use % 2], 1)
                    for half in range(2):
                        k_use = me.next_big()
                        act.wait_ge(big_filled, me.fills(k_use))
                        act.activation(UT[:, 2 * half:2 * half + 2, :],
                                       BIG[k_use % 2][:, :].rearrange("p (a b) -> p a b", b=N), ACT.Copy)\
                            .then_inc(big_free[k_use % 2], 1)
                    me.big += 8
                uses = list(range(me.big, me.big + KT))
                me.big += KT
                return uses

            def conformer():
                for j in range(KT):
                    k_use = me.next_big()
                    act.wait_ge(big_filled, me.fills(k_use))
                    act.activation(CSIG[:, j % 2, :], BIG[k_use % 2][:, N:1024], ACT.Sigmoid,
                                   bias=vec("cf_b1", KT + j)).then_inc(glu_sig, 1)
                first = me.big - KT
                for j in range(KT):
                    act.wait_ge(big_free[(first + j) % 2], me.over(first + j))
                    act.activation(CY[:, j, :], CU[:, j, :], ACT.Identity, bias=vec("cf_dw_b", j),
                                   scale=vec("cf_dw_w", TAPS * KT + j)).then_inc(dw_base, 1)
                mean_use = me.big
                me.big += 1
                for k in range(KT):
                    if k < KT - 1:
                        act.wait_ge(centred, me.next("centred"))
                    else:
                        act.wait_ge(big_free[mean_use % 2], me.over(mean_use))
                    act.activation(HT[:, k, 0:N], CY[:, k, :], ACT.Square).then_inc(squares, 1)
                k_use = me.next_big()
                act.wait_ge(big_filled, me.fills(k_use))
                act.activation(RS[:, 0:N], BIG[k_use % 2][:, 0:N], ACT.Ln, bias=EPSC[:, 0:1], scale=1.0 / D)\
                    .then_inc(big_free[k_use % 2], 1)
                act.wait_ge(big_free[k_use % 2], me.over(k_use))
                act.activation(RS[:, 0:N], RS[:, 0:N], ACT.Exp, scale=-0.5).then_inc(rs_ready, 1)
                for k in range(KT):
                    act.wait_ge(ln_scaled, me.next("ln_scaled"))
                    act.activation(CU[:, k, :], CY[:, k, :], ACT.Silu, bias=vec("cf_ln_b", k)).then_inc(h_ready, 1)
                uses = list(range(me.big, me.big + KT))
                for k in range(KT):
                    if k >= 2:
                        act.wait_ge(big_free[uses[k - 2] % 2], me.over(uses[k - 2]))
                    k_use = me.next_big()
                    act.wait_ge(big_filled, me.fills(k_use))
                    act.activation(CFT[:, k % 2, :], BIG[k_use % 2][:, 0:N], ACT.Identity,
                                   bias=vec("cf_b2", k)).then_inc(cf_add, 1)
                return uses

            def experts(layer):
                for t in range(TT):
                    k_use = me.next_big()
                    act.wait_ge(big_filled, me.fills(k_use))
                    act.activation(HTOK[:, t, :], BIG[k_use % 2][:, :], ACT.Copy).then_inc(big_free[k_use % 2], 1)
                act.wait_ge(pt_free, me.pt_over(me.pt))
                act.activation(PROBS, PROBS, ACT.Exp).then_inc(logits_exp, 1)
                me.pt += 3

                def gathered():
                    k_use = me.next_big()
                    act.wait_ge(big_filled, me.fills(k_use))
                    act.activation(XS.rearrange("p a b -> p (a b)"), BIG[k_use % 2][:, :], ACT.Copy)\
                        .then_inc(big_free[k_use % 2], 1)

                gathered()
                with act.Fori(0, MOE_PAIRS) as i:
                    me.enter(i, PER_PAIR)
                    me.pt += 1
                    k_use = me.next_big()
                    act.wait_ge(big_filled, me.fills(k_use))
                    act.activation(SIL, BIG[k_use % 2][:, :], ACT.Silu).then_inc(big_free[k_use % 2], 1)
                    me.big += 1
                    gathered()
                    m_hid = me.next_pt()
                    act.wait_ge(pt_filled, me.pt_fills(m_hid))
                    act.activation(HXT.rearrange("p a b -> p (a b)"), PT[:, :], ACT.Copy).then_inc(pt_free, 1)
                    k_use = me.next_big()
                    act.wait_ge(big_filled, me.fills(k_use))
                    act.activation(YK, BIG[k_use % 2][:, :], ACT.Copy).then_inc(big_free[k_use % 2], 1)
                    me.big += 4
                    me.leave(MOE_PAIRS)
                return [me.big - 4 + k // 2 for k in range(KT)]

            act.wait_ge(consts_loaded, 32)
            act.activation(CCS[:, 0:32], vec("cvec", 0, 32), ACT.Silu).then_inc(cvec_ready, 1)
            act.wait_ge(x_loaded, 16)
            act.wait_ge(eps_ready, 1)
            for _ in range(MOD_STEPS[0]):
                mod_rows()
            updates = None
            act.wait_ge(mods_filled, me.next("mods_filled"))
            for layer in range(DEPTH):
                mod_waits[0] = False
                norm(NA, updates, lambda k, c: mod(layer, 0, k, c))
                updates = attention(layer)
            norm(N, updates, None)
            act.wait_ge(ctx2_loaded, 16)
            act.wait_ge(block_done, 1)
            norm(NA, None, lambda k, c: mod(2, 0, k, c))
            updates = even_layer()
            norm(N, updates, lambda k, c: mod(2, 3, k, c))
            updates = experts(0)
            norm(N, updates, lambda k, c: mod(3, 0, k, c))
            updates = conformer()
            norm(N, updates, lambda k, c: mod(3, 3, k, c))
            updates = experts(1)
            norm(N, updates, None)

        @block.vector
        def _(dve):
            me = Count()

            def link(ins):
                ins.then_inc(dve_chain, 1)
                dve.wait_ge(dve_chain, me.next("dve_chain"))

            def modulation(group):
                dve.wait_ge(mods_filled, me.next("mods_filled", MOD_STEPS[group]))
                a, n = MOD_AT[group], 2 * MOD_TILES[group]
                link(dve.tensor_tensor(MOD[:, a:a + n], MODP[:, a:a + n], vec("mod_b", a, n), ALU.add))

            def norm(n, weight, group, scale_chunk, dst, done):
                if group is not None:
                    for c in range(2 if n > N else 1):
                        link(dve.scalar_tensor_tensor(COEF[:, c * KT:c * KT + KT], mod_row(group, scale_chunk, c),
                                                      1.0, weight, ALU.add, ALU.mult))
                me.big += 1
                dve.wait_ge(rs_ready, me.next("rs_ready"))
                for k in range(KT):
                    for c in range(2 if n > N else 1):
                        a, b = (0, N) if c == 0 else (N, NA)
                        factor = COEF[:, c * KT + k:c * KT + k + 1] if group is not None else weight[:, k:k + 1]
                        ins = dve.scalar_tensor_tensor(dst[:, k, a:b], XC[:, k, a:b], factor, RS[:, a:b],
                                                       ALU.mult, ALU.mult)
                    if done is not None:
                        ins.then_inc(done, 1)
                return ins

            def add_gated(n, gates):
                for m in range(KT):
                    k_use = me.next_big()
                    dve.wait_ge(big_filled, me.fills(k_use))
                    for c in range(2 if n > N else 1):
                        a, b = (0, N) if c == 0 else (N, NA)
                        ins = dve.scalar_tensor_tensor(XC[:, m, a:b], BIG[k_use % 2][:, a:b], gates(m, c),
                                                       XC[:, m, a:b], ALU.mult, ALU.add)
                    ins.then_inc(big_free[k_use % 2], 1)

            def attention(layer):
                steps, order = schedule(layer)
                nq = NA if layer == 0 else N
                kv = -1
                score_use = {}
                for what, x in order:
                    if what == "mod_rows":
                        me.big += 1
                    elif what == "k":
                        kv += 1
                        me.big += 1
                    elif what == "q":
                        me.big += 1
                    elif what == "v":
                        k_use = me.next_big()
                        dve.wait_ge(big_filled, me.fills(k_use))
                        dve.tensor_copy(V[:, kv % 2, :, :].rearrange("p a b -> p (a b)"),
                                        BIG[k_use % 2][:, 0:NA]).then_inc(big_free[k_use % 2], 1)
                    elif what == "g":
                        k_use = me.next_big()
                        dve.wait_ge(big_filled, me.fills(k_use))
                        dve.wait_ge(gate_tanh, me.next("gate_tanh"))
                        dve.scalar_tensor_tensor(SG[:, x % 2, 0:nq], GATE_T[:, 0:nq], 1.0,
                                                 BIG[k_use % 2][:, 0:nq], ALU.add, ALU.mult)\
                            .then_inc(big_free[k_use % 2], 1)
                    elif what.startswith("norm_"):
                        me.big += 1
                        dve.wait_ge(qk_rs, me.next("qk_rs"))
                        dst, n, w = (K[:, kv % 2, :], NA, "kn") if what == "norm_k" else (Q[:, x % 2, :], nq, "qn")
                        dve.scalar_tensor_tensor(dst[:, 0:n], dst[:, 0:n], vec(w, layer), SQT[:, 0:n],
                                                 ALU.mult, ALU.mult).then_inc(qk_normed, 1)
                        dve.wait_ge(qk_normed, me.next("qk_normed"))
                    elif what.startswith("rope_"):
                        dst = K[:, kv % 2, 0:N] if what == "rope_k" else Q[:, x % 2, 0:N]
                        k_use = me.next_big()
                        dve.wait_ge(big_filled, me.fills(k_use))
                        dve.tensor_tensor(ROPE_T, BIG[k_use % 2][:, 0:N], const("sin"), ALU.mult)\
                            .then_inc(big_free[k_use % 2], 1)
                        link(dve.tensor_tensor(dst, dst, const("cos"), ALU.mult))
                        dve.wait_ge(big_free[k_use % 2], me.over(k_use))
                        dve.tensor_tensor(dst, dst, ROPE_T, ALU.add).then_inc(qk_roped, 1)
                    elif what == "S":
                        i, h, t = steps[x]
                        kind, j = PAIRS[i]
                        k_use = score_use[x] = me.next_big()
                        dve.wait_ge(big_filled, me.fills(k_use))
                        out = BIG[k_use % 2]
                        if kind == "B" and t < TT:
                            head = 8 * layer + 2 * j + h
                            if t == 0:
                                dve.wait_ge(bias_loaded[head % BIAS_SLOTS], 16 * (head // BIAS_SLOTS + 1))
                            a = (7 - 2 * t) * HD
                            ins = dve.tensor_tensor(out[:, 0:N], out[:, 0:N], BIAS[:, head % BIAS_SLOTS, a:a + N], ALU.add)
                            if t == TT - 1:
                                ins.then_inc(bias_used, 1)
                                dve.wait_ge(bias_used, me.next("bias_used"))
                            else:
                                link(ins)
                        if kind == "C":
                            a, b = score_span(kind, t)
                            if t < TT:
                                if t > 0:
                                    link(dve.tensor_tensor(out[:, a:a + P], out[:, a:a + P], const("mprev"), ALU.add))
                                if t < TT - 1:
                                    link(dve.tensor_tensor(out[:, N - P:N], out[:, N - P:N], const("mnext"), ALU.add))
                            head = j + 4 * h
                            link(dve.tensor_copy(out[:, NA:NA + 1], vec("sink", 8 * layer + head)))
                        a, b = score_span(kind, t)
                        dve.tensor_reduce(STAT[:, x % 4:x % 4 + 1], out[:, a:b], AX.X, ALU.max, negate=True)\
                            .then_inc(max_ready, 1)
                    elif what == "T":
                        me.pt += 1
                        if x % 2:
                            dve.wait_ge(big_free[score_use[x] % 2], me.over(score_use[x]))
                            dve.wait_ge(big_free[score_use[x - 1] % 2], me.over(score_use[x - 1]))
                            c = x % 4 - 1
                            link(dve.reciprocal(STAT[:, 8 + c:10 + c], STAT[:, 4 + c:6 + c]))
                            dve.tensor_copy(RB, STAT[:, 8 + c:10 + c].unsqueeze(2).to_broadcast([P, 2, HD]))\
                                .then_inc(sums_inverted, 1)
                    elif what == "O":
                        i, h, t = steps[x]
                        dve.wait_ge(o_filled, me.next("o_filled"))
                        y = U[:, i, t * P:t * P + P]
                        link(dve.scalar_tensor_tensor(y, OP[:, 0:P], 0.5, SG[:, i % 2, t * P:t * P + P],
                                                      ALU.mult, ALU.mult))
                        dve.tensor_tensor(y, y, OP[:, P:2 * P], ALU.mult).then_inc(y_ready, 1)
                        dve.wait_ge(y_ready, me.next("y_ready"))
                add_gated(nq, lambda m, c: mod(layer, 2, m, c))

            def convolve(dst, raw, n, taps, weight, bias):
                link(dve.tensor_scalar(dst, raw[:, 0:n], weight(0), bias, ALU.mult, ALU.add))
                for j in range(1, taps):
                    ins = dve.scalar_tensor_tensor(dst, raw[:, j:j + n], weight(j), dst, ALU.mult, ALU.add)
                    if j < taps - 1:
                        link(ins)
                return ins

            def even_layer():
                for t in range(4):
                    k_use = me.next_big()
                    dve.wait_ge(big_filled, me.fills(k_use))
                    dve.wait_ge(big_free[(me.big - 1) % 2], me.over(me.big - 1))
                    link(convolve(XAC[:, t, :], XAR[:, t, :], N, 4, lambda j: vec("conv_a_w", j * 4 + t),
                                  vec("conv_a_b", t)))
                    convolve(CXC[:, t, :], CXR[:, t, :], NC, 4, lambda j: vec("conv_a_w", j * 4 + t),
                             vec("conv_a_b", t)).then_inc(xa_ready, 1)
                me.big += 4
                for t in range(12):
                    k_use = me.big
                    me.big += 1
                    dve.wait_ge(big_free[k_use % 2], me.over(k_use))
                    convolve(HY[:, t, :], HYR[:, t % 2, :], N, 3, lambda j: vec("conv_b_w", j * 12 + t),
                             vec("conv_b_b", t)).then_inc(hy_ready, 1)
                dve.wait_ge(lam_exp, me.next("lam_exp"))
                e, s, s2, q = (SPT[:, x, :] for x in (1, 2, 3, 4))
                link(dve.tensor_scalar(q, e, 2.0, None, ALU.add))
                link(dve.reciprocal(s, q))
                link(dve.tensor_tensor(s, s, e, ALU.mult))
                link(dve.tensor_tensor(s2, s, s, ALU.mult))
                link(dve.tensor_scalar(q, s2, 1.0 / 15, None, ALU.mult))
                for odd in (13, 11, 9, 7, 5, 3):
                    link(dve.scalar_tensor_tensor(q, q, 1.0 / odd, s2, ALU.add, ALU.mult))
                link(dve.scalar_tensor_tensor(q, q, 1.0, s, ALU.add, ALU.mult))
                link(dve.tensor_scalar(s2, vec("lru_lam", 0, 8), -1.0, 0.0, ALU.mult, ALU.max))
                link(dve.scalar_tensor_tensor(q, q, 2.0, s2, ALU.mult, ALU.add))
                link(dve.tensor_scalar(SPT[:, 6, :], q, 8.0, None, ALU.mult))
                dve.tensor_scalar(SPT[:, 7, :], q, -8.0, None, ALU.mult).then_inc(decay_ready, 1)
                for t in range(4):
                    for d in range(2):
                        me.big += 2
                        s = d * 4 + t
                        dve.wait_ge(big_free[(me.big - 1) % 2], me.over(me.big - 1))
                        dve.tensor_tensor(IX[:, s, 0:N], IX[:, s, 0:N], XAC[:, t, :], ALU.mult)
                        link(dve.tensor_tensor(IX[:, s, N:NA], IX[:, s, N:NA], CXC[:, t, :], ALU.mult))
                for t in range(4):
                    for d in range(2):
                        n = 2 * t + d
                        s = d * 4 + t
                        a = LA[:, n % 2, :]
                        dve.wait_ge(lru_a, me.next("lru_a"))
                        link(dve.tensor_tensor(LT, a, a, ALU.mult))
                        dve.scalar_tensor_tensor(LR[:, s, :], LT, 1.0, LR[:, s, :], ALU.add, ALU.mult)\
                            .then_inc(lru_v, 1)
                        dve.wait_ge(lru_sqrt, me.next("lru_sqrt"))
                        link(dve.tensor_tensor(LT, LR[:, s, :], IX[:, s, :], ALU.mult))
                        h = LH[:, d, :]
                        if d == 0:
                            link(dve.tensor_tensor_scan(h[:, N:NA], a[:, N:NA], LT[:, N:NA], 0.0, ALU.mult, ALU.add))
                            ins = dve.tensor_tensor_scan(h[:, 0:N], a[:, 0:N], LT[:, 0:N], h[:, NA - 1:NA],
                                                         ALU.mult, ALU.add)
                        else:
                            link(dve.tensor_tensor_scan(h[:, NA - 1:N - 1:-1], a[:, NA - 1:N - 1:-1],
                                                        LT[:, NA - 1:N - 1:-1], 0.0, ALU.mult, ALU.add))
                            ins = dve.tensor_tensor_scan(h[:, N - 1::-1], a[:, N - 1::-1], LT[:, N - 1::-1],
                                                         h[:, N:N + 1], ALU.mult, ALU.add)
                        ins.then_inc(lru_scanned, 1)
                        dve.wait_ge(lru_scanned, me.next("lru_scanned"))
                    link(dve.tensor_tensor(LT[:, 0:N], LH[:, 0, 0:N], LH[:, 1, 0:N], ALU.add))
                    dve.tensor_tensor(YA[:, t, :], LT[:, 0:N], GATE[:, t, :], ALU.mult).then_inc(lru_done, 1)
                    dve.wait_ge(lru_done, me.next("lru_done"))
                magic = 1.5 * 2.0 ** 23
                two_pi = 2 * np.pi
                two_pi_hi = float(np.float32(6.28125))
                dve.wait_ge(hyena_loaded, 96)
                link(dve.memset(HID2[64:65, :], 1.0))
                for x in range(2):
                    k_use = me.next_big()
                    dve.wait_ge(big_filled, me.fills(k_use))
                    arg, rnd = HARG[0:64, :], HRND[0:64, :]
                    dve.tensor_scalar(arg, BIG[k_use % 2][0:64, 0:N], vec(f"filt_b{x + 1}", 0)[0:64],
                                      vec(f"filt_f{x}", 0)[0:64], ALU.add, ALU.mult)\
                        .then_inc(big_free[k_use % 2], 1)
                    dve.wait_ge(big_free[k_use % 2], me.over(k_use))
                    link(dve.tensor_scalar(rnd, arg, 1.0 / two_pi, magic, ALU.mult, ALU.add))
                    link(dve.tensor_scalar(rnd, rnd, -magic, None, ALU.add))
                    link(dve.scalar_tensor_tensor(arg, rnd, -two_pi_hi, arg, ALU.mult, ALU.add))
                    link(dve.scalar_tensor_tensor(arg, rnd, -(two_pi - two_pi_hi), arg, ALU.mult, ALU.add))
                    pi32 = 3.1415925
                    dve.tensor_scalar(arg, arg, -pi32, pi32, ALU.max, ALU.min).then_inc(sin_arg, 1)
                dve.wait_ge(sin_ready, 2)
                for o in range(2):
                    for t in range(TT):
                        k_use = me.next_big()
                        dve.wait_ge(big_filled, me.fills(k_use))
                        out = BIG[k_use % 2]
                        fwd, bwd = FS[:, t, :], KF[:, t, :]
                        link(dve.tensor_tensor(fwd, out[:, 0:N], WIN[:, t, :], ALU.mult))
                        dve.tensor_tensor(bwd, out[:, N:1024], WIN[:, t, :], ALU.mult)\
                            .then_inc(big_free[k_use % 2], 1)
                        dve.wait_ge(big_free[k_use % 2], me.over(k_use))
                        if t == 0:
                            link(dve.memset(bwd[0:1, :], 0.0))
                        link(dve.tensor_tensor(FD[:, t, :], fwd, bwd, ALU.subtract))
                        dve.tensor_tensor(fwd, fwd, bwd, ALU.add).then_inc(filt_ready, 1)
                    me.big += 4
                    spec_last = me.big - 1
                    me.big += 2
                    dve.wait_ge(big_free[spec_last % 2], me.over(spec_last))
                    dve.wait_ge(big_free[(spec_last - 1) % 2], me.over(spec_last - 1))
                    for f in range(4):
                        k_use = me.next_big()
                        dve.wait_ge(big_filled, me.fills(k_use))
                        ur, us = BIG[k_use % 2][:, 0:N], BIG[k_use % 2][:, N:1024]
                        kr, ks = KF[:, f, :], KF[:, 4 + f, :]
                        zr, zs = ZF[:, f, :], ZF[:, 4 + f, :]
                        t0, t1 = FD[:, 0, :], FD[:, 1, :]
                        dve.tensor_tensor(zr, ur, kr, ALU.mult)
                        dve.tensor_tensor(t0, us, ks, ALU.mult)
                        dve.tensor_tensor(zs, ur, ks, ALU.mult)
                        dve.tensor_tensor(t1, us, kr, ALU.mult).then_inc(big_free[k_use % 2], 1)
                        dve.wait_ge(big_free[k_use % 2], me.over(k_use))
                        if f == 0:
                            link(dve.tensor_copy(zs[0:1, :], t0[0:1, :]))
                            link(dve.memset(t0[0:1, :], 0.0))
                            link(dve.memset(t1[0:1, :], 0.0))
                        link(dve.tensor_tensor(zr, zr, t0, ALU.subtract))
                        dve.tensor_tensor(zs, zs, t1, ALU.add).then_inc(spec_ready, 1)
                        dve.wait_ge(spec_ready, me.next("spec_ready"))
                    for c in range(4):
                        k_use = me.next_big()
                        dve.wait_ge(big_filled, me.fills(k_use))
                        u = HY[:, c, :]
                        link(dve.scalar_tensor_tensor(u, u, vec("filt_bias", o * 4 + c), BIG[k_use % 2][:, 0:N],
                                                      ALU.mult, ALU.add))
                        dve.tensor_tensor(u, u, HY[:, 4 * (o + 1) + c, :], ALU.mult)\
                            .then_inc(big_free[k_use % 2], 1)
                add_gated(N, lambda m, c: mod(2, 2, m, c))

            def conformer():
                for j in range(KT):
                    k_use = me.next_big()
                    dve.wait_ge(big_filled, me.fills(k_use))
                    dve.wait_ge(glu_sig, me.next("glu_sig"))
                    dve.scalar_tensor_tensor(CU[:, j, :], BIG[k_use % 2][:, 0:N], vec("cf_b1", j),
                                             CSIG[:, j % 2, :], ALU.add, ALU.mult).then_inc(big_free[k_use % 2], 1)
                for j in range(KT):
                    dve.wait_ge(dw_base, me.next("dw_base"))
                    shifts = [s for s in range(-TAPS, TAPS + 1) if s]
                    for s in shifts:
                        lo, hi = max(0, -s) * GRID_W, (ROWS - max(0, s)) * GRID_W
                        ins = dve.scalar_tensor_tensor(CY[:, j, lo:hi], CU[:, j, lo + s * GRID_W:hi + s * GRID_W],
                                                       vec("cf_dw_w", (s + TAPS) * KT + j), CY[:, j, lo:hi],
                                                       ALU.mult, ALU.add)
                        if s == shifts[-1]:
                            ins.then_inc(dw_ready, 1)
                            dve.wait_ge(dw_ready, me.next("dw_ready"))
                        else:
                            link(ins)
                k_use = me.next_big()
                dve.wait_ge(big_filled, me.fills(k_use))
                for k in range(KT):
                    ins = dve.scalar_tensor_tensor(CY[:, k, :], BIG[k_use % 2][:, 0:N], -1.0 / D, CY[:, k, :],
                                                   ALU.mult, ALU.add)
                    ins.then_inc(centred if k < KT - 1 else big_free[k_use % 2], 1)
                dve.wait_ge(big_free[k_use % 2], me.over(k_use))
                me.big += 1
                dve.wait_ge(rs_ready, me.next("rs_ready"))
                for k in range(KT):
                    dve.scalar_tensor_tensor(CY[:, k, :], CY[:, k, :], vec("cf_ln_g", k), RS[:, 0:N],
                                             ALU.mult, ALU.mult).then_inc(ln_scaled, 1)
                for m in range(KT):
                    k_use = me.big
                    me.big += 1
                    dve.wait_ge(cf_add, me.next("cf_add"))
                    dve.scalar_tensor_tensor(XC[:, m, 0:N], CFT[:, m % 2, :], mod(3, 2, m, 0), XC[:, m, 0:N],
                                             ALU.mult, ALU.add).then_inc(big_free[k_use % 2], 1)

            def experts(layer):
                group = 2 + layer
                me.big += TT
                m_pt = me.next_pt()
                dve.wait_ge(pt_filled, me.pt_fills(m_pt))
                logits = PT[:, 0:64].rearrange("p (t e) -> p t e", e=N_EXPERTS)
                top, total = SMALL[:, 0:4], SMALL[:, 4:8]
                link(dve.tensor_reduce(top, logits, AX.X, ALU.max))
                dve.tensor_tensor(PROBS, logits, top.unsqueeze(2).to_broadcast([P, TT, N_EXPERTS]),
                                  ALU.subtract).then_inc(pt_free, 1)
                dve.wait_ge(logits_exp, me.next("logits_exp"))
                link(dve.tensor_reduce(total, PROBS, AX.X, ALU.add))
                link(dve.reciprocal(total, total))
                dve.tensor_tensor(PROBS, PROBS, total.unsqueeze(2).to_broadcast([P, TT, N_EXPERTS]),
                                  ALU.mult).then_inc(probs_ready, 1)
                m_pt = me.next_pt()
                dve.wait_ge(pt_filled, me.pt_fills(m_pt))
                rows = [ROW0[0:16, :], ROW1[0:16, :]]
                dve.tensor_copy(rows[0], PT[0:16, 0:N]).then_inc(pt_free, 1)
                dve.wait_ge(pt_free, me.pt_over(me.pt - 1))
                for r in range(CAP // 8):
                    link(dve.max(MAX8[0:16, :], rows[r % 2]))
                    link(dve.match_replace(rows[(r + 1) % 2], MAX8[0:16, :], rows[r % 2], -1.0))
                chosen, upto, slot = ROW2[0:16, :], ROW3[0:16, :], ROW1[0:16, :]
                link(dve.tensor_scalar(chosen, rows[0], 0.0, None, ALU.is_lt))
                link(dve.tensor_tensor_scan(upto, chosen, chosen, 0.0, ALU.add, ALU.max))
                link(dve.tensor_tensor(slot, chosen, upto, ALU.mult))
                dve.tensor_scalar(slot, slot, -1.0, None, ALU.add).then_inc(slots_ready, 1)
                m_pt = me.next_pt()
                dve.wait_ge(pt_filled, me.pt_fills(m_pt))
                dve.memset(SLOT[:, :, N_EXPERTS:], -2.0)
                dve.tensor_copy(SLOT[:, :, 0:N_EXPERTS], PT[:, 0:64].rearrange("p (t e) -> p t e", e=N_EXPERTS))\
                   .then_inc(pt_free, 1)
                dve.wait_ge(pt_free, me.pt_over(me.pt - 1))
                lanes = vec("iota", 0, CAP).unsqueeze(1).unsqueeze(1)

                def onehots(first):
                    slots = SLOT[:, :, first].unsqueeze(3).to_broadcast([P, TT, 2, CAP])
                    dve.tensor_tensor(ONEH, lanes.to_broadcast([P, TT, 2, CAP]), slots, ALU.is_equal)\
                        .then_inc(onehot_ready, 1)
                    dve.wait_ge(onehot_ready, me.next("onehot_ready"))

                onehots(slice(0, 2))
                me.big += 1
                with dve.Fori(0, MOE_PAIRS) as i:
                    me.enter(i, dict(PER_PAIR, onehot_ready=1))
                    gate = PROBS[:, :, bass.ds(i * 2, 2)].unsqueeze(3).to_broadcast([P, TT, 2, CAP])
                    dve.tensor_tensor(GONEH, ONEH, gate, ALU.mult).then_inc(gates_ready, 1)
                    m_pt = me.next_pt()
                    dve.wait_ge(pt_filled, me.pt_fills(m_pt))
                    dve.tensor_copy(GSCAT, PT[:, 0:N]).then_inc(pt_free, 1)
                    onehots(bass.ds(i * 2 + 2, 2))
                    k_silu = me.next_big()
                    k_use = me.next_big()
                    dve.wait_ge(big_filled, me.fills(k_use))
                    dve.wait_ge(big_free[k_silu % 2], me.over(k_silu))
                    dve.tensor_tensor(HX, SIL, BIG[k_use % 2][:, :], ALU.mult).then_inc(big_free[k_use % 2], 1)
                    me.big += 1
                    me.pt += 1
                    me.big += 1
                    for m2 in range(4):
                        k_use = me.next_big()
                        dve.wait_ge(big_filled, me.fills(k_use))
                        for half in range(2):
                            m = 2 * m2 + half
                            ins = dve.scalar_tensor_tensor(XC[:, m, 0:N], BIG[k_use % 2][:, half * N:half * N + N],
                                                           mod(group, 5, m, 0), XC[:, m, 0:N], ALU.mult, ALU.add)
                        ins.then_inc(big_free[k_use % 2], 1)
                    me.leave(MOE_PAIRS)

            dve.memset(CCS[:, 32:64], 0.0).then_inc(cvec_ready, 1)
            dve.memset(EPSC[:, 0:1], EPS)
            dve.memset(EPSC[:, 1:2], EPS * HD).then_inc(eps_ready, 1)
            dve.wait_ge(consts_loaded, 32)
            dve.wait_ge(x_loaded, 16)
            me.big += MOD_STEPS[0]
            for layer in range(DEPTH):
                modulation(layer)
                norm(NA, vec("norm_w", 8 * layer, 8), layer, 1, HT, h_scaled)
                attention(layer)
            norm(N, vec("final_norm_w", 0, 8), None, None, XC, None).then_inc(block_done, 1)
            dve.wait_ge(block_done, me.next("block_done"))
            dve.memset(XAR[:, :, 0:1], 0.0)
            dve.memset(XAR[:, :, N + 1:N + 4], 0.0)
            dve.memset(CXR[:, :, 0:1], 0.0)
            dve.memset(CXR[:, :, NC + 1:NC + 4], 0.0)
            dve.memset(HYR[:, :, 0:1], 0.0)
            dve.memset(HYR[:, :, N + 1:N + 4], 0.0).then_inc(pads_ready, 1)
            dve.wait_ge(pads_ready, me.next("pads_ready"))
            dve.wait_ge(ctx2_loaded, 16)
            modulation(2)
            norm(NA, vec("norm1_g", 0, 8), 2, 1, HT, h_scaled)
            even_layer()
            norm(N, vec("norm2_g", 0, 8), 2, 4, HT, h_scaled)
            experts(0)
            modulation(3)
            norm(N, vec("norm1_g", 8, 8), 3, 1, HT, h_scaled)
            conformer()
            norm(N, vec("norm2_g", 8, 8), 3, 4, HT, h_scaled)
            experts(1)
            norm(N, vec("final_g", 0, 8), None, None, HT, out_ready)


def constants():
    c = {}
    packed = np.zeros((P, NK), np.float32)
    packed[:, COFF["ident"]:COFF["ident"] + P] = np.eye(P)
    packed[:, COFF["ones"]:COFF["ones"] + P] = 1
    half = HD // 2
    for b in range(2):
        a = COFF["blk"] + b * HD
        packed[b * HD:(b + 1) * HD, a:a + HD] = 1
        for m in range(half):
            packed[b * HD + m + half, COFF["rot"] + b * HD + m] = -1
            packed[b * HD + m, COFF["rot"] + b * HD + m + half] = 1
    t = np.arange(N)
    freq = (np.float32(10000.0) ** (-np.arange(HD // 4, dtype=np.float32) / np.float32(HD // 4))).astype(np.float32)
    ang = np.concatenate([(t // GRID_W).astype(np.float32)[:, None] * freq,
                          (t % GRID_W).astype(np.float32)[:, None] * freq], axis=1)
    packed[:, COFF["cos"]:COFF["cos"] + N] = np.tile(np.cos(ang).T, (4, 1))
    packed[:, COFF["sin"]:COFF["sin"] + N] = np.tile(np.sin(ang).T, (4, 1))
    q, k = np.arange(P)[:, None], np.arange(P)[None, :]
    packed[:, COFF["mprev"]:COFF["mprev"] + P] = np.where(k >= q, 0, MASKED)
    packed[:, COFF["mnext"]:COFF["mnext"] + P] = np.where(k <= q, 0, MASKED)
    packed[0::32, COFF["sel"]] = 1
    packed[1::32, COFF["sel"] + 1] = 1
    c["consts"] = packed

    def tiled(a):
        return np.ascontiguousarray(a.reshape(a.shape[0] // P, P, -1).transpose(1, 0, 2).astype(np.float32))

    f = np.arange(NF)
    turns = (t[:, None] * f[None, :]) % (2 * N)
    c["dft_cos"] = tiled(np.cos(np.pi * turns / N))
    sines = np.sin(np.pi * turns / N)
    sines[turns % N == 0] = 0
    c["dft_sin"] = tiled(sines)
    alternate = 1.0 - 2.0 * (t % 2)
    nyq = np.zeros((N, P))
    nyq[:, 0] = alternate
    c["dft_nyq"] = tiled(nyq)
    c["dft_alt"] = alternate[None, :].astype(np.float32)
    pos = np.linspace(0.0, 1.0, N, dtype=np.float32)[:, None]
    deltas = np.abs(np.linspace(np.log(1e-2) / 1.5, np.log(1e-2) / 0.3, 512, dtype=np.float32))
    c["window"] = tiled(np.exp(-pos * deltas[None, :]) + np.float32(0.05))
    bands = 16
    w = (np.float32(2.0 * np.pi / N) * np.arange(N, dtype=np.float32))[:, None]
    fb = np.linspace(1e-4, bands - 1, bands, dtype=np.float32)[None, :]
    c["z"] = np.concatenate([pos, np.cos(fb * w), -np.sin(fb * w)], axis=1).astype(np.float32)
    return c


def lay_out(x):
    c = constants()
    f32 = np.float32

    def feature_major(a):
        return np.ascontiguousarray(a.T.reshape(KT, P, -1).transpose(1, 0, 2))

    def cols(v):
        v = np.asarray(v, f32)
        return v.reshape(-1, P).T

    vec = {
        "norm_w": cols(x["norm_w"]), "final_norm_w": cols(x["final_norm_w"]),
        "norm1_g": cols(x["norm1_g_2"]), "norm2_g": cols(x["norm2_g_2"]), "final_g": cols(x["final_g_2"]),
        "qn": np.tile(x["q_norm_a"].T, (2, 1)), "kn": np.tile(x["k_norm_a"].T, (2, 1)),
        "sink": np.broadcast_to(x["sink_c"].reshape(1, 16), (P, 16)),
        "mod_b": np.repeat(np.concatenate([cols(x["ada_b"]), cols(x["b_mod_2"])], axis=1), 2, axis=1),
        "cvec": np.stack([cols(x["c"]), cols(x["c_ctx"]), cols(x["c_2"]), cols(x["c_ctx_2"])], axis=2).reshape(P, 32),
        "conv_a_w": cols(x["conv_a_w_2"]), "conv_a_b": cols(x["conv_a_b_2"]),
        "lru_br": cols(x["lru_br_2"]), "lru_bi": cols(x["lru_bi_2"]), "lru_lam": cols(x["lru_lam_2"]),
        "conv_b_w": cols(x["conv_b_w_2"]), "conv_b_b": cols(x["conv_b_b_2"]),
        "filt_bias": cols(x["filt_bias_2"]), "cf_b1": cols(x["cf_b1_2"]),
        "cf_dw_w": cols(x["cf_dw_w_2"][0, 15 - TAPS:16 + TAPS]),
        "cf_dw_b": cols(x["cf_dw_b_2"]), "cf_ln_g": cols(x["cf_ln_g_2"]), "cf_ln_b": cols(x["cf_ln_b_2"]),
        "cf_b2": cols(x["cf_b2_2"]),
        "iota": np.broadcast_to(np.arange(CAP, dtype=f32)[None, :], (P, CAP)),
    }
    for name, v in (("filt_b1", x["filt_b1_2"]), ("filt_b2", x["filt_b2_2"]),
                    ("filt_f0", x["filt_freq_2"][0, 0]), ("filt_f1", x["filt_freq_2"][0, 1])):
        vec[name] = np.zeros((P, 1), f32)
        vec[name][:64, 0] = v.reshape(-1)
    kscale = np.full((P, 4), 1.0 / N, f32)
    kscale[0, 0] = 0.5 / N
    vec["kscale"] = kscale
    vecs = np.zeros((P, NV), f32)
    for name, n in VECTORS:
        assert vec[name].shape == (P, n), (name, vec[name].shape)
        vecs[:, VOFF[name]:VOFF[name] + n] = vec[name]

    def unit(w):
        out = np.zeros((P, UNIT), f32)
        flat = w.reshape(-1, P, w.shape[1]).transpose(1, 0, 2).reshape(P, -1)
        out[:, :flat.shape[1]] = flat
        return out

    off = dict(zip(["qA", "kA", "vA", "qB", "kB", "vB", "qC", "kC", "vC", "gate"],
                   np.cumsum([0, 512, 128, 128, 512, 512, 512, 512, 128, 128])))

    def pair_cols(i):
        kind, j = PAIRS[i]
        base = {"A": 0, "B": 512, "C": 1024}[kind]
        heads = (2 * j, 2 * j + 1) if kind == "B" else (j, j + 4)
        return np.concatenate([base + h * HD + np.arange(HD) for h in heads])

    w_in_units = []
    for what, i in schedule(0)[1]:
        if what not in ("k", "q"):
            continue
        kind, j = PAIRS[i]
        if what == "k":
            a = j * P if kind == "B" else 0
            w_in_units.append(np.concatenate([off["k" + kind] + a + np.arange(P), off["v" + kind] + a + np.arange(P)]))
        else:
            mixed = pair_cols(i)
            own = mixed - {"A": 0, "B": 512, "C": 1024}[kind]
            w_in_units.append(np.concatenate([off["q" + kind] + own, off["gate"] + mixed]))
    out_rows = np.concatenate([pair_cols(i) for i in range(12)])
    order2 = np.concatenate([np.arange(512, 1024), np.arange(512), np.arange(1024, 2560)])

    def lru_unit():
        out = np.zeros((16, P, P), f32)
        for g, name in enumerate(("lru_wr_2", "lru_wi_2")):
            for d in range(2):
                for h in range(8):
                    s = slice(h % 2 * HD, h % 2 * HD + HD)
                    out[(g * 2 + d) * 4 + h // 2, s, s] = x[name][0, d, h]
        return out.transpose(1, 0, 2).reshape(P, UNIT)

    def filter_unit():
        out = np.zeros((P, UNIT), f32)
        out[:64] = x["filt_w3_2"][0]
        out[64] = x["filt_b3_2"][0]
        return out

    def make(name, layer, u):
        c256 = slice(u * 256, u * 256 + 256)
        if name == "ada":
            return unit(x["ada_w"][layer][:, c256])
        if name == "w_mod":
            return unit(x["w_mod_2"][layer][:, c256])
        if name == "w_in":
            return unit(x["w_in"][layer][:, w_in_units[u]])
        if name == "w_out":
            return unit(x["w_out"][layer][out_rows, u * P:u * P + P])
        if name == "w_in_2":
            return unit(x["w_in_2"][0][:, order2[c256]])
        if name == "w_out_2":
            return unit(x["w_out_2"][0][:, c256])
        if name == "lru":
            return lru_unit()
        if name == "filt_w3":
            return filter_unit()
        if name == "cf_w1":
            cc = np.concatenate([u * P + np.arange(P), D + u * P + np.arange(P)])
            return unit(x["cf_w1_2"][0][:, cc])
        return unit(x["cf_w2_2"][0][:, c256])

    first, second = unit_order()
    r = np.arange(2)[:, None, None, None]
    col = np.arange(GRID_W)[None, :, None, None]
    rel_r = np.arange(16)[None, None, :, None] - r
    kc = np.arange(GRID_W)[None, None, None, :]
    start = np.clip(col - 8, 0, GRID_W - 16)
    inside = (kc >= start) & (kc < start + 16) & (rel_r >= 0) & (rel_r < 15)
    rr, cc = np.broadcast_arrays(np.clip(rel_r, 0, 14), np.clip(kc - col + 15, 0, 30))
    inside = np.broadcast_to(inside, rr.shape)
    bias = np.where(inside, x["rpb_b"][:, :, rr, cc], f32(MASKED)).reshape(DEPTH, 8, P, 16 * GRID_W)

    small = np.zeros((P, 640), f32)
    small[:33, 0:64] = x["filt_w1_2"][0]
    small[:64, 64:128] = x["filt_w2_2"][0]
    small[:33, 128:640] = c["z"].T
    return {
        "consts": c["consts"], "vecs": vecs,
        "x0": np.concatenate([feature_major(x["x"][0]), feature_major(x["ctx"][0])], axis=2),
        "ctx2": feature_major(x["ctx_2"][0]),
        "units1": np.stack([make(*u) for u in first]), "units2": np.stack([make(*u) for u in second]),
        "bias_b": bias.astype(f32),
        "dft_cos": c["dft_cos"], "dft_sin": c["dft_sin"], "dft_nyq": c["dft_nyq"], "dft_alt": c["dft_alt"],
        "window": c["window"], "filt_small": small,
        "router": np.ascontiguousarray(x["router_2"].reshape(DEPTH, KT, P, N_EXPERTS).transpose(0, 2, 1, 3)),
        "exp_w1": x["exp_w1_2"], "exp_w3": x["exp_w3_2"], "exp_w2": x["exp_w2_2"],
    }


def kernel(**inputs):
    import concourse.bacc as bacc
    from concourse.bass_utils import run_bass_kernel_spmd

    arrays = {name: np.ascontiguousarray(a) for name, a in
              lay_out({k: np.asarray(v) for k, v in inputs.items()}).items()}
    nc = bacc.Bacc("TRN2", target_bir_lowering=False, num_devices=1)
    aps = {name: nc.dram_tensor("in_" + name, a.shape, mybir.dt.from_np(a.dtype), kind="ExternalInput").ap()
           for name, a in arrays.items()}
    aps["out"] = nc.dram_tensor("out_t", (P, KT, N), mybir.dt.float32, kind="ExternalOutput").ap()
    build(nc, aps)
    r = run_bass_kernel_spmd(nc, [{"in_" + name: a for name, a in arrays.items()}], core_ids=[0])
    return r.results[0]["out_t"].transpose(2, 1, 0).reshape(1, N, D)
```

```python
import numpy as np
import concourse.bass as bass
from concourse import mybir
from contextlib import ExitStack

P = 128
D = 1024
KT = D // P
N = 512
NC = 256
NA = N + NC
TT = N // P
DEPTH = 2
HD = 64
GRID_W = 64
ROWS = N // GRID_W
N_EXPERTS = 16
CAP = 2 * N // N_EXPERTS
EPS = 1e-6
RING = 6
UNIT = 2048
MASKED = -1e30
PAIRS = [("B", j) for j in range(4)] + [("A", j) for j in range(4)] + [("C", j) for j in range(4)]
LRU_BEFORE = [0, 3, 5, 8]
HYENA_UNITS = ["filt_w3", "window", "dft_cos", "dft_sin", "dft_edge"]
TAPS = ROWS - 1
NF = N

VECTORS = [("norm_w", 16), ("final_norm_w", 8), ("norm1_g", 16), ("norm2_g", 16), ("final_g", 8),
           ("qn", 2), ("kn", 2), ("sink", 16), ("mod_b", 288), ("cvec", 32), ("conv_a_w", 16),
           ("conv_a_b", 4), ("lru_br", 8), ("lru_bi", 8), ("lru_lam", 8), ("conv_b_w", 36),
           ("conv_b_b", 12), ("filt_b1", 1), ("filt_b2", 1), ("filt_f0", 1), ("filt_f1", 1),
           ("filt_bias", 8), ("cf_b1", 16), ("cf_dw_w", (2 * TAPS + 1) * 8), ("cf_dw_b", 8),
           ("cf_ln_g", 8), ("cf_ln_b", 8), ("cf_b2", 8), ("iota", CAP), ("kscale", 4)]
NV = sum(n for _, n in VECTORS)
VOFF = {}
_at = 0
for _name, _n in VECTORS:
    VOFF[_name] = _at
    _at += _n
CONSTS = [("ident", P), ("blk", P), ("ones", P), ("rot", P), ("cos", N), ("sin", N),
          ("mprev", P), ("mnext", P), ("sel", 2)]
NK = sum(n for _, n in CONSTS)
COFF = {}
_at = 0
for _name, _n in CONSTS:
    COFF[_name] = _at
    _at += _n
MOD_AT = [0, 48, 96, 192]
MOD_TILES = [24, 24, 48, 48]
BIAS_SLOTS = 3
BIAS_AT = [0, 2 * P, 2 * P, 5 * P]
BIAS_N = 7 * P
MOD_UNITS = 3
MOD_STEPS = [n // (2 * MOD_UNITS) for n in MOD_TILES]
FIRST_STEPS = MOD_STEPS[0] - 1
MODS_DONE = [FIRST_STEPS + 11, sum(MOD_STEPS)]


def insertions(layer):
    mods = [1] * 4 + [2] * 6 + [0] if layer == 0 else [2] * 2 + [3] * 8
    out = []
    for i, (kind, j) in enumerate(PAIRS):
        own = []
        if kind == "B" or j == 0:
            own += [("k", i), ("v", i)]
        own += [("q", i), ("g", i)]
        if kind == "B":
            own.append(("v_tokens", i))
        if kind != "B":
            for what in (("k", "q") if j == 0 else ("q",)):
                if kind == "A":
                    own.append(("norm_" + what, i))
                own.append(("rope_" + what, i))
        if 0 < i <= len(mods):
            own = [("mod_rows", mods[i - 1])] + own + [("mod_cols", mods[i - 1])]
        out.append(own)
    return out


def schedule(layer):
    tiles = 6 if layer == 0 else 4
    steps = [(i, h, t) for i in range(len(PAIRS)) for t in range(tiles) for h in range(2)]
    per = 2 * tiles
    inserted = insertions(layer)
    order = list(inserted[0])
    last = len(steps) - 1
    for n in range(-1, last + 2):
        if n + 1 <= last:
            order.append(("S", n + 1))
        if 0 <= n - 1 and n % 2 == 0:
            order.append(("O", n - 1))
        if 0 <= n <= last:
            order.append(("T", n))
        if n + 1 <= last:
            order.append(("E", n + 1))
        if 0 <= n <= last:
            i, at = divmod(n, per)
            if i + 1 < len(PAIRS):
                todo = inserted[i + 1]
                room = per - 2
                for x, item in enumerate(todo):
                    if x * room // len(todo) == at:
                        order.append(item)
    return steps, order


def unit_order():
    first = [("ada", 0, u) for u in range(9)]
    mods = {0: [("ada", 0, u) for u in range(9, 12)], 1: [("ada", 1, u) for u in range(12)], 2: [("w_mod", 0, u) for u in range(24)],
            3: [("w_mod", 1, u) for u in range(24)]}
    for layer in range(DEPTH):
        u = 0
        for item in schedule(layer)[1]:
            if item[0] in ("k", "q"):
                first.append(("w_in", layer, u))
                u += 1
            elif item[0] == "mod_rows":
                first += [mods[item[1]].pop(0) for _ in range(MOD_UNITS)]
        first += [("w_out", layer, m) for m in range(KT)]
    first += [("w_in_2", 0, u) for u in range(4)] + [("lru", 0, 0)] + [("w_in_2", 0, u) for u in range(4, 10)]
    first += [(table, 0, 0) for table in HYENA_UNITS]
    first += [("w_out_2", 0, u) for u in range(4)]
    second = [("cf_w1", 0, u) for u in range(8)] + [("cf_w2", 0, u) for u in range(4)]
    return first, second


class Count:

    def __init__(self):
        self.big = self.pt = 0
        self.seen = {}
        self.i, self.per, self.at_start = None, {}, {}

    def value(self, value, per=0):
        return value if self.i is None else self.i * per + value

    def next(self, name, k=1):
        self.seen[name] = self.seen.get(name, 0) + k
        return self.value(self.seen[name], self.per.get(name, 0))

    def next_big(self):
        self.big += 1
        return self.big - 1

    def next_pt(self):
        self.pt += 1
        return self.pt - 1

    def fills(self, k):
        return self.value(k + 1, self.per.get("big", 0))

    def over(self, k):
        return self.value(k // 2 + 1, self.per.get("big", 0) // 2)

    def pt_fills(self, m):
        return self.value(m + 1, self.per.get("pt", 0))

    def pt_over(self, m):
        return self.value(m + 1, self.per.get("pt", 0))

    def enter(self, i, per):
        self.i, self.per = i, per
        self.at_start = dict(self.seen, big=self.big, pt=self.pt)

    def leave(self, iterations):
        now = dict(self.seen, big=self.big, pt=self.pt)
        for name, value in now.items():
            grown = value - self.at_start.get(name, 0)
            assert grown == self.per.get(name, 0), (name, grown, self.per)
        for name, per in self.per.items():
            if name not in ("big", "pt") and name in self.seen:
                self.seen[name] += per * (iterations - 1)
        self.big += self.per["big"] * (iterations - 1)
        self.pt += self.per["pt"] * (iterations - 1)
        self.i, self.per = None, {}


def build(nc, A):
    F = mybir.dt.float32
    ALU = mybir.AluOpType
    ACT = mybir.ActivationFunctionType
    AX = mybir.AxisListType
    first_units, second_units = unit_order()
    MOE_UNITS = 24
    MOE_PAIRS = N_EXPERTS // 2
    MOE_ALL = MOE_UNITS * MOE_PAIRS
    MOE_RING = 2 * RING
    moe_base = [len(first_units), len(first_units) + MOE_ALL + len(second_units)]
    ring_base = [len(first_units), len(first_units) + len(second_units)]
    assert len(second_units) % RING == 0 and MOE_UNITS % MOE_RING == 0

    with ExitStack() as ctx:
        def sb(name, shape):
            return ctx.enter_context(nc.sbuf_tensor(name, shape, F))

        def pb(name, shape):
            return ctx.enter_context(nc.psum_tensor(name, shape, F))

        W = sb("W", [P, RING, UNIT])
        XC = sb("XC", [P, KT, NA])
        HT = sb("HT", [P, KT, NA])
        CONST = sb("CONST", [P, NK])
        VEC = sb("VEC", [P, NV])
        MOD = sb("MOD", [P, 288])
        CCS = sb("CCS", [P, 64])
        COEF = sb("COEF", [P, 16])
        EPSC = sb("EPSC", [P, 2])
        RS = sb("RS", [P, NA])
        STAT = sb("STAT", [P, 12])
        ROUTER = sb("ROUTER", [P, DEPTH, KT, N_EXPERTS])
        ARENA_N = 23600
        ARENA = sb("ARENA", [P, ARENA_N])

        BIG = [pb(f"BIG{s}", [P, 1024]) for s in range(2)]
        PT = pb("PT", [P, 1024])
        OP = pb("OP", [P, 512])
        MODP = pb("MODP", [P, 512])

        def const(name, a=0, n=None):
            n = n if n is not None else dict(CONSTS)[name]
            return CONST[:, COFF[name] + a:COFF[name] + a + n]

        def vec(name, a, n=1):
            return VEC[:, VOFF[name] + a:VOFF[name] + a + n]

        def mod(group, chunk, tile, which):
            c = MOD_AT[group] + 2 * (chunk * KT + tile) + which
            return MOD[:, c:c + 1]

        def mod_row(group, chunk, which):
            c = MOD_AT[group] + 2 * chunk * KT + which
            return MOD[:, c:c + 2 * KT - 1:2]

        class Arena:
            def __init__(self):
                self.at = 0

            def __call__(self, *shape):
                n = int(np.prod(shape))
                view = ARENA[:, self.at:self.at + n]
                self.at += n
                assert self.at <= ARENA_N, self.at
                if len(shape) == 2:
                    return view.rearrange("p (a b) -> p a b", b=shape[1])
                if len(shape) == 3:
                    return view.rearrange("p (a b c) -> p a b c", b=shape[1], c=shape[2])
                return view

        at = Arena()
        U = at(12, NA)
        Q = at(2, NA)
        K = at(2, NA)
        V = at(2, 6, P)
        SQT = at(NA)
        GATE_T = at(NA)
        SG = at(2, NA)
        PROB = at(2, NA + 1)
        PTS = at(2, NA)
        RB = at(2, HD)
        BIAS = at(BIAS_SLOTS, BIAS_N)
        ROPE_T = at(N)
        at = Arena()
        HY = at(12, N)
        XAC = at(4, N)
        YA = XAC
        lru_start = at.at
        GATE = at(4, N)
        CXC = at(4, NC)
        LR = at(2, NA)
        IX = at(2, NA)
        LA = at(2, NA)
        LT = at(NA)
        LH = at(2, NA)
        SPT = at(8, 8)
        XAR = at(4, N + 4)
        CXR = at(4, NC + 4)
        HYR = at(2, N + 4)
        sine_net = at(N)
        at.at = lru_start
        KF = at(8, N)
        ZF = at(8, N)
        FSMALL = RS[:, 0:640]
        HARG, HRND = const("cos"), const("sin")
        HID = sine_net
        hyena_slots = [(len(first_units) - 4 - len(HYENA_UNITS) + x) % RING for x in range(len(HYENA_UNITS))]
        FILT_W3 = W[:, hyena_slots[0], :]
        WIN, COS_T, SIN_T = (W[:, hyena_slots[x], :].rearrange("p (a b) -> p a b", b=N) for x in (1, 2, 3))
        NYQ_T = W[:, hyena_slots[4], 0:4 * P].rearrange("p (a b) -> p a b", b=P)
        ALT_T = W[:, hyena_slots[4], 4 * P:4 * P + N]
        HTF = HT[:, :, :].rearrange("p a b -> p (a b)")
        FS, FD, UT = (HTF[:, x * 2048:(x + 1) * 2048].rearrange("p (a b) -> p a b", b=N) for x in range(3))
        at = Arena()
        CU = at(KT, N)
        CY = at(KT, N)
        CSIG = at(2, N)
        CFT = at(2, N)
        conformer_end = at.at
        at = Arena()
        HTOK = at(TT, D)
        XS = at(KT, P)
        HX = at(D)
        HXT = at(KT, P)
        SIL = HX
        YK = at(D)
        ONEH = at(TT, 2, CAP)
        GONEH = at(TT, 2, CAP)
        GSCAT = at(N)
        PROBS = at(TT, N_EXPERTS)
        SLOT = at(TT, N_EXPERTS + 2)
        MAX8 = at(8)
        SMALL = at(16)
        ROW0, ROW1 = (XS.rearrange("p a b -> p (a b)")[:, x * N:x * N + N] for x in range(2))
        ROW2, ROW3 = (HXT.rearrange("p a b -> p (a b)")[:, x * N:x * N + N] for x in range(2))
        assert at.at <= conformer_end
        at.at = conformer_end
        W_MORE = at(RING, UNIT)

        def moe_slot(m):
            m %= MOE_RING
            return W[:, (moe_base[0] + m) % RING, :] if m < RING else W_MORE[:, m - RING, :]

        def sem(name):
            return ctx.enter_context(nc.semaphore(name))

        consts_loaded = sem("consts_loaded")
        x_loaded = sem("x_loaded")
        ctx2_loaded = sem("ctx2_loaded")
        unit_loaded = [sem(f"unit_loaded{s}") for s in range(RING)]
        moe_loaded = [sem(f"moe_loaded{s}") for s in range(MOE_RING)]
        unit_used = sem("unit_used")
        big_filled = sem("big_filled")
        big_free = [sem("big_free0"), sem("big_free1")]
        pt_filled = sem("pt_filled")
        pt_free = sem("pt_free")
        cvec_ready = sem("cvec_ready")
        mods_filled = sem("mods_filled")
        eps_ready = sem("eps_ready")
        squares = sem("squares")
        rs_ready = sem("rs_ready")
        h_scaled = sem("h_scaled")
        h_ready = sem("h_ready")
        qk_squared = sem("qk_squared")
        qk_rs = sem("qk_rs")
        qk_normed = sem("qk_normed")
        qk_roped = sem("qk_roped")
        gate_tanh = sem("gate_tanh")
        max_ready = sem("max_ready")
        sums_inverted = sem("sums_inverted")
        o_filled = sem("o_filled")
        y_ready = sem("y_ready")
        bias_loaded = [sem(f"bias_loaded{s}") for s in range(BIAS_SLOTS)]
        bias_used = sem("bias_used")
        act_chain = sem("act_chain")
        dve_chain = sem("dve_chain")
        pads_ready = sem("pads_ready")
        xa_ready = sem("xa_ready")
        hy_ready = sem("hy_ready")
        lam_exp = sem("lam_exp")
        decay_ready = sem("decay_ready")
        lru_gates = sem("lru_gates")
        lru_a = sem("lru_a")
        lru_v = sem("lru_v")
        lru_sqrt = sem("lru_sqrt")
        lru_done = sem("lru_done")
        hyena_loaded = sem("hyena_loaded")
        sin_arg = sem("sin_arg")
        sin_ready = sem("sin_ready")
        filt_ready = sem("filt_ready")
        spec_ready = sem("spec_ready")
        glu_sig = sem("glu_sig")
        dw_base = sem("dw_base")
        dw_ready = sem("dw_ready")
        centred = sem("centred")
        ln_scaled = sem("ln_scaled")
        cf_add = sem("cf_add")
        router_loaded = sem("router_loaded")
        block_done = sem("block_done")
        probs_ready = sem("probs_ready")
        slots_ready = sem("slots_ready")
        logits_exp = sem("logits_exp")
        onehot_ready = sem("onehot_ready")
        gates_ready = sem("gates_ready")
        out_ready = sem("out_ready")
        out_stored = sem("out_stored")

        def key_tiles(kind, t):
            if t >= TT:
                return [4, 5]
            if kind != "A":
                return list(range(max(t - 1, 0), min(t + 1, TT - 1) + 1)) + [4, 5]
            return list(range(6))

        def score_span(kind, t):
            b = NA + (kind == "C")
            if t >= TT:
                return N, b
            if kind != "A":
                return N - (min(t + 1, TT - 1) + 1 - max(t - 1, 0)) * P, b
            return 0, b

        def by_columns(tokens):
            return tokens.rearrange("p (r c) -> p c r", c=GRID_W)

        def query_tile(i, t, tokens):
            if PAIRS[i][0] != "B" or t >= TT:
                return tokens[:, t * P:t * P + P]
            return by_columns(tokens[:, 0:N])[:, t * P // ROWS:(t + 1) * P // ROWS, :]

        def like_query_tile(i, t, out):
            return out if PAIRS[i][0] != "B" or t >= TT else out.rearrange("p (c r) -> p c r", r=ROWS)

        block = ctx.enter_context(nc.Block())
        PER_PAIR = {"big": 8, "pt": 2}

        @block.sync
        def _(sp):
            sp.dma_start(CONST[:, :], A["consts"]).then_inc(consts_loaded, 16)
            sp.dma_start(VEC[:, :], A["vecs"]).then_inc(consts_loaded, 16)

            def load(n, src):
                if n >= RING:
                    sp.wait_ge(unit_used, n - RING + 1)
                sp.dma_start(W[:, n % RING, :], src).then_inc(unit_loaded[n % RING], 16)

            def stream(source, count, start):
                rounds = (count - start) // RING
                with sp.Fori(0, rounds) as i:
                    for s in range(RING):
                        n = start + s
                        sp.wait_ge(unit_used, i * RING + (n - RING + 1))
                        sp.dma_start(W[:, n % RING, :],
                                     source[bass.ds(i * RING + n, 1)].rearrange("a p n -> p (a n)"))\
                          .then_inc(unit_loaded[n % RING], 16)
                for n in range(start + rounds * RING, count):
                    load(n, source[n])

            def experts(layer):
                base = moe_base[layer]
                srcs = [A[w][layer].rearrange("e (q k p) n -> (e q) p k n", k=2, p=P)
                        for w in ("exp_w1", "exp_w3", "exp_w2")]

                def load_expert(m, src_of_pair):
                    which, q, expert = m // 8, m % 8 // 2, m % 2
                    sp.dma_start(moe_slot(m).rearrange("p (k n) -> p k n", k=2),
                                 srcs[which][bass.ds(src_of_pair + (4 * expert + q), 1)]
                                 .rearrange("a p k n -> p (a k) n"))\
                      .then_inc(moe_loaded[m % MOE_RING], 16)

                for m in range(MOE_RING):
                    if m < RING:
                        sp.wait_ge(unit_used, base + m - RING + 1)
                    elif m == RING:
                        sp.wait_ge(unit_used, base - 4)
                    load_expert(m, 0)
                with sp.Fori(0, MOE_PAIRS - 1) as i:
                    for x in range(MOE_UNITS):
                        m = MOE_RING + x
                        sp.wait_ge(unit_used, i * MOE_UNITS + (base + m - MOE_RING + 1))
                        load_expert(m % MOE_UNITS, i * 8 + 8 * (m // MOE_UNITS))
                for m in range(MOE_RING, MOE_UNITS):
                    sp.wait_ge(unit_used, base + MOE_ALL - MOE_UNITS + m - MOE_RING + 1)
                    load_expert(m, 8 * (MOE_PAIRS - 1))

            for n in range(RING):
                load(n, A["units1"][n])
                if n == 2:
                    sp.dma_start(XC[:, :, :], A["x0"]).then_inc(x_loaded, 16)
            stream(A["units1"], len(first_units), RING)
            experts(0)
            for u in range(len(second_units)):
                n = ring_base[0] + u
                before = moe_base[0] + MOE_ALL - (MOE_RING - u if u < RING else RING - u)
                sp.wait_ge(unit_used, before + 1)
                sp.dma_start(W[:, n % RING, :], A["units2"][u]).then_inc(unit_loaded[n % RING], 16)
            experts(1)
            for k in range(KT):
                sp.wait_ge(out_ready, k + 1)
                sp.dma_start(A["out"][:, k, :], HT[:, k, 0:N]).then_inc(out_stored, 16)
            sp.wait_ge(out_stored, 16 * KT)

        @block.gpsimd
        def _(pool):
            for layer in range(DEPTH):
                pool.dma_start(ROUTER[:, layer], A["router"][layer]).then_inc(router_loaded, 16)
            for layer in range(DEPTH):
                for h in range(8):
                    n = 8 * layer + h
                    if n >= BIAS_SLOTS:
                        pool.wait_ge(bias_used, n - BIAS_SLOTS + 1)
                    pool.dma_start(BIAS[:, n % BIAS_SLOTS, :], A["bias_b"][layer, h])\
                        .then_inc(bias_loaded[n % BIAS_SLOTS], 16)
            pool.wait_ge(h_scaled, 2 * KT)
            pool.dma_start(XC[:, :, N:NA], A["ctx2"]).then_inc(ctx2_loaded, 16)
            pool.wait_ge(h_ready, KT * 3)
            pool.dma_start(FSMALL, A["filt_small"]).then_inc(hyena_loaded, 16)

        @block.tensor
        def _(pe):
            me = Count()
            unit = {"n": 0, "open": 0}

            def mm(out, lhsT, rhs, start, stop):
                ins = pe.matmul(out, lhsT, rhs, start=start, stop=stop)
                if unit["open"]:
                    assert not (start and stop)
                    ins.then_inc(unit_used, unit["open"])
                    unit["open"] = 0
                return ins

            def next_unit():
                n = unit["n"]
                unit["n"] += 1
                pe.wait_ge(unit_loaded[n % RING], 16 * (n // RING + 1))
                return W[:, n % RING, :]

            def unit_done():
                unit["open"] += 1

            def mod_rows(group):
                k_use = me.next_big()
                if k_use >= 2:
                    pe.wait_ge(big_free[k_use % 2], me.over(k_use - 2))
                v = 0 if group < 2 else 2
                for x in range(MOD_UNITS):
                    w = next_unit().rearrange("p (k n) -> p k n", k=KT)
                    for half in range(2):
                        for j in range(4):
                            c = 4 * (4 * half + j) + v
                            last = mm(BIG[k_use % 2][32 * j:32 * j + 32, x * 256:x * 256 + 256],
                                      CCS[:, c:c + 32], w[:, 4 * half + j, :], half == 0, half == 1)
                    unit_done()
                last.then_inc(big_filled, 1)
                mod_use[0] = k_use

            def mod_cols(group):
                pe.wait_ge(big_free[mod_use[0] % 2], me.over(mod_use[0]))
                at = MOD_AT[group] + 2 * 2 * MOD_UNITS * mods_done[group]
                for x in range(2 * MOD_UNITS):
                    last = pe.matmul(MODP[:, at + 2 * x:at + 2 * x + 2], RS[:, x * P:x * P + P], const("sel"),
                                     start=True, stop=True)
                last.then_inc(mods_filled, 1)
                mods_done[group] += 1

            mods_done = [0, 0, 0, 0]
            mod_use = [0]

            def project(w, cols, src, n, K_TILES=KT, follow=False, last_output=None):
                k_use = me.next_big()
                if k_use >= 2:
                    pe.wait_ge(big_free[k_use % 2], me.over(k_use - 2))
                out = BIG[k_use % 2]
                for k in range(K_TILES):
                    lhsT = w[:, k, cols]
                    if follow:
                        pe.wait_ge(h_ready, me.next("h_ready"))
                    if last_output is not None and k == K_TILES - 1:
                        pe.wait_ge(y_ready, last_output)
                    last = mm(out[:, 0:N], lhsT, src[:, k, 0:N], k == 0, k == K_TILES - 1)
                if n > N:
                    for k in range(K_TILES):
                        last = mm(out[:, N:n], w[:, k, cols], src[:, k, N:n], k == 0, k == K_TILES - 1)
                last.then_inc(big_filled, 1)
                return k_use

            def norm_sums(n):
                k_use = me.next_big()
                if k_use >= 2:
                    pe.wait_ge(big_free[k_use % 2], me.over(k_use - 2))
                out = BIG[k_use % 2]
                for half in range(2):
                    for j in range(4):
                        k = 4 * half + j
                        pe.wait_ge(squares, me.next("squares"))
                        last = mm(out[32 * j:32 * j + 32, 0:N], const("ones", 0, 32), HT[:, k, 0:N],
                                  half == 0, half == 1)
                if n > N:
                    for half in range(2):
                        for j in range(4):
                            last = mm(out[32 * j:32 * j + 32, N:n], const("ones", 0, 32), HT[:, 4 * half + j, N:n],
                                      half == 0, half == 1)
                last.then_inc(big_filled, 1)
                pe.wait_ge(big_free[k_use % 2], me.over(k_use))
                k_use = me.next_big()
                pe.wait_ge(big_free[k_use % 2], me.over(k_use - 2))
                out = BIG[k_use % 2]
                last = pe.matmul(out[:, 0:N], const("ones"), RS[:, 0:N], start=True, stop=True)
                if n > N:
                    last = pe.matmul(out[:, N:n], const("ones"), RS[:, N:n], start=True, stop=True)
                last.then_inc(big_filled, 1)

            def attention(layer):
                steps, order = schedule(layer)
                nq = NA if layer == 0 else N
                score_use, probs_at, k_ready, q_ready = {}, {}, {}, {}
                raw_use = {}
                kv = {"n": -1}
                buf_of = {}
                w = None
                for what, x in order:
                    if what == "mod_rows":
                        mod_rows(x)
                    elif what == "mod_cols":
                        mod_cols(x)
                    elif what == "k":
                        w = next_unit().rearrange("p (k n) -> p k n", k=KT)
                        raw_use["k", x] = project(w, slice(0, P), HT, NA, follow=x == 0)
                        kv["n"] += 1
                        if PAIRS[x][0] == "B":
                            k_ready[x] = ("use", raw_use["k", x])
                    elif what == "v" and PAIRS[x][0] == "B":
                        raw_use["v", x] = project(w, slice(P, 2 * P), HT, NA)
                        unit_done()
                    elif what == "v_tokens":
                        pe.wait_ge(big_free[raw_use["v", x] % 2], me.over(raw_use["v", x]))
                        k_use = k_ready["v", x] = me.next_big()
                        pe.wait_ge(big_free[k_use % 2], me.over(k_use - 2))
                        for t in range(6):
                            last = pe.transpose(BIG[k_use % 2][:, t * P:t * P + P], SQT[:, t * P:t * P + P],
                                                const("ident"))
                        last.then_inc(big_filled, 1)
                    elif what == "v":
                        k_use = me.next_big()
                        if k_use >= 2:
                            pe.wait_ge(big_free[k_use % 2], me.over(k_use - 2))
                        for t in range(6):
                            for k in range(KT):
                                last = mm(BIG[k_use % 2][:, t * P:t * P + P], HT[:, k, t * P:t * P + P],
                                          w[:, k, P:2 * P], k == 0, k == KT - 1)
                        last.then_inc(big_filled, 1)
                        unit_done()
                        k_ready["v", x] = k_use
                    elif what == "q":
                        w = next_unit().rearrange("p (k n) -> p k n", k=KT)
                        raw_use["q", x] = project(w, slice(0, P), HT, nq)
                        buf_of[x] = kv["n"] % 2
                        if PAIRS[x][0] == "B":
                            q_ready[x] = ("use", raw_use["q", x])
                    elif what == "g":
                        project(w, slice(P, 2 * P), HT, nq)
                        unit_done()
                    elif what.startswith("norm_"):
                        pe.wait_ge(qk_squared, me.next("qk_squared"))
                        n = NA if what == "norm_k" else nq
                        k_use = me.next_big()
                        if k_use >= 2:
                            pe.wait_ge(big_free[k_use % 2], me.over(k_use - 2))
                        last = pe.matmul(BIG[k_use % 2][:, 0:N], const("blk"), SQT[:, 0:N],
                                         start=True, stop=True)
                        if n > N:
                            last = pe.matmul(BIG[k_use % 2][:, N:n], const("blk"), SQT[:, N:n],
                                             start=True, stop=True)
                        last.then_inc(big_filled, 1)
                    elif what.startswith("rope_"):
                        if PAIRS[x][0] == "A":
                            pe.wait_ge(qk_normed, me.next("qk_normed"))
                        else:
                            pe.wait_ge(big_free[(raw_use[what[5:], x]) % 2], me.over(raw_use[what[5:], x]))
                        src = K[:, kv["n"] % 2, 0:N] if what == "rope_k" else Q[:, x % 2, 0:N]
                        k_use = me.next_big()
                        if k_use >= 2:
                            pe.wait_ge(big_free[k_use % 2], me.over(k_use - 2))
                        pe.matmul(BIG[k_use % 2][:, 0:N], const("rot"), src, start=True, stop=True)\
                            .then_inc(big_filled, 1)
                        (k_ready if what == "rope_k" else q_ready)[x] = ("roped", None)
                    elif what == "S":
                        i, h, t = steps[x]
                        kind, j = PAIRS[i]
                        if h == 0 and t == 0:
                            for ready in (k_ready, q_ready):
                                if i in ready:
                                    how, use = ready[i]
                                    if how == "use":
                                        pe.wait_ge(big_free[use % 2], me.over(use))
                                    else:
                                        pe.wait_ge(qk_roped, me.next("qk_roped"))
                        k_use = score_use[x] = me.next_big()
                        if k_use >= 2:
                            pe.wait_ge(big_free[k_use % 2], me.over(k_use - 2))
                        out = BIG[k_use % 2]
                        rows = slice(HD * h, HD * h + HD)
                        lhsT = Q[rows, i % 2, t * P:t * P + P]
                        keys = K[:, buf_of[i], :]
                        if t < TT:
                            if kind != "A":
                                a, b = max(t - 1, 0), min(t + 1, TT - 1) + 1
                                pe.matmul(out[:, N - (b - a) * P:N], lhsT, keys[rows, a * P:b * P],
                                          start=True, stop=True)
                            else:
                                pe.matmul(out[:, 0:N], lhsT, keys[rows, 0:N], start=True, stop=True)
                        pe.matmul(out[:, N:NA], lhsT, keys[rows, N:NA], start=True, stop=True)\
                            .then_inc(big_filled, 1)
                    elif what == "T":
                        i, h, t = steps[x]
                        pe.wait_ge(big_free[score_use[x] % 2], me.over(score_use[x]))
                        m = probs_at[x] = me.next_pt()
                        if m >= 1:
                            pe.wait_ge(pt_free, me.pt_over(m - 1))
                        tiles = key_tiles(PAIRS[i][0], t)
                        for y in range(len(tiles)):
                            last = pe.transpose(PT[:, y * P:y * P + P], PROB[:, x % 2, y * P:y * P + P],
                                                const("ident"))
                        last.then_inc(pt_filled, 1)
                    elif what == "O":
                        i, h, t = steps[x]
                        kind = PAIRS[i][0]
                        pe.wait_ge(pt_free, me.pt_over(probs_at[x]))
                        if ("v", i) in k_ready and t == 0:
                            pe.wait_ge(big_free[k_ready["v", i] % 2], me.over(k_ready["v", i]))
                        if y_before[layer] + x // 2:
                            pe.wait_ge(y_ready, y_before[layer] + x // 2)
                        tiles = key_tiles(kind, t)
                        for y, tile in enumerate(tiles):
                            for head in range(2):
                                pe.matmul(OP[head * HD:head * HD + HD, 0:P],
                                          V[:, buf_of[i], tile, head * HD:head * HD + HD],
                                          PTS[:, head, y * P:y * P + P], start=y == 0, stop=y == len(tiles) - 1)
                        pe.wait_ge(sums_inverted, me.next("sums_inverted"))
                        pe.matmul(OP[:, P:2 * P], RB.rearrange("p h d -> p (h d)"), const("ident"),
                                  start=True, stop=True).then_inc(o_filled, 1)
                outputs = y_before[layer] + len(steps) // 2
                pe.wait_ge(y_ready, outputs - nq // P)
                for m in range(KT):
                    w = next_unit()[:, 0:12 * P].rearrange("p (k n) -> p k n", k=12)
                    project(w, slice(0, P), U, nq, 12, last_output=outputs if m == 0 else None)
                    unit_done()

            def lru_gates_of(t, w):
                pe.wait_ge(xa_ready, me.next("xa_ready"))
                for d in range(2):
                    for g in range(2):
                        k_use = me.next_big()
                        pe.wait_ge(big_free[k_use % 2], me.over(k_use - 2))
                        lhsT = w[:, (g * 2 + d) * 4 + t, :]
                        out = BIG[k_use % 2]
                        pe.matmul(out[:, 0:N], lhsT, XAC[:, t, :], start=True, stop=True)
                        pe.matmul(out[:, N:NA], lhsT, CXC[:, t, :], start=True, stop=True)\
                            .then_inc(big_filled, 1)

            def even_layer():
                lru_weights = None
                for u in range(10):
                    if u == 4:
                        lru_weights = next_unit().rearrange("p (g n) -> p g n", n=P)
                    w = next_unit().rearrange("p (k n) -> p k n", k=KT)
                    for half in range(2):
                        y = 2 * (u - 4) + half
                        if y in (0, 6):
                            if y == 0:
                                pe.wait_ge(hyena_loaded, me.next("hyena_loaded", 16))
                                lhsT, rhs = FSMALL[0:33, 0:64], FSMALL[0:33, 128:640]
                            else:
                                pe.wait_ge(sin_ready, me.next("sin_ready"))
                                lhsT, rhs = FSMALL[0:64, 64:128], HID[0:64, :]
                            k_use = me.next_big()
                            pe.wait_ge(big_free[k_use % 2], me.over(k_use - 2))
                            pe.matmul(BIG[k_use % 2][0:64, 0:N], lhsT, rhs, start=True, stop=True)\
                                .then_inc(big_filled, 1)
                        if y in LRU_BEFORE:
                            lru_gates_of(LRU_BEFORE.index(y), lru_weights)
                            if y == LRU_BEFORE[-1]:
                                for _ in range(u - 3):
                                    unit_done()
                        project(w, slice(half * P, half * P + P), HT, NA if u < 2 else N,
                                follow=u == 0 and half == 0)
                    if u < 4 or y > LRU_BEFORE[-1]:
                        unit_done()
                assert unit["n"] % RING == hyena_slots[0]
                for _ in HYENA_UNITS:
                    next_unit()
                pe.wait_ge(sin_ready, me.next("sin_ready"))
                for o in range(2):
                    for t in range(TT):
                        k_use = me.next_big()
                        if k_use >= 2:
                            pe.wait_ge(big_free[k_use % 2], me.over(k_use - 2))
                        for way in range(2):
                            c = (o * 2 + way) * 512
                            ins = pe.matmul(BIG[k_use % 2][:, way * N:way * N + N], HID[0:65, t * P:t * P + P],
                                            FILT_W3[0:65, c:c + 512], start=True, stop=True)
                            if way == 0 and unit["open"]:
                                ins.then_inc(unit_used, unit["open"])
                                unit["open"] = 0
                        ins.then_inc(big_filled, 1)
                    for f in range(4):
                        k_use = me.next_big()
                        if k_use >= 2:
                            pe.wait_ge(big_free[k_use % 2], me.over(k_use - 2))
                        out = BIG[k_use % 2]
                        fs = slice(f * P, f * P + P)
                        for t in range(TT):
                            if f == 0:
                                pe.wait_ge(filt_ready, me.next("filt_ready"))
                            mm(out[:, 0:N], COS_T[:, t, fs], FS[:, t, :], t == 0, t == TT - 1)
                        for t in range(TT):
                            last = mm(out[:, N:1024], SIN_T[:, t, fs], FD[:, t, :], t == 0, t == TT - 1 and f > 0)
                        if f == 0:
                            for t in range(TT):
                                last = mm(out[:, N:1024], NYQ_T[:, t, :], FS[:, t, :], False, t == TT - 1)
                        last.then_inc(big_filled, 1)
                        spec_use = k_use
                    if o == 0:
                        pe.wait_ge(hy_ready, 12)
                    for half in range(2):
                        k_use = me.next_big()
                        if k_use >= 2:
                            pe.wait_ge(big_free[k_use % 2], me.over(k_use - 2))
                        for t in range(2):
                            for c in range(4):
                                if o == 1 and half == 0 and t == 0:
                                    pe.wait_ge(big_free[conv_uses[c] % 2], me.over(conv_uses[c]))
                                tok = (2 * half + t) * P
                                last = pe.transpose(BIG[k_use % 2][:, t * N + c * P:t * N + c * P + P],
                                                    HY[:, c, tok:tok + P], const("ident"))
                        last.then_inc(big_filled, 1)
                    signal_uses = [k_use - 1, k_use]
                    for f in range(4):
                        k_use = me.next_big()
                        if k_use >= 2:
                            pe.wait_ge(big_free[k_use % 2], me.over(k_use - 2))
                        out = BIG[k_use % 2]
                        fs = slice(f * P, f * P + P)
                        for t in range(TT):
                            if f == 0 and t % 2 == 0:
                                half_use = signal_uses[t // 2]
                                pe.wait_ge(big_free[half_use % 2], me.over(half_use))
                            mm(out[:, 0:N], COS_T[:, t, fs], UT[:, t, :], t == 0, t == TT - 1)
                        for t in range(TT):
                            last = mm(out[:, N:1024], SIN_T[:, t, fs], UT[:, t, :], t == 0, t == TT - 1 and f > 0)
                        if f == 0:
                            for t in range(TT):
                                last = mm(out[:, N:1024], NYQ_T[:, t, :], UT[:, t, :], False, t == TT - 1)
                        last.then_inc(big_filled, 1)
                    conv_uses = []
                    for c in range(4):
                        k_use = me.next_big()
                        if k_use >= 2:
                            pe.wait_ge(big_free[k_use % 2], me.over(k_use - 2))
                        out = BIG[k_use % 2][:, 0:N]
                        cs = slice(c * P, c * P + P)
                        for f in range(4):
                            if c == 0:
                                pe.wait_ge(spec_ready, me.next("spec_ready"))
                            mm(out, ZF[:, f, cs], COS_T[:, f, :], f == 0, False)
                            mm(out, ZF[:, 4 + f, cs], SIN_T[:, f, :], False, False)
                        mm(out, ZF[0:1, 4, cs], ALT_T[0:1, :], False, True).then_inc(big_filled, 1)
                        conv_uses.append(k_use)
                for _ in HYENA_UNITS:
                    unit_done()
                for u in range(4):
                    w = next_unit().rearrange("p (k n) -> p k n", k=KT)
                    for half in range(2):
                        k_use = me.next_big()
                        if k_use >= 2:
                            pe.wait_ge(big_free[k_use % 2], me.over(k_use - 2))
                        for k in range(KT):
                            src = YA[:, k, :] if k < 4 else HY[:, k - 4, :]
                            if u == 0 and half == 0 and k >= 4:
                                pe.wait_ge(big_free[conv_uses[k - 4] % 2], me.over(conv_uses[k - 4]))
                            last = mm(BIG[k_use % 2][:, 0:N], w[:, k, half * P:half * P + P], src,
                                      k == 0, k == KT - 1)
                        last.then_inc(big_filled, 1)
                    unit_done()

            def conformer():
                for j in range(KT):
                    w = next_unit().rearrange("p (k n) -> p k n", k=KT)
                    k_use = me.next_big()
                    if k_use >= 2:
                        pe.wait_ge(big_free[k_use % 2], me.over(k_use - 2))
                    for half in range(2):
                        for k in range(KT):
                            if j == 0 and half == 0:
                                pe.wait_ge(h_ready, me.next("h_ready"))
                            last = mm(BIG[k_use % 2][:, half * N:half * N + N], w[:, k, half * P:half * P + P],
                                      HT[:, k, 0:N], k == 0, k == KT - 1)
                    last.then_inc(big_filled, 1)
                    unit_done()
                k_use = me.next_big()
                pe.wait_ge(big_free[k_use % 2], me.over(k_use - 2))
                for k in range(KT):
                    pe.wait_ge(dw_ready, me.next("dw_ready"))
                    last = mm(BIG[k_use % 2][:, 0:N], const("ones"), CY[:, k, 0:N], k == 0, k == KT - 1)
                last.then_inc(big_filled, 1)
                norm_sums(N)
                for u in range(4):
                    w = next_unit().rearrange("p (k n) -> p k n", k=KT)
                    for half in range(2):
                        project(w, slice(half * P, half * P + P), CU, N, follow=u == 0 and half == 0)
                    unit_done()

            def experts(layer):
                pe.wait_ge(router_loaded, 16 * DEPTH)
                m_pt = me.next_pt()
                if m_pt >= 1:
                    pe.wait_ge(pt_free, me.pt_over(m_pt - 1))
                for t in range(TT):
                    for k in range(KT):
                        if t == 0:
                            pe.wait_ge(h_ready, me.next("h_ready"))
                        last = mm(PT[:, t * 16:t * 16 + 16], HT[:, k, t * P:t * P + P], ROUTER[:, layer, k, :],
                                  k == 0, k == KT - 1)
                last.then_inc(pt_filled, 1)
                for t in range(TT):
                    k_use = me.next_big()
                    if k_use >= 2:
                        pe.wait_ge(big_free[k_use % 2], me.over(k_use - 2))
                    for k in range(KT):
                        last = pe.transpose(BIG[k_use % 2][:, k * P:k * P + P], HT[:, k, t * P:t * P + P],
                                            const("ident"))
                    last.then_inc(big_filled, 1)
                tok_use = k_use
                pe.wait_ge(probs_ready, me.next("probs_ready"))
                m_pt = me.next_pt()
                if m_pt >= 1:
                    pe.wait_ge(pt_free, me.pt_over(m_pt - 1))
                for t in range(TT):
                    last = pe.transpose(PT[0:16, t * P:t * P + P], PROBS[:, t, :], const("ident"))
                last.then_inc(pt_filled, 1)
                pe.wait_ge(slots_ready, me.next("slots_ready"))
                m_pt = me.next_pt()
                if m_pt >= 1:
                    pe.wait_ge(pt_free, me.pt_over(m_pt - 1))
                for t in range(TT):
                    last = pe.transpose(PT[:, t * 16:t * 16 + 16], ROW1[0:16, t * P:t * P + P],
                                        const("ident")[0:16, 0:16])
                last.then_inc(pt_filled, 1)
                pe.wait_ge(big_free[tok_use % 2], me.over(tok_use))
                pe.wait_ge(big_free[(tok_use - 1) % 2], me.over(tok_use - 1))
                assert not unit["open"] and unit["n"] == ring_base[layer]

                def gather():
                    pe.wait_ge(onehot_ready, me.next("onehot_ready"))
                    k_use = me.next_big()
                    pe.wait_ge(big_free[k_use % 2], me.over(k_use - 2))
                    for k in range(KT):
                        for t in range(TT):
                            last = mm(BIG[k_use % 2][:, k * P:k * P + P], HTOK[:, t, k * P:k * P + P],
                                      ONEH[:, t, :, :].rearrange("p a b -> p (a b)"), t == 0, t == TT - 1)
                    last.then_inc(big_filled, 1)
                    return k_use

                k_use = gather()
                pe.wait_ge(big_free[k_use % 2], me.over(k_use))
                with pe.Fori(0, MOE_PAIRS) as i:
                    me.enter(i, dict(PER_PAIR, onehot_ready=1, gates_ready=1))

                    def both_experts(out, rows, which):
                        for q in range(4):
                            w = []
                            for m in range(8 * which + 2 * q, 8 * which + 2 * q + 2):
                                rounds = layer * (MOE_ALL // MOE_RING) + m // MOE_RING + 1
                                pe.wait_ge(moe_loaded[m % MOE_RING],
                                           me.value(16 * rounds, 16 * MOE_UNITS // MOE_RING))
                                w.append(moe_slot(m).rearrange("p (k n) -> p k n", k=2))
                            for k in range(2):
                                for half in range(2):
                                    for e in range(2):
                                        last = mm(out[e * CAP:e * CAP + CAP, half * 512:half * 512 + 512],
                                                  rows[:, 2 * q + k, e * CAP:e * CAP + CAP],
                                                  w[e][:, k, half * 512:half * 512 + 512],
                                                  q == 0 and k == 0, q == 3 and k == 1)
                            unit_done()
                            unit_done()
                        last.then_inc(big_filled, 1)

                    k_use = me.next_big()
                    pe.wait_ge(big_free[k_use % 2], me.over(k_use - 2))
                    both_experts(BIG[k_use % 2], XS, 0)
                    pe.wait_ge(gates_ready, me.next("gates_ready"))
                    m_gate = me.next_pt()
                    pe.wait_ge(pt_free, me.pt_over(m_gate - 1))
                    for t in range(TT):
                        ins = pe.transpose(PT[:, t * P:t * P + P],
                                           GONEH[:, t, :, :].rearrange("p a b -> p (a b)"), const("ident"))
                        if t == 0:
                            ins.then_inc(unit_used, unit["open"])
                            unit["open"] = 0
                    ins.then_inc(pt_filled, 1)
                    k_hidden = me.next_big()
                    pe.wait_ge(big_free[k_hidden % 2], me.over(k_hidden - 2))
                    both_experts(BIG[k_hidden % 2], XS, 1)
                    k_next = gather()
                    pe.wait_ge(big_free[k_hidden % 2], me.over(k_hidden))
                    m_hid = me.next_pt()
                    pe.wait_ge(pt_free, me.pt_over(m_hid - 1))
                    for f in range(KT):
                        ins = pe.transpose(PT[:, f * P:f * P + P], HX[:, f * P:f * P + P], const("ident"))
                    ins.then_inc(pt_filled, 1)
                    pe.wait_ge(big_free[k_next % 2], me.over(k_next))
                    pe.wait_ge(pt_free, me.pt_over(m_hid))
                    k_use = me.next_big()
                    pe.wait_ge(big_free[k_use % 2], me.over(k_use - 2))
                    both_experts(BIG[k_use % 2], HXT, 2)
                    pe.wait_ge(big_free[k_use % 2], me.over(k_use))
                    for m2 in range(4):
                        k_use = me.next_big()
                        if k_use >= 2:
                            pe.wait_ge(big_free[k_use % 2], me.over(k_use - 2))
                        for half in range(2):
                            m = 2 * m2 + half
                            last = pe.matmul(BIG[k_use % 2][:, half * N:half * N + N], YK[:, m * P:m * P + P],
                                             GSCAT[:, :], start=True, stop=True)
                            if m == 0:
                                last.then_inc(unit_used, unit["open"])
                                unit["open"] = 0
                        last.then_inc(big_filled, 1)
                    me.leave(MOE_PAIRS)

            y_before = [0, len(PAIRS) * NA // P]
            pe.wait_ge(consts_loaded, 32)
            pe.wait_ge(cvec_ready, me.next("cvec_ready", 2))
            for _ in range(FIRST_STEPS):
                mod_rows(0)
                mod_cols(0)
            for layer in range(DEPTH):
                norm_sums(NA)
                attention(layer)
            norm_sums(N)
            norm_sums(NA)
            even_layer()
            norm_sums(N)
            experts(0)
            norm_sums(N)
            conformer()
            norm_sums(N)
            experts(1)
            norm_sums(N)

        @block.scalar
        def _(act):
            me = Count()

            def norm(n, updates, shift, follow=None):
                for k in range(KT):
                    if follow is not None:
                        act.wait_ge(follow, k + 1)
                    if updates:
                        act.wait_ge(big_free[updates[k] % 2], me.over(updates[k]))
                    act.activation(HT[:, k, 0:n], XC[:, k, 0:n], ACT.Square).then_inc(squares, 1)
                k_use = me.next_big()
                act.wait_ge(big_filled, me.fills(k_use))
                act.activation(RS[:, 0:n], BIG[k_use % 2][:, 0:n], ACT.Copy).then_inc(big_free[k_use % 2], 1)
                k_use = me.next_big()
                act.wait_ge(big_filled, me.fills(k_use))
                act.activation(RS[:, 0:n], BIG[k_use % 2][:, 0:n], ACT.Ln, bias=EPSC[:, 0:1],
                               scale=1.0 / (32 * D))\
                    .then_inc(big_free[k_use % 2], 1)
                act.wait_ge(big_free[k_use % 2], me.over(k_use))
                act.activation(RS[:, 0:n], RS[:, 0:n], ACT.Exp, scale=-0.5).then_inc(rs_ready, 1)
                if shift is None:
                    return
                for k in range(KT):
                    act.wait_ge(h_scaled, me.next("h_scaled"))
                    ins = act.activation(HT[:, k, 0:N], HT[:, k, 0:N], ACT.Identity, bias=shift(k, 0))
                    if n > N:
                        ins = act.activation(HT[:, k, N:n], HT[:, k, N:n], ACT.Identity, bias=shift(k, 1))
                    ins.then_inc(h_ready, 1)

            def attention(layer):
                steps, order = schedule(layer)
                nq = NA if layer == 0 else N
                kv = -1
                score_use = {}
                for what, x in order:
                    if what == "mod_rows":
                        mod_rows()
                    elif what in ("k", "q"):
                        if what == "k":
                            kv += 1
                        kind = PAIRS[x][0]
                        n = NA if what == "k" else nq
                        k_use = me.next_big()
                        act.wait_ge(big_filled, me.fills(k_use))
                        dst = K[:, kv % 2, 0:n] if what == "k" else Q[:, x % 2, 0:n]
                        scale = HD ** -0.5 if what == "q" and kind != "A" else 1.0
                        if kind == "B":
                            ins = act.activation(dst[:, 0:N].rearrange("p (c r) -> p c r", r=ROWS),
                                                 by_columns(BIG[k_use % 2][:, 0:N]), ACT.Copy, scale=scale)
                            if n > N:
                                ins = act.activation(dst[:, N:n], BIG[k_use % 2][:, N:n], ACT.Copy, scale=scale)
                        else:
                            ins = act.activation(dst, BIG[k_use % 2][:, 0:n], ACT.Copy, scale=scale)
                        ins.then_inc(big_free[k_use % 2], 1)
                        raw = (k_use, dst, n)
                        raws[what, x] = raw
                        if kind == "A" and (what == "q" and PAIRS[x][1] or what == "k"):
                            square(raw)
                    elif what == "v" and PAIRS[x][0] == "B":
                        k_use = me.next_big()
                        act.wait_ge(big_filled, me.fills(k_use))
                        act.activation(SQT[:, 0:N].rearrange("p (c r) -> p c r", r=ROWS),
                                       by_columns(BIG[k_use % 2][:, 0:N]), ACT.Copy)
                        act.activation(SQT[:, N:NA], BIG[k_use % 2][:, N:NA], ACT.Copy)\
                            .then_inc(big_free[k_use % 2], 1)
                    elif what in ("v", "v_tokens"):
                        me.big += 1
                    elif what == "g":
                        k_use = me.next_big()
                        act.wait_ge(big_filled, me.fills(k_use))
                        act.activation(GATE_T[:, 0:nq], BIG[k_use % 2][:, 0:nq], ACT.Tanh, scale=0.5)\
                            .then_inc(gate_tanh, 1)
                    elif what.startswith("norm_"):
                        n = NA if what == "norm_k" else nq
                        k_use = me.next_big()
                        act.wait_ge(big_filled, me.fills(k_use))
                        scale, bias = (1.0 / HD, 0) if what == "norm_k" else (1.0, 1)
                        act.activation(SQT[:, 0:n], BIG[k_use % 2][:, 0:n], ACT.Ln, bias=EPSC[:, bias:bias + 1],
                                       scale=scale).then_inc(big_free[k_use % 2], 1)
                        act.wait_ge(big_free[k_use % 2], me.over(k_use))
                        act.activation(SQT[:, 0:n], SQT[:, 0:n], ACT.Exp, scale=-0.5).then_inc(qk_rs, 1)
                        if what == "norm_k":
                            act.wait_ge(qk_normed, me.next("qk_normed"))
                            square(raws["q", x])
                        else:
                            me.seen["qk_normed"] = me.seen.get("qk_normed", 0) + 1
                    elif what.startswith("rope_"):
                        me.big += 1
                    elif what == "S":
                        k_use = me.big
                        me.big += 1
                        score_use[x] = k_use
                    elif what == "E":
                        i, h, t = steps[x]
                        a, b = score_span(PAIRS[i][0], t)
                        k_use = score_use[x]
                        act.wait_ge(max_ready, me.next("max_ready"))
                        act.activation(PROB[:, x % 2, 0:b - a], BIG[k_use % 2][:, a:b], ACT.Exp,
                                       bias=STAT[:, x % 4:x % 4 + 1],
                                       accum_out=STAT[:, 4 + x % 4:5 + x % 4]).then_inc(big_free[k_use % 2], 1)
                    elif what == "T":
                        i, h, t = steps[x]
                        w = len(key_tiles(PAIRS[i][0], t)) * P
                        m_pt = me.next_pt()
                        act.wait_ge(pt_filled, me.pt_fills(m_pt))
                        act.activation(PTS[:, x % 2, 0:w], PT[:, 0:w], ACT.Copy).then_inc(pt_free, 1)
                uses = list(range(me.big, me.big + KT))
                me.big += KT
                act.wait_ge(mods_filled, me.next("mods_filled"))
                return uses

            raws = {}

            def mod_rows():
                k_use = me.next_big()
                act.wait_ge(big_filled, me.fills(k_use))
                if mod_waits[0]:
                    act.wait_ge(mods_filled, me.next("mods_filled"))
                mod_waits[0] = True
                act.activation(RS[:, :], BIG[k_use % 2][:, 0:NA], ACT.Copy).then_inc(big_free[k_use % 2], 1)

            mod_waits = [False]

            def square(raw):
                k_use, dst, n = raw
                act.wait_ge(big_free[k_use % 2], me.over(k_use))
                act.activation(SQT[:, 0:n], dst, ACT.Square).then_inc(qk_squared, 1)

            def even_layer():
                act.wait_ge(pads_ready, me.next("pads_ready"))
                act.activation(SPT[:, 0, :], vec("lru_lam", 0, 8), ACT.Abs).then_inc(act_chain, 1)
                act.wait_ge(act_chain, me.next("act_chain"))
                act.activation(SPT[:, 1, :], SPT[:, 0, :], ACT.Exp, scale=-1.0).then_inc(lam_exp, 1)
                for t in range(4):
                    k_use = me.next_big()
                    act.wait_ge(big_filled, me.fills(k_use))
                    act.activation(XAR[:, t, 1:1 + N], BIG[k_use % 2][:, 0:N], ACT.Copy)
                    act.activation(CXR[:, t, 1:1 + NC], BIG[k_use % 2][:, N:NA], ACT.Copy)\
                        .then_inc(big_free[k_use % 2], 1)
                for t in range(4):
                    k_use = me.next_big()
                    act.wait_ge(big_filled, me.fills(k_use))
                    act.activation(GATE[:, t, :], BIG[k_use % 2][:, 0:N], ACT.Gelu_apprx_tanh)\
                        .then_inc(big_free[k_use % 2], 1)

                def lru_gates_and_decay(t):
                    if t > 0:
                        act.wait_ge(lru_done, t)
                    else:
                        act.wait_ge(decay_ready, me.next("decay_ready"))
                    for d in range(2):
                        for g, (dst, name) in enumerate(((LR, "lru_br"), (IX, "lru_bi"))):
                            k_use = me.next_big()
                            act.wait_ge(big_filled, me.fills(k_use))
                            act.activation(dst[:, d, :], BIG[k_use % 2][:, 0:NA], ACT.Sigmoid,
                                           bias=vec(name, d * 4 + t)).then_inc(big_free[k_use % 2], 1)
                    for d in range(2):
                        s = d * 4 + t
                        k_use = me.big - 4 + 2 * d
                        act.wait_ge(big_free[k_use % 2], me.over(k_use))
                        act.activation(LA[:, d, :], LR[:, d, :], ACT.Exp, scale=SPT[:, 7, s:s + 1])
                        act.activation(LR[:, d, :], LR[:, d, :], ACT.Tanh, scale=SPT[:, 6, s:s + 1])\
                            .then_inc(lru_a, 1)

                def lru_roots():
                    for d in range(2):
                        act.wait_ge(lru_v, me.next("lru_v"))
                        act.activation(LR[:, d, :], LR[:, d, :], ACT.Sqrt).then_inc(lru_sqrt, 1)

                for t in range(12):
                    if t == 0 or t == 6:
                        me.big += 1
                    if t in LRU_BEFORE:
                        lru_gates_and_decay(LRU_BEFORE.index(t))
                    if t >= 2:
                        act.wait_ge(hy_ready, t - 1)
                    k_use = me.next_big()
                    act.wait_ge(big_filled, me.fills(k_use))
                    act.activation(HYR[:, t % 2, 1:1 + N], BIG[k_use % 2][:, 0:N], ACT.Copy)\
                        .then_inc(big_free[k_use % 2], 1)
                    if t in LRU_BEFORE:
                        lru_roots()
                    if t == 1 or t == 7:
                        act.wait_ge(sin_arg, me.next("sin_arg"))
                        act.activation(HID[0:64, :], HARG[0:64, :], ACT.Sin).then_inc(sin_ready, 1)
                for o in range(2):
                    me.big += TT
                    for f in range(4):
                        k_use = me.next_big()
                        act.wait_ge(big_filled, me.fills(k_use))
                        for part in range(2):
                            ins = act.activation(KF[:, part * 4 + f, :], BIG[k_use % 2][:, part * N:part * N + N],
                                                 ACT.Copy, scale=vec("kscale", f))
                        ins.then_inc(big_free[k_use % 2], 1)
                    for half in range(2):
                        k_use = me.next_big()
                        act.wait_ge(big_filled, me.fills(k_use))
                        act.activation(UT[:, 2 * half:2 * half + 2, :],
                                       BIG[k_use % 2][:, :].rearrange("p (a b) -> p a b", b=N), ACT.Copy)\
                            .then_inc(big_free[k_use % 2], 1)
                    me.big += 8
                uses = list(range(me.big, me.big + KT))
                me.big += KT
                return uses

            def conformer():
                for j in range(KT):
                    k_use = me.next_big()
                    act.wait_ge(big_filled, me.fills(k_use))
                    act.activation(CSIG[:, j % 2, :], BIG[k_use % 2][:, N:1024], ACT.Sigmoid,
                                   bias=vec("cf_b1", KT + j)).then_inc(glu_sig, 1)
                    act.wait_ge(big_free[k_use % 2], me.over(k_use))
                    act.activation(CY[:, j, :], CU[:, j, :], ACT.Identity, bias=vec("cf_dw_b", j),
                                   scale=vec("cf_dw_w", TAPS * KT + j)).then_inc(dw_base, 1)
                mean_use = me.big
                me.big += 1
                for k in range(KT):
                    if k < KT - 1:
                        act.wait_ge(centred, me.next("centred"))
                    else:
                        act.wait_ge(big_free[mean_use % 2], me.over(mean_use))
                    act.activation(HT[:, k, 0:N], CY[:, k, :], ACT.Square).then_inc(squares, 1)
                k_use = me.next_big()
                act.wait_ge(big_filled, me.fills(k_use))
                act.activation(RS[:, 0:N], BIG[k_use % 2][:, 0:N], ACT.Copy).then_inc(big_free[k_use % 2], 1)
                k_use = me.next_big()
                act.wait_ge(big_filled, me.fills(k_use))
                act.activation(RS[:, 0:N], BIG[k_use % 2][:, 0:N], ACT.Ln, bias=EPSC[:, 0:1], scale=1.0 / (32 * D))\
                    .then_inc(big_free[k_use % 2], 1)
                act.wait_ge(big_free[k_use % 2], me.over(k_use))
                act.activation(RS[:, 0:N], RS[:, 0:N], ACT.Exp, scale=-0.5).then_inc(rs_ready, 1)
                for k in range(KT):
                    act.wait_ge(ln_scaled, me.next("ln_scaled"))
                    act.activation(CU[:, k, :], CY[:, k, :], ACT.Silu, bias=vec("cf_ln_b", k)).then_inc(h_ready, 1)
                uses = list(range(me.big, me.big + KT))
                for k in range(KT):
                    if k >= 2:
                        act.wait_ge(big_free[uses[k - 2] % 2], me.over(uses[k - 2]))
                    k_use = me.next_big()
                    act.wait_ge(big_filled, me.fills(k_use))
                    act.activation(CFT[:, k % 2, :], BIG[k_use % 2][:, 0:N], ACT.Identity,
                                   bias=vec("cf_b2", k)).then_inc(cf_add, 1)
                return uses

            def experts(layer):
                act.wait_ge(pt_free, me.pt_over(me.pt))
                act.activation(PROBS, PROBS, ACT.Exp).then_inc(logits_exp, 1)
                for t in range(TT):
                    k_use = me.next_big()
                    act.wait_ge(big_filled, me.fills(k_use))
                    act.activation(HTOK[:, t, :], BIG[k_use % 2][:, :], ACT.Copy).then_inc(big_free[k_use % 2], 1)
                me.pt += 3

                def gathered():
                    k_use = me.next_big()
                    act.wait_ge(big_filled, me.fills(k_use))
                    act.activation(XS.rearrange("p a b -> p (a b)"), BIG[k_use % 2][:, :], ACT.Copy)\
                        .then_inc(big_free[k_use % 2], 1)

                gathered()
                with act.Fori(0, MOE_PAIRS) as i:
                    me.enter(i, PER_PAIR)
                    me.pt += 1
                    k_use = me.next_big()
                    act.wait_ge(big_filled, me.fills(k_use))
                    act.activation(SIL, BIG[k_use % 2][:, :], ACT.Silu).then_inc(big_free[k_use % 2], 1)
                    me.big += 1
                    gathered()
                    m_hid = me.next_pt()
                    act.wait_ge(pt_filled, me.pt_fills(m_hid))
                    act.activation(HXT.rearrange("p a b -> p (a b)"), PT[:, :], ACT.Copy).then_inc(pt_free, 1)
                    k_use = me.next_big()
                    act.wait_ge(big_filled, me.fills(k_use))
                    act.activation(YK, BIG[k_use % 2][:, :], ACT.Copy).then_inc(big_free[k_use % 2], 1)
                    me.big += 4
                    me.leave(MOE_PAIRS)
                return [me.big - 4 + k // 2 for k in range(KT)]

            act.wait_ge(consts_loaded, 32)
            act.activation(CCS[:, 0:32], vec("cvec", 0, 32), ACT.Silu).then_inc(cvec_ready, 1)
            act.wait_ge(x_loaded, 16)
            act.wait_ge(eps_ready, 1)
            for _ in range(FIRST_STEPS):
                mod_rows()
            updates = None
            act.wait_ge(mods_filled, me.next("mods_filled"))
            for layer in range(DEPTH):
                mod_waits[0] = False
                norm(NA, updates, lambda k, c: mod(layer, 0, k, c))
                updates = attention(layer)
            norm(N, updates, None)
            act.wait_ge(ctx2_loaded, 16)
            norm(NA, None, lambda k, c: mod(2, 0, k, c), block_done)
            updates = even_layer()
            norm(N, updates, lambda k, c: mod(2, 3, k, c))
            updates = experts(0)
            norm(N, updates, lambda k, c: mod(3, 0, k, c))
            updates = conformer()
            norm(N, updates, lambda k, c: mod(3, 3, k, c))
            updates = experts(1)
            norm(N, updates, None)

        @block.vector
        def _(dve):
            me = Count()

            def link(ins):
                ins.then_inc(dve_chain, 1)
                dve.wait_ge(dve_chain, me.next("dve_chain"))

            def modulation(group, done, first=0, steps=None):
                dve.wait_ge(mods_filled, done)
                steps = MOD_STEPS[group] if steps is None else steps
                a, n = MOD_AT[group] + 4 * MOD_UNITS * first, 4 * MOD_UNITS * steps
                link(dve.tensor_tensor(MOD[:, a:a + n], MODP[:, a:a + n], vec("mod_b", a, n), ALU.add))

            def norm(n, weight, group, scale_chunk, dst, done):
                if group is not None:
                    for c in range(2 if n > N else 1):
                        link(dve.scalar_tensor_tensor(COEF[:, c * KT:c * KT + KT], mod_row(group, scale_chunk, c),
                                                      1.0, weight, ALU.add, ALU.mult))
                me.big += 2
                dve.wait_ge(rs_ready, me.next("rs_ready"))
                for k in range(KT):
                    for c in range(2 if n > N else 1):
                        a, b = (0, N) if c == 0 else (N, NA)
                        factor = COEF[:, c * KT + k:c * KT + k + 1] if group is not None else weight[:, k:k + 1]
                        ins = dve.scalar_tensor_tensor(dst[:, k, a:b], XC[:, k, a:b], factor, RS[:, a:b],
                                                       ALU.mult, ALU.mult)
                    if done is not None:
                        ins.then_inc(done, 1)
                return ins

            def add_gated(n, gates):
                for m in range(KT):
                    k_use = me.next_big()
                    dve.wait_ge(big_filled, me.fills(k_use))
                    for c in range(2 if n > N else 1):
                        a, b = (0, N) if c == 0 else (N, NA)
                        ins = dve.scalar_tensor_tensor(XC[:, m, a:b], BIG[k_use % 2][:, a:b], gates(m, c),
                                                       XC[:, m, a:b], ALU.mult, ALU.add)
                    ins.then_inc(big_free[k_use % 2], 1)

            def attention(layer):
                steps, order = schedule(layer)
                nq = NA if layer == 0 else N
                kv = -1
                score_use = {}
                for what, x in order:
                    if what == "mod_rows":
                        me.big += 1
                    elif what == "k":
                        kv += 1
                        me.big += 1
                    elif what == "q":
                        me.big += 1
                    elif what == "v" and PAIRS[x][0] == "B":
                        me.big += 1
                    elif what in ("v", "v_tokens"):
                        k_use = me.next_big()
                        dve.wait_ge(big_filled, me.fills(k_use))
                        dve.tensor_copy(V[:, kv % 2, :, :].rearrange("p a b -> p (a b)"),
                                        BIG[k_use % 2][:, 0:NA]).then_inc(big_free[k_use % 2], 1)
                    elif what == "g":
                        k_use = me.next_big()
                        dve.wait_ge(big_filled, me.fills(k_use))
                        dve.wait_ge(gate_tanh, me.next("gate_tanh"))
                        dve.scalar_tensor_tensor(SG[:, x % 2, 0:nq], GATE_T[:, 0:nq], 1.0,
                                                 BIG[k_use % 2][:, 0:nq], ALU.add, ALU.mult)\
                            .then_inc(big_free[k_use % 2], 1)
                    elif what.startswith("norm_"):
                        me.big += 1
                        dve.wait_ge(qk_rs, me.next("qk_rs"))
                        dst, n, w = (K[:, kv % 2, :], NA, "kn") if what == "norm_k" else (Q[:, x % 2, :], nq, "qn")
                        dve.scalar_tensor_tensor(dst[:, 0:n], dst[:, 0:n], vec(w, layer), SQT[:, 0:n],
                                                 ALU.mult, ALU.mult).then_inc(qk_normed, 1)
                        dve.wait_ge(qk_normed, me.next("qk_normed"))
                    elif what.startswith("rope_"):
                        dst = K[:, kv % 2, 0:N] if what == "rope_k" else Q[:, x % 2, 0:N]
                        k_use = me.next_big()
                        dve.wait_ge(big_filled, me.fills(k_use))
                        dve.tensor_tensor(ROPE_T, BIG[k_use % 2][:, 0:N], const("sin"), ALU.mult)\
                            .then_inc(big_free[k_use % 2], 1)
                        link(dve.tensor_tensor(dst, dst, const("cos"), ALU.mult))
                        dve.wait_ge(big_free[k_use % 2], me.over(k_use))
                        dve.tensor_tensor(dst, dst, ROPE_T, ALU.add).then_inc(qk_roped, 1)
                    elif what == "S":
                        i, h, t = steps[x]
                        kind, j = PAIRS[i]
                        k_use = score_use[x] = me.next_big()
                        dve.wait_ge(big_filled, me.fills(k_use))
                        out = BIG[k_use % 2]
                        if kind == "B" and t < TT:
                            head = 8 * layer + 2 * j + h
                            if t == 0:
                                dve.wait_ge(bias_loaded[head % BIAS_SLOTS], 16 * (head // BIAS_SLOTS + 1))
                            a, _ = score_span(kind, t)
                            at_bias = BIAS_AT[t]
                            ins = dve.tensor_tensor(out[:, a:N], out[:, a:N],
                                                    BIAS[:, head % BIAS_SLOTS, at_bias:at_bias + N - a], ALU.add)
                            if t == TT - 1:
                                ins.then_inc(bias_used, 1)
                                dve.wait_ge(bias_used, me.next("bias_used"))
                            else:
                                link(ins)
                        if kind == "C":
                            a, b = score_span(kind, t)
                            if t < TT:
                                if t > 0:
                                    link(dve.tensor_tensor(out[:, a:a + P], out[:, a:a + P], const("mprev"), ALU.add))
                                if t < TT - 1:
                                    link(dve.tensor_tensor(out[:, N - P:N], out[:, N - P:N], const("mnext"), ALU.add))
                            head = j + 4 * h
                            link(dve.tensor_copy(out[:, NA:NA + 1], vec("sink", 8 * layer + head)))
                        a, b = score_span(kind, t)
                        dve.tensor_reduce(STAT[:, x % 4:x % 4 + 1], out[:, a:b], AX.X, ALU.max, negate=True)\
                            .then_inc(max_ready, 1)
                    elif what == "T":
                        me.pt += 1
                        if x % 2:
                            dve.wait_ge(big_free[score_use[x] % 2], me.over(score_use[x]))
                            dve.wait_ge(big_free[score_use[x - 1] % 2], me.over(score_use[x - 1]))
                            c = x % 4 - 1
                            link(dve.reciprocal(STAT[:, 8 + c:10 + c], STAT[:, 4 + c:6 + c]))
                            dve.tensor_copy(RB, STAT[:, 8 + c:10 + c].unsqueeze(2).to_broadcast([P, 2, HD]))\
                                .then_inc(sums_inverted, 1)
                    elif what == "O":
                        i, h, t = steps[x]
                        dve.wait_ge(o_filled, me.next("o_filled"))
                        y = query_tile(i, t, U[:, i, :])
                        link(dve.scalar_tensor_tensor(y, like_query_tile(i, t, OP[:, 0:P]), 0.5,
                                                      query_tile(i, t, SG[:, i % 2, :]), ALU.mult, ALU.mult))
                        dve.tensor_tensor(y, y, like_query_tile(i, t, OP[:, P:2 * P]), ALU.mult)\
                            .then_inc(y_ready, 1)
                        dve.wait_ge(y_ready, me.next("y_ready"))
                if layer == 0:
                    modulation(0, MODS_DONE[0], FIRST_STEPS, MOD_STEPS[0] - FIRST_STEPS)
                add_gated(nq, lambda m, c: mod(layer, 2, m, c))

            def convolve(dst, raw, n, taps, weight, bias):
                link(dve.tensor_scalar(dst, raw[:, 0:n], weight(0), bias, ALU.mult, ALU.add))
                for j in range(1, taps):
                    ins = dve.scalar_tensor_tensor(dst, raw[:, j:j + n], weight(j), dst, ALU.mult, ALU.add)
                    if j < taps - 1:
                        link(ins)
                return ins

            def even_layer():
                for t in range(4):
                    k_use = me.next_big()
                    dve.wait_ge(big_filled, me.fills(k_use))
                    dve.wait_ge(big_free[(me.big - 1) % 2], me.over(me.big - 1))
                    link(convolve(XAC[:, t, :], XAR[:, t, :], N, 4, lambda j: vec("conv_a_w", j * 4 + t),
                                  vec("conv_a_b", t)))
                    convolve(CXC[:, t, :], CXR[:, t, :], NC, 4, lambda j: vec("conv_a_w", j * 4 + t),
                             vec("conv_a_b", t)).then_inc(xa_ready, 1)
                me.big += 4
                dve.wait_ge(lam_exp, me.next("lam_exp"))
                e, s, s2, q = (SPT[:, x, :] for x in (1, 2, 3, 4))
                link(dve.tensor_scalar(q, e, 2.0, None, ALU.add))
                link(dve.reciprocal(s, q))
                link(dve.tensor_tensor(s, s, e, ALU.mult))
                link(dve.tensor_tensor(s2, s, s, ALU.mult))
                link(dve.tensor_scalar(q, s2, 1.0 / 15, None, ALU.mult))
                for odd in (13, 11, 9, 7, 5, 3):
                    link(dve.scalar_tensor_tensor(q, q, 1.0 / odd, s2, ALU.add, ALU.mult))
                link(dve.scalar_tensor_tensor(q, q, 1.0, s, ALU.add, ALU.mult))
                link(dve.tensor_scalar(s2, vec("lru_lam", 0, 8), -1.0, 0.0, ALU.mult, ALU.max))
                link(dve.scalar_tensor_tensor(q, q, 2.0, s2, ALU.mult, ALU.add))
                link(dve.tensor_scalar(SPT[:, 6, :], q, 8.0, None, ALU.mult))
                dve.tensor_scalar(SPT[:, 7, :], q, -8.0, None, ALU.mult).then_inc(decay_ready, 1)
                link(dve.memset(HID[64:65, :], 1.0))

                def sine_argument(x):
                    magic = 1.5 * 2.0 ** 23
                    two_pi = 2 * np.pi
                    two_pi_hi = float(np.float32(6.28125))
                    k_use = me.next_big()
                    dve.wait_ge(big_filled, me.fills(k_use))
                    arg, rnd = HARG[0:64, :], HRND[0:64, :]
                    dve.tensor_scalar(arg, BIG[k_use % 2][0:64, 0:N], vec(f"filt_b{x + 1}", 0)[0:64],
                                      vec(f"filt_f{x}", 0)[0:64], ALU.add, ALU.mult)\
                        .then_inc(big_free[k_use % 2], 1)
                    dve.wait_ge(big_free[k_use % 2], me.over(k_use))
                    link(dve.tensor_scalar(rnd, arg, 1.0 / two_pi, magic, ALU.mult, ALU.add))
                    link(dve.tensor_scalar(rnd, rnd, -magic, None, ALU.add))
                    link(dve.scalar_tensor_tensor(arg, rnd, -two_pi_hi, arg, ALU.mult, ALU.add))
                    link(dve.scalar_tensor_tensor(arg, rnd, -(two_pi - two_pi_hi), arg, ALU.mult, ALU.add))
                    pi32 = 3.1415925
                    dve.tensor_scalar(arg, arg, -pi32, pi32, ALU.max, ALU.min).then_inc(sin_arg, 1)

                def lru_inputs(t):
                    for d in range(2):
                        me.big += 2
                        dve.wait_ge(big_free[(me.big - 1) % 2], me.over(me.big - 1))
                        dve.tensor_tensor(IX[:, d, 0:N], IX[:, d, 0:N], XAC[:, t, :], ALU.mult)
                        link(dve.tensor_tensor(IX[:, d, N:NA], IX[:, d, N:NA], CXC[:, t, :], ALU.mult))
                    for d in range(2):
                        dve.wait_ge(lru_a, me.next("lru_a"))
                        link(dve.tensor_tensor(LT, LA[:, d, :], LA[:, d, :], ALU.mult))
                        dve.scalar_tensor_tensor(LR[:, d, :], LT, 1.0, LR[:, d, :], ALU.add, ALU.mult)\
                            .then_inc(lru_v, 1)
                        dve.wait_ge(lru_v, me.next("lru_v"))

                def lru_scans(t):
                    for d in range(2):
                        a, h = LA[:, d, :], LH[:, d, :]
                        dve.wait_ge(lru_sqrt, me.next("lru_sqrt"))
                        link(dve.tensor_tensor(LT, LR[:, d, :], IX[:, d, :], ALU.mult))
                        if d == 0:
                            link(dve.tensor_tensor_scan(h[:, N:NA], a[:, N:NA], LT[:, N:NA], 0.0, ALU.mult, ALU.add))
                            ins = dve.tensor_tensor_scan(h[:, 0:N], a[:, 0:N], LT[:, 0:N], h[:, NA - 1:NA],
                                                         ALU.mult, ALU.add)
                        else:
                            link(dve.tensor_tensor_scan(h[:, NA - 1:N - 1:-1], a[:, NA - 1:N - 1:-1],
                                                        LT[:, NA - 1:N - 1:-1], 0.0, ALU.mult, ALU.add))
                            ins = dve.tensor_tensor_scan(h[:, N - 1::-1], a[:, N - 1::-1], LT[:, N - 1::-1],
                                                         h[:, N:N + 1], ALU.mult, ALU.add)
                        link(ins)
                    link(dve.tensor_tensor(LT[:, 0:N], LH[:, 0, 0:N], LH[:, 1, 0:N], ALU.add))
                    dve.tensor_tensor(YA[:, t, :], LT[:, 0:N], GATE[:, t, :], ALU.mult).then_inc(lru_done, 1)
                    dve.wait_ge(lru_done, me.next("lru_done"))

                for t in range(12):
                    if t % 6 == 0:
                        sine_argument(t // 6)
                    if t in LRU_BEFORE:
                        lru_inputs(LRU_BEFORE.index(t))
                    k_use = me.big
                    me.big += 1
                    dve.wait_ge(big_free[k_use % 2], me.over(k_use))
                    convolve(HY[:, t, :], HYR[:, t % 2, :], N, 3, lambda j: vec("conv_b_w", j * 12 + t),
                             vec("conv_b_b", t)).then_inc(hy_ready, 1)
                    if t in LRU_BEFORE:
                        lru_scans(LRU_BEFORE.index(t))
                dve.wait_ge(unit_loaded[hyena_slots[1]], 16 * ((len(first_units) - 3 - len(HYENA_UNITS)) // RING + 1))
                for o in range(2):
                    for t in range(TT):
                        k_use = me.next_big()
                        dve.wait_ge(big_filled, me.fills(k_use))
                        out = BIG[k_use % 2]
                        fwd, bwd = FS[:, t, :], KF[:, t, :]
                        link(dve.tensor_tensor(fwd, out[:, 0:N], WIN[:, t, :], ALU.mult))
                        dve.tensor_tensor(bwd, out[:, N:1024], WIN[:, t, :], ALU.mult)\
                            .then_inc(big_free[k_use % 2], 1)
                        dve.wait_ge(big_free[k_use % 2], me.over(k_use))
                        if t == 0:
                            link(dve.memset(bwd[0:1, :], 0.0))
                        link(dve.tensor_tensor(FD[:, t, :], fwd, bwd, ALU.subtract))
                        dve.tensor_tensor(fwd, fwd, bwd, ALU.add).then_inc(filt_ready, 1)
                    me.big += 4
                    spec_last = me.big - 1
                    me.big += 2
                    dve.wait_ge(big_free[spec_last % 2], me.over(spec_last))
                    dve.wait_ge(big_free[(spec_last - 1) % 2], me.over(spec_last - 1))
                    for f in range(4):
                        k_use = me.next_big()
                        dve.wait_ge(big_filled, me.fills(k_use))
                        ur, us = BIG[k_use % 2][:, 0:N], BIG[k_use % 2][:, N:1024]
                        kr, ks = KF[:, f, :], KF[:, 4 + f, :]
                        zr, zs = ZF[:, f, :], ZF[:, 4 + f, :]
                        t0, t1 = FD[:, 0, :], FD[:, 1, :]
                        dve.tensor_tensor(zr, ur, kr, ALU.mult)
                        dve.tensor_tensor(t0, us, ks, ALU.mult)
                        dve.tensor_tensor(zs, ur, ks, ALU.mult)
                        dve.tensor_tensor(t1, us, kr, ALU.mult).then_inc(big_free[k_use % 2], 1)
                        dve.wait_ge(big_free[k_use % 2], me.over(k_use))
                        if f == 0:
                            link(dve.tensor_copy(zs[0:1, :], t0[0:1, :]))
                            link(dve.memset(t0[0:1, :], 0.0))
                            link(dve.memset(t1[0:1, :], 0.0))
                        link(dve.tensor_tensor(zr, zr, t0, ALU.subtract))
                        dve.tensor_tensor(zs, zs, t1, ALU.add).then_inc(spec_ready, 1)
                        dve.wait_ge(spec_ready, me.next("spec_ready"))
                    for c in range(4):
                        k_use = me.next_big()
                        dve.wait_ge(big_filled, me.fills(k_use))
                        u = HY[:, c, :]
                        link(dve.scalar_tensor_tensor(u, u, vec("filt_bias", o * 4 + c), BIG[k_use % 2][:, 0:N],
                                                      ALU.mult, ALU.add))
                        dve.tensor_tensor(u, u, HY[:, 4 * (o + 1) + c, :], ALU.mult)\
                            .then_inc(big_free[k_use % 2], 1)
                add_gated(N, lambda m, c: mod(2, 2, m, c))

            def conformer():
                for j in range(KT):
                    k_use = me.next_big()
                    dve.wait_ge(big_filled, me.fills(k_use))
                    dve.wait_ge(glu_sig, me.next("glu_sig"))
                    dve.scalar_tensor_tensor(CU[:, j, :], BIG[k_use % 2][:, 0:N], vec("cf_b1", j),
                                             CSIG[:, j % 2, :], ALU.add, ALU.mult).then_inc(big_free[k_use % 2], 1)
                    dve.wait_ge(dw_base, me.next("dw_base"))
                    shifts = [s for s in range(-TAPS, TAPS + 1) if s]
                    for s in shifts:
                        lo, hi = max(0, -s) * GRID_W, (ROWS - max(0, s)) * GRID_W
                        ins = dve.scalar_tensor_tensor(CY[:, j, lo:hi], CU[:, j, lo + s * GRID_W:hi + s * GRID_W],
                                                       vec("cf_dw_w", (s + TAPS) * KT + j), CY[:, j, lo:hi],
                                                       ALU.mult, ALU.add)
                        if s == shifts[-1]:
                            ins.then_inc(dw_ready, 1)
                            dve.wait_ge(dw_ready, me.next("dw_ready"))
                        else:
                            link(ins)
                k_use = me.next_big()
                dve.wait_ge(big_filled, me.fills(k_use))
                for k in range(KT):
                    ins = dve.scalar_tensor_tensor(CY[:, k, :], BIG[k_use % 2][:, 0:N], -1.0 / D, CY[:, k, :],
                                                   ALU.mult, ALU.add)
                    ins.then_inc(centred if k < KT - 1 else big_free[k_use % 2], 1)
                dve.wait_ge(big_free[k_use % 2], me.over(k_use))
                me.big += 2
                dve.wait_ge(rs_ready, me.next("rs_ready"))
                for k in range(KT):
                    dve.scalar_tensor_tensor(CY[:, k, :], CY[:, k, :], vec("cf_ln_g", k), RS[:, 0:N],
                                             ALU.mult, ALU.mult).then_inc(ln_scaled, 1)
                for m in range(KT):
                    k_use = me.big
                    me.big += 1
                    dve.wait_ge(cf_add, me.next("cf_add"))
                    dve.scalar_tensor_tensor(XC[:, m, 0:N], CFT[:, m % 2, :], mod(3, 2, m, 0), XC[:, m, 0:N],
                                             ALU.mult, ALU.add).then_inc(big_free[k_use % 2], 1)

            def experts(layer):
                group = 2 + layer
                me.big += TT
                m_pt = me.next_pt()
                dve.wait_ge(pt_filled, me.pt_fills(m_pt))
                logits = PT[:, 0:64].rearrange("p (t e) -> p t e", e=N_EXPERTS)
                top, total = SMALL[:, 0:4], SMALL[:, 4:8]
                link(dve.tensor_reduce(top, logits, AX.X, ALU.max))
                dve.tensor_tensor(PROBS, logits, top.unsqueeze(2).to_broadcast([P, TT, N_EXPERTS]),
                                  ALU.subtract).then_inc(pt_free, 1)
                dve.wait_ge(logits_exp, me.next("logits_exp"))
                link(dve.tensor_reduce(total, PROBS, AX.X, ALU.add))
                link(dve.reciprocal(total, total))
                dve.tensor_tensor(PROBS, PROBS, total.unsqueeze(2).to_broadcast([P, TT, N_EXPERTS]),
                                  ALU.mult).then_inc(probs_ready, 1)
                m_pt = me.next_pt()
                dve.wait_ge(pt_filled, me.pt_fills(m_pt))
                rows = [ROW0[0:16, :], ROW1[0:16, :]]
                dve.tensor_copy(rows[0], PT[0:16, 0:N]).then_inc(pt_free, 1)
                dve.wait_ge(pt_free, me.pt_over(me.pt - 1))
                for r in range(CAP // 8):
                    link(dve.max(MAX8[0:16, :], rows[r % 2]))
                    link(dve.match_replace(rows[(r + 1) % 2], MAX8[0:16, :], rows[r % 2], -1.0))
                chosen, upto, slot = ROW2[0:16, :], ROW3[0:16, :], ROW1[0:16, :]
                link(dve.tensor_scalar(chosen, rows[0], 0.0, None, ALU.is_lt))
                link(dve.tensor_tensor_scan(upto, chosen, chosen, 0.0, ALU.add, ALU.max))
                link(dve.tensor_tensor(slot, chosen, upto, ALU.mult))
                dve.tensor_scalar(slot, slot, -1.0, None, ALU.add).then_inc(slots_ready, 1)
                m_pt = me.next_pt()
                dve.wait_ge(pt_filled, me.pt_fills(m_pt))
                dve.memset(SLOT[:, :, N_EXPERTS:], -2.0)
                dve.tensor_copy(SLOT[:, :, 0:N_EXPERTS], PT[:, 0:64].rearrange("p (t e) -> p t e", e=N_EXPERTS))\
                   .then_inc(pt_free, 1)
                dve.wait_ge(pt_free, me.pt_over(me.pt - 1))
                lanes = vec("iota", 0, CAP).unsqueeze(1).unsqueeze(1)

                def onehots(first):
                    slots = SLOT[:, :, first].unsqueeze(3).to_broadcast([P, TT, 2, CAP])
                    dve.tensor_tensor(ONEH, lanes.to_broadcast([P, TT, 2, CAP]), slots, ALU.is_equal)\
                        .then_inc(onehot_ready, 1)
                    dve.wait_ge(onehot_ready, me.next("onehot_ready"))

                onehots(slice(0, 2))
                me.big += 1
                with dve.Fori(0, MOE_PAIRS) as i:
                    me.enter(i, dict(PER_PAIR, onehot_ready=1))
                    gate = PROBS[:, :, bass.ds(i * 2, 2)].unsqueeze(3).to_broadcast([P, TT, 2, CAP])
                    dve.tensor_tensor(GONEH, ONEH, gate, ALU.mult).then_inc(gates_ready, 1)
                    m_pt = me.next_pt()
                    dve.wait_ge(pt_filled, me.pt_fills(m_pt))
                    dve.tensor_copy(GSCAT, PT[:, 0:N]).then_inc(pt_free, 1)
                    onehots(bass.ds(i * 2 + 2, 2))
                    k_silu = me.next_big()
                    k_use = me.next_big()
                    dve.wait_ge(big_filled, me.fills(k_use))
                    dve.wait_ge(big_free[k_silu % 2], me.over(k_silu))
                    dve.tensor_tensor(HX, SIL, BIG[k_use % 2][:, :], ALU.mult).then_inc(big_free[k_use % 2], 1)
                    me.big += 1
                    me.pt += 1
                    me.big += 1
                    for m2 in range(4):
                        k_use = me.next_big()
                        dve.wait_ge(big_filled, me.fills(k_use))
                        for half in range(2):
                            m = 2 * m2 + half
                            ins = dve.scalar_tensor_tensor(XC[:, m, 0:N], BIG[k_use % 2][:, half * N:half * N + N],
                                                           mod(group, 5, m, 0), XC[:, m, 0:N], ALU.mult, ALU.add)
                        ins.then_inc(big_free[k_use % 2], 1)
                    me.leave(MOE_PAIRS)

            dve.memset(CCS[:, 32:64], 0.0).then_inc(cvec_ready, 1)
            dve.memset(EPSC[:, 0:1], EPS)
            dve.memset(EPSC[:, 1:2], EPS * HD).then_inc(eps_ready, 1)
            dve.wait_ge(consts_loaded, 32)
            dve.wait_ge(x_loaded, 16)
            me.big += FIRST_STEPS
            for layer in range(DEPTH):
                if layer == 0:
                    modulation(0, FIRST_STEPS, 0, FIRST_STEPS)
                else:
                    modulation(1, MODS_DONE[0])
                norm(NA, vec("norm_w", 8 * layer, 8), layer, 1, HT, h_scaled)
                attention(layer)
            norm(N, vec("final_norm_w", 0, 8), None, None, XC, block_done)
            dve.wait_ge(block_done, KT)
            dve.memset(XAR[:, :, 0:1], 0.0)
            dve.memset(XAR[:, :, N + 1:N + 4], 0.0)
            dve.memset(CXR[:, :, 0:1], 0.0)
            dve.memset(CXR[:, :, NC + 1:NC + 4], 0.0)
            dve.memset(HYR[:, :, 0:1], 0.0)
            dve.memset(HYR[:, :, N + 1:N + 4], 0.0).then_inc(pads_ready, 1)
            dve.wait_ge(pads_ready, me.next("pads_ready"))
            dve.wait_ge(ctx2_loaded, 16)
            modulation(2, MODS_DONE[1])
            norm(NA, vec("norm1_g", 0, 8), 2, 1, HT, h_scaled)
            even_layer()
            norm(N, vec("norm2_g", 0, 8), 2, 4, HT, h_scaled)
            experts(0)
            modulation(3, MODS_DONE[1])
            norm(N, vec("norm1_g", 8, 8), 3, 1, HT, h_scaled)
            conformer()
            norm(N, vec("norm2_g", 8, 8), 3, 4, HT, h_scaled)
            experts(1)
            norm(N, vec("final_g", 0, 8), None, None, HT, out_ready)


def constants():
    c = {}
    packed = np.zeros((P, NK), np.float32)
    packed[:, COFF["ident"]:COFF["ident"] + P] = np.eye(P)
    packed[:, COFF["ones"]:COFF["ones"] + P] = 1
    half = HD // 2
    for b in range(2):
        a = COFF["blk"] + b * HD
        packed[b * HD:(b + 1) * HD, a:a + HD] = 1
        for m in range(half):
            packed[b * HD + m + half, COFF["rot"] + b * HD + m] = -1
            packed[b * HD + m, COFF["rot"] + b * HD + m + half] = 1
    t = np.arange(N)
    freq = (np.float32(10000.0) ** (-np.arange(HD // 4, dtype=np.float32) / np.float32(HD // 4))).astype(np.float32)
    ang = np.concatenate([(t // GRID_W).astype(np.float32)[:, None] * freq,
                          (t % GRID_W).astype(np.float32)[:, None] * freq], axis=1)
    packed[:, COFF["cos"]:COFF["cos"] + N] = np.tile(np.cos(ang).T, (4, 1))
    packed[:, COFF["sin"]:COFF["sin"] + N] = np.tile(np.sin(ang).T, (4, 1))
    q, k = np.arange(P)[:, None], np.arange(P)[None, :]
    packed[:, COFF["mprev"]:COFF["mprev"] + P] = np.where(k >= q, 0, MASKED)
    packed[:, COFF["mnext"]:COFF["mnext"] + P] = np.where(k <= q, 0, MASKED)
    packed[0::32, COFF["sel"]] = 1
    packed[1::32, COFF["sel"] + 1] = 1
    c["consts"] = packed

    def tiled(a):
        return np.ascontiguousarray(a.reshape(a.shape[0] // P, P, -1).transpose(1, 0, 2).astype(np.float32))

    f = np.arange(NF)
    turns = (t[:, None] * f[None, :]) % (2 * N)
    c["dft_cos"] = tiled(np.cos(np.pi * turns / N))
    sines = np.sin(np.pi * turns / N)
    sines[turns % N == 0] = 0
    c["dft_sin"] = tiled(sines)
    alternate = 1.0 - 2.0 * (t % 2)
    nyq = np.zeros((N, P))
    nyq[:, 0] = alternate
    c["dft_nyq"] = tiled(nyq)
    c["dft_alt"] = alternate[None, :].astype(np.float32)
    pos = np.linspace(0.0, 1.0, N, dtype=np.float32)[:, None]
    deltas = np.abs(np.linspace(np.log(1e-2) / 1.5, np.log(1e-2) / 0.3, 512, dtype=np.float32))
    c["window"] = tiled(np.exp(-pos * deltas[None, :]) + np.float32(0.05))
    bands = 16
    w = (np.float32(2.0 * np.pi / N) * np.arange(N, dtype=np.float32))[:, None]
    fb = np.linspace(1e-4, bands - 1, bands, dtype=np.float32)[None, :]
    c["z"] = np.concatenate([pos, np.cos(fb * w), -np.sin(fb * w)], axis=1).astype(np.float32)
    return c


def lay_out(x):
    c = constants()
    f32 = np.float32

    def feature_major(a):
        return np.ascontiguousarray(a.T.reshape(KT, P, -1).transpose(1, 0, 2))

    def cols(v):
        v = np.asarray(v, f32)
        return v.reshape(-1, P).T

    vec = {
        "norm_w": cols(x["norm_w"]), "final_norm_w": cols(x["final_norm_w"]),
        "norm1_g": cols(x["norm1_g_2"]), "norm2_g": cols(x["norm2_g_2"]), "final_g": cols(x["final_g_2"]),
        "qn": np.tile(x["q_norm_a"].T, (2, 1)), "kn": np.tile(x["k_norm_a"].T, (2, 1)),
        "sink": np.broadcast_to(x["sink_c"].reshape(1, 16), (P, 16)),
        "mod_b": np.repeat(np.concatenate([cols(x["ada_b"]), cols(x["b_mod_2"])], axis=1), 2, axis=1),
        "cvec": np.stack([cols(x["c"]), cols(x["c_ctx"]), cols(x["c_2"]), cols(x["c_ctx_2"])], axis=2).reshape(P, 32),
        "conv_a_w": cols(x["conv_a_w_2"]), "conv_a_b": cols(x["conv_a_b_2"]),
        "lru_br": cols(x["lru_br_2"]), "lru_bi": cols(x["lru_bi_2"]), "lru_lam": cols(x["lru_lam_2"]),
        "conv_b_w": cols(x["conv_b_w_2"]), "conv_b_b": cols(x["conv_b_b_2"]),
        "filt_bias": cols(x["filt_bias_2"]), "cf_b1": cols(x["cf_b1_2"]),
        "cf_dw_w": cols(x["cf_dw_w_2"][0, 15 - TAPS:16 + TAPS]),
        "cf_dw_b": cols(x["cf_dw_b_2"]), "cf_ln_g": cols(x["cf_ln_g_2"]), "cf_ln_b": cols(x["cf_ln_b_2"]),
        "cf_b2": cols(x["cf_b2_2"]),
        "iota": np.broadcast_to(np.arange(CAP, dtype=f32)[None, :], (P, CAP)),
    }
    for name, v in (("filt_b1", x["filt_b1_2"]), ("filt_b2", x["filt_b2_2"]),
                    ("filt_f0", x["filt_freq_2"][0, 0]), ("filt_f1", x["filt_freq_2"][0, 1])):
        vec[name] = np.zeros((P, 1), f32)
        vec[name][:64, 0] = v.reshape(-1)
    kscale = np.full((P, 4), 1.0 / N, f32)
    kscale[0, 0] = 0.5 / N
    vec["kscale"] = kscale
    vecs = np.zeros((P, NV), f32)
    for name, n in VECTORS:
        assert vec[name].shape == (P, n), (name, vec[name].shape)
        vecs[:, VOFF[name]:VOFF[name] + n] = vec[name]

    def unit(w):
        out = np.zeros((P, UNIT), f32)
        flat = w.reshape(-1, P, w.shape[1]).transpose(1, 0, 2).reshape(P, -1)
        out[:, :flat.shape[1]] = flat
        return out

    off = dict(zip(["qA", "kA", "vA", "qB", "kB", "vB", "qC", "kC", "vC", "gate"],
                   np.cumsum([0, 512, 128, 128, 512, 512, 512, 512, 128, 128])))

    def pair_cols(i):
        kind, j = PAIRS[i]
        base = {"A": 0, "B": 512, "C": 1024}[kind]
        heads = (2 * j, 2 * j + 1) if kind == "B" else (j, j + 4)
        return np.concatenate([base + h * HD + np.arange(HD) for h in heads])

    w_in_units = []
    for what, i in schedule(0)[1]:
        if what not in ("k", "q"):
            continue
        kind, j = PAIRS[i]
        if what == "k":
            a = j * P if kind == "B" else 0
            w_in_units.append(np.concatenate([off["k" + kind] + a + np.arange(P), off["v" + kind] + a + np.arange(P)]))
        else:
            mixed = pair_cols(i)
            own = mixed - {"A": 0, "B": 512, "C": 1024}[kind]
            w_in_units.append(np.concatenate([off["q" + kind] + own, off["gate"] + mixed]))
    out_rows = np.concatenate([pair_cols(i) for i in range(12)])
    order2 = np.concatenate([np.arange(512, 1024), np.arange(512), np.arange(1024, 2560)])

    def lru_unit():
        out = np.zeros((16, P, P), f32)
        for g, name in enumerate(("lru_wr_2", "lru_wi_2")):
            for d in range(2):
                for h in range(8):
                    s = slice(h % 2 * HD, h % 2 * HD + HD)
                    out[(g * 2 + d) * 4 + h // 2, s, s] = x[name][0, d, h]
        return out.transpose(1, 0, 2).reshape(P, UNIT)

    def filter_unit():
        out = np.zeros((P, UNIT), f32)
        out[:64] = x["filt_w3_2"][0]
        out[64] = x["filt_b3_2"][0]
        return out

    def make(name, layer, u):
        c256 = slice(u * 256, u * 256 + 256)
        if name == "ada":
            return unit(x["ada_w"][layer][:, c256])
        if name == "w_mod":
            return unit(x["w_mod_2"][layer][:, c256])
        if name == "w_in":
            return unit(x["w_in"][layer][:, w_in_units[u]])
        if name == "w_out":
            return unit(x["w_out"][layer][out_rows, u * P:u * P + P])
        if name == "w_in_2":
            return unit(x["w_in_2"][0][:, order2[c256]])
        if name == "w_out_2":
            return unit(x["w_out_2"][0][:, c256])
        if name == "lru":
            return lru_unit()
        if name == "filt_w3":
            return filter_unit()
        if name == "dft_edge":
            edge = np.zeros((P, UNIT), f32)
            edge[:, 0:4 * P] = c["dft_nyq"].reshape(P, -1)
            edge[0:1, 4 * P:4 * P + N] = c["dft_alt"]
            return edge
        if name in HYENA_UNITS:
            return c[name].reshape(P, UNIT)
        if name == "cf_w1":
            cc = np.concatenate([u * P + np.arange(P), D + u * P + np.arange(P)])
            return unit(x["cf_w1_2"][0][:, cc])
        return unit(x["cf_w2_2"][0][:, c256])

    first, second = unit_order()
    tables = []
    for t in (0, 1, TT - 1):
        per = P // ROWS
        col = t * per + np.arange(per)[:, None, None, None]
        row = np.arange(ROWS)[None, :, None, None]
        kc = np.arange(max(t - 1, 0) * per, min(t + 2, TT) * per)[None, None, :, None]
        kr = np.arange(ROWS)[None, None, None, :]
        start = np.clip(col - 8, 0, GRID_W - 16)
        rr, cc, inside = np.broadcast_arrays(kr - row + ROWS - 1, np.clip(kc - col + 15, 0, 30),
                                             (kc >= start) & (kc < start + 16))
        tables.append(np.where(inside, x["rpb_b"][:, :, rr, cc], f32(MASKED)).reshape(DEPTH, 8, P, -1))
    bias = np.concatenate(tables, axis=3)

    small = np.zeros((P, 640), f32)
    small[:33, 0:64] = x["filt_w1_2"][0]
    small[:64, 64:128] = x["filt_w2_2"][0]
    small[:33, 128:640] = c["z"].T
    return {
        "consts": c["consts"], "vecs": vecs,
        "x0": np.concatenate([feature_major(x["x"][0]), feature_major(x["ctx"][0])], axis=2),
        "ctx2": feature_major(x["ctx_2"][0]),
        "units1": np.stack([make(*u) for u in first]), "units2": np.stack([make(*u) for u in second]),
        "bias_b": bias.astype(f32),
        "filt_small": small,
        "router": np.ascontiguousarray(x["router_2"].reshape(DEPTH, KT, P, N_EXPERTS).transpose(0, 2, 1, 3)),
        "exp_w1": x["exp_w1_2"], "exp_w3": x["exp_w3_2"], "exp_w2": x["exp_w2_2"],
    }


def kernel(**inputs):
    import concourse.bacc as bacc
    from concourse.bass_utils import run_bass_kernel_spmd

    arrays = {name: np.ascontiguousarray(a) for name, a in
              lay_out({k: np.asarray(v) for k, v in inputs.items()}).items()}
    nc = bacc.Bacc("TRN2", target_bir_lowering=False, num_devices=1)
    aps = {name: nc.dram_tensor("in_" + name, a.shape, mybir.dt.from_np(a.dtype), kind="ExternalInput").ap()
           for name, a in arrays.items()}
    aps["out"] = nc.dram_tensor("out_t", (P, KT, N), mybir.dt.float32, kind="ExternalOutput").ap()
    build(nc, aps)
    r = run_bass_kernel_spmd(nc, [{"in_" + name: a for name, a in arrays.items()}], core_ids=[0])
    return r.results[0]["out_t"].transpose(2, 1, 0).reshape(1, N, D)
```
